# Optimizing a Trainium2 kernel written in Bass

```python
import jax, jax.numpy as jnp
from jax import lax
import numpy as np

D_MODEL = 1024
BATCH = 1
SEQ = 256
DEPTH = 2

N_EVEN = (DEPTH + 1) // 2
N_ODD = DEPTH // 2
N_NORMS = 6

D_FF = ((8 * D_MODEL // 3 + 127) // 128) * 128
FFN_RES = 0.5

SB_HEADS = 8
SB_HEAD_DIM = 64
SB_WIDTH = SB_HEADS * SB_HEAD_DIM
SB_BLOCK = 128

CONV_CH = D_MODEL // 2
CONV_WIDTH = 31

EVEN_IN = 3 * SB_WIDTH + 2 * CONV_CH
EVEN_OUT = SB_WIDTH + CONV_CH

GLA_HEADS = 4
GLA_KEY = D_MODEL // 2
GLA_VAL = D_MODEL
GLA_DK = GLA_KEY // GLA_HEADS
GLA_DV = GLA_VAL // GLA_HEADS
GATE_RANK = 16
GATE_TAU = 16.0
GLA_CHUNK = 64
ODD_IN = 2 * GLA_KEY + 2 * GLA_VAL + GATE_RANK

NORM_EPS = 1e-6


def rms_norm(x, g):
    xf = x.astype(jnp.float32)
    y = xf * lax.rsqrt(jnp.mean(xf * xf, axis=-1, keepdims=True) + NORM_EPS)
    return (y * g.astype(jnp.float32)).astype(x.dtype)

def layer_norm(x, g, b):
    xf = x.astype(jnp.float32)
    mu = jnp.mean(xf, axis=-1, keepdims=True)
    var = jnp.mean(jnp.square(xf - mu), axis=-1, keepdims=True)
    y = (xf - mu) * lax.rsqrt(var + NORM_EPS)
    return (y * g.astype(jnp.float32) + b.astype(jnp.float32)).astype(x.dtype)

def swiglu(x, w_in, w_out):
    a, b = jnp.split(x @ w_in, 2, axis=-1)
    return (jax.nn.silu(a) * b) @ w_out

def split_heads(t, n):
    B, S, W = t.shape
    return t.reshape(B, S, n, W // n).transpose(0, 2, 1, 3)

def merge_heads(t):
    B, H, S, d = t.shape
    return t.transpose(0, 2, 1, 3).reshape(B, S, H * d)

def stick_breaking_attention(q, k, v):
    B, H, S, Dh = q.shape
    scale = Dh ** -0.5
    outs = []
    for i in range(S // SB_BLOCK):
        t0, t1 = i * SB_BLOCK, (i + 1) * SB_BLOCK
        qb = q[:, :, t0:t1]
        kb = k[:, :, :t1]
        vb = v[:, :, :t1]
        z = jnp.einsum('bhqd,bhkd->bhqk', qb, kb).astype(jnp.float32) * scale
        mask = jnp.arange(t1)[None, :] < jnp.arange(t0, t1)[:, None]
        log_1m = jnp.where(mask, jax.nn.log_sigmoid(-z), 0.0)
        rest = lax.cumsum(log_1m, axis=3, reverse=True) - log_1m
        w = jnp.where(mask, jnp.exp(jax.nn.log_sigmoid(z) + rest), 0.0)
        outs.append(jnp.einsum('bhqk,bhkd->bhqd', w.astype(vb.dtype), vb))
    return jnp.concatenate(outs, axis=2)

def causal_depthwise_conv(x, w, b):
    K, C = w.shape
    xp = jnp.pad(x, ((0, 0), (K - 1, 0), (0, 0)))
    y = lax.conv_general_dilated(
        xp, w[:, None, :].astype(x.dtype), window_strides=(1,), padding='VALID',
        dimension_numbers=('NWC', 'WIO', 'NWC'), feature_group_count=C)
    return y + b.astype(x.dtype)

def even_mixer(h, w_in, w_out, dw_w, dw_b, ln_g, ln_b):
    proj = h @ w_in
    q, k, v, u, gate = jnp.split(
        proj, [SB_WIDTH, 2 * SB_WIDTH, 3 * SB_WIDTH, 3 * SB_WIDTH + CONV_CH], axis=-1)
    a_out = merge_heads(stick_breaking_attention(
        split_heads(q, SB_HEADS), split_heads(k, SB_HEADS), split_heads(v, SB_HEADS)))
    c = u * jax.nn.sigmoid(gate)
    c = causal_depthwise_conv(c, dw_w, dw_b)
    c = jax.nn.silu(layer_norm(c, ln_g, ln_b))
    return jnp.concatenate([a_out.astype(h.dtype), c], axis=-1) @ w_out

def gla_chunked(q, k, v, g):
    B, H, S, dk = q.shape
    dv = v.shape[-1]
    N = S // GLA_CHUNK

    def to_chunks(t):
        return t.reshape(B, H, N, GLA_CHUNK, t.shape[-1]).transpose(2, 0, 1, 3, 4)

    mask = jnp.tril(jnp.ones((GLA_CHUNK, GLA_CHUNK), dtype=bool))

    def step(state, inp):
        qc, kc, vc, gc = inp
        b = jnp.cumsum(gc, axis=2)
        inter = jnp.einsum('bhtk,bhkv->bhtv', qc * jnp.exp(b), state)
        diff = b[:, :, :, None, :] - b[:, :, None, :, :]
        decay = jnp.exp(jnp.where(mask[:, :, None], diff, -jnp.inf))
        scores = jnp.einsum('bhtk,bhsk,bhtsk->bhts', qc, kc, decay)
        out = inter + jnp.einsum('bhts,bhsv->bhtv', scores, vc)
        b_last = b[:, :, -1, :]
        state = jnp.exp(b_last)[..., None] * state + jnp.einsum(
            'bhsk,bhsv->bhkv', kc * jnp.exp(b_last[:, :, None, :] - b), vc)
        return state, out

    init = jnp.zeros((B, H, dk, dv), jnp.float32)
    _, o = lax.scan(step, init, (to_chunks(q), to_chunks(k), to_chunks(v), to_chunks(g)))
    return o.transpose(1, 2, 0, 3, 4).reshape(B, H, S, dv)

def odd_mixer(h, w_in, w_gate, b_gate, norm_g, w_out):
    proj = h @ w_in
    q, k, v, r, g_lr = jnp.split(
        proj, [GLA_KEY, 2 * GLA_KEY, 2 * GLA_KEY + GLA_VAL, 2 * GLA_KEY + 2 * GLA_VAL], axis=-1)
    g = jax.nn.log_sigmoid((g_lr @ w_gate + b_gate).astype(jnp.float32)) / GATE_TAU
    f32 = jnp.float32
    qh = split_heads(q, GLA_HEADS).astype(f32) * (GLA_DK ** -0.5)
    kh = split_heads(k, GLA_HEADS).astype(f32)
    vh = split_heads(v, GLA_HEADS).astype(f32)
    gh = split_heads(g, GLA_HEADS)
    o = gla_chunked(qh, kh, vh, gh)
    o = merge_heads(rms_norm(o, norm_g)).astype(h.dtype)
    return (o * jax.nn.silu(r)) @ w_out

def first_inputs(seed: int = 0) -> dict:
    key = jax.random.key(seed)
    ks = jax.random.split(key, 20)
    f32 = jnp.float32

    def w(k, shape, fan_in):
        return jax.random.normal(k, shape, f32) * (fan_in ** -0.5)

    return {
        "x": jax.random.normal(ks[0], (BATCH, SEQ, D_MODEL), f32),
        "norm_g": 1.0 + 0.05 * jax.random.normal(ks[1], (DEPTH, N_NORMS, D_MODEL), f32),
        "ffn1_w_in": w(ks[2], (DEPTH, D_MODEL, 2 * D_FF), D_MODEL),
        "ffn1_w_out": w(ks[3], (DEPTH, D_FF, D_MODEL), D_FF),
        "ffn2_w_in": w(ks[4], (DEPTH, D_MODEL, 2 * D_FF), D_MODEL),
        "ffn2_w_out": w(ks[5], (DEPTH, D_FF, D_MODEL), D_FF),
        "hyb_w_in": w(ks[6], (N_EVEN, D_MODEL, EVEN_IN), D_MODEL),
        "hyb_w_out": w(ks[7], (N_EVEN, EVEN_OUT, D_MODEL), EVEN_OUT),
        "conv_dw_w": w(ks[8], (N_EVEN, CONV_WIDTH, CONV_CH), CONV_WIDTH),
        "conv_dw_b": 0.02 * jax.random.normal(ks[9], (N_EVEN, CONV_CH), f32),
        "conv_ln_g": 1.0 + 0.05 * jax.random.normal(ks[10], (N_EVEN, CONV_CH), f32),
        "conv_ln_b": 0.02 * jax.random.normal(ks[11], (N_EVEN, CONV_CH), f32),
        "gla_w_in": w(ks[12], (N_ODD, D_MODEL, ODD_IN), D_MODEL),
        "gla_w_gate": w(ks[13], (N_ODD, GATE_RANK, GLA_KEY), GATE_RANK),
        "gla_b_gate": 0.02 * jax.random.normal(ks[14], (N_ODD, GLA_KEY), f32),
        "gla_norm_g": 1.0 + 0.05 * jax.random.normal(ks[15], (N_ODD, GLA_DV), f32),
        "gla_w_out": w(ks[16], (N_ODD, GLA_VAL, D_MODEL), GLA_VAL),
    }

def first_block(x, norm_g, ffn1_w_in, ffn1_w_out, ffn2_w_in, ffn2_w_out,
              hyb_w_in, hyb_w_out, conv_dw_w, conv_dw_b, conv_ln_g, conv_ln_b,
              gla_w_in, gla_w_gate, gla_b_gate, gla_norm_g, gla_w_out):
    h = x
    for l in range(DEPTH):
        g = norm_g[l]
        f = swiglu(rms_norm(h, g[0]), ffn1_w_in[l], ffn1_w_out[l])
        h = h + FFN_RES * rms_norm(f, g[1])
        hn = rms_norm(h, g[2])
        if l % 2 == 0:
            e = l // 2
            m = even_mixer(hn, hyb_w_in[e], hyb_w_out[e], conv_dw_w[e], conv_dw_b[e],
                           conv_ln_g[e], conv_ln_b[e])
        else:
            o = l // 2
            m = odd_mixer(hn, gla_w_in[o], gla_w_gate[o], gla_b_gate[o], gla_norm_g[o],
                          gla_w_out[o])
        h = h + rms_norm(m, g[3])
        f = swiglu(rms_norm(h, g[4]), ffn2_w_in[l], ffn2_w_out[l])
        h = h + FFN_RES * rms_norm(f, g[5])
    return h


DEPTH_2 = 1

N_HEADS_A = 8
HEAD_DIM_A = 64
ROT_DIM = HEAD_DIM_A // 4
ROPE_THETA = 500000.0
N_HEADS_IDX = 8
HEAD_DIM_IDX = 64
TOPK_MAX = 256
Q_BLOCK = 128
N_HEADS_R = 4
HEAD_DIM_RK = 128
HEAD_DIM_RV = 256
RET_CHUNK = 128
RET_THETA = 10000.0
D_FF_2 = 2816
NEG = -1e30

SPLIT_SIZES = (
    N_HEADS_A * HEAD_DIM_A,
    N_HEADS_A * HEAD_DIM_A,
    N_HEADS_A * HEAD_DIM_A,
    N_HEADS_IDX * HEAD_DIM_IDX,
    HEAD_DIM_IDX,
    N_HEADS_IDX,
    N_HEADS_R * HEAD_DIM_RK,
    N_HEADS_R * HEAD_DIM_RK,
    N_HEADS_R * HEAD_DIM_RV,
    N_HEADS_R * HEAD_DIM_RV,
    D_MODEL,
    D_MODEL,
)
D_IN = sum(SPLIT_SIZES)


def _rmsnorm(x, w):
    xf = x.astype(jnp.float32)
    y = xf * lax.rsqrt(jnp.mean(xf * xf, axis=-1, keepdims=True) + NORM_EPS)
    return (y * w.astype(jnp.float32)).astype(x.dtype)

def _rope_tables(seq_len, dim, theta):
    inv = 1.0 / (theta ** (jnp.arange(0, dim, 2, dtype=jnp.float32) / dim))
    ang = jnp.arange(seq_len, dtype=jnp.float32)[:, None] * inv[None, :]
    return jnp.cos(ang), jnp.sin(ang)

def _rotate(x, cos, sin):
    x1, x2 = jnp.split(x, 2, axis=-1)
    cs, sn = cos[:, None, :], sin[:, None, :]
    return jnp.concatenate([x1 * cs - x2 * sn, x1 * sn + x2 * cs], axis=-1).astype(x.dtype)

def _partial_rope(x, cos, sin):
    return jnp.concatenate([_rotate(x[..., :ROT_DIM], cos, sin), x[..., ROT_DIM:]], axis=-1)

def _dsa_attention(q, k, v, iq, ik, iw, topk):
    B, S, H, Dh = q.shape
    n_blk = S // Q_BLOCK
    kpos = jnp.arange(S)
    ikf = ik.astype(jnp.float32)
    idx_scale = HEAD_DIM_IDX ** -0.5
    w_scale = N_HEADS_IDX ** -0.5
    att_scale = Dh ** -0.5

    def block(i):
        start = i * Q_BLOCK
        qb = lax.dynamic_slice_in_dim(q, start, Q_BLOCK, axis=1)
        iqb = lax.dynamic_slice_in_dim(iq, start, Q_BLOCK, axis=1).astype(jnp.float32)
        iwb = lax.dynamic_slice_in_dim(iw, start, Q_BLOCK, axis=1).astype(jnp.float32)
        qpos = start + jnp.arange(Q_BLOCK)
        causal = kpos[None, :] <= qpos[:, None]
        s_h = jnp.einsum('bqhd,bsd->bqhs', iqb, ikf) * idx_scale
        score = jnp.einsum('bqh,bqhs->bqs', iwb * w_scale, jax.nn.relu(s_h))
        score = jnp.where(causal[None], score, NEG)
        _, idx = lax.top_k(score, topk)
        valid = idx <= qpos[None, :, None]
        kg = jax.vmap(lambda kb, ib: kb[ib])(k, idx)
        vg = jax.vmap(lambda vb, ib: vb[ib])(v, idx)
        logits = jnp.einsum('bqhd,bqkhd->bqhk', qb, kg).astype(jnp.float32) * att_scale
        logits = jnp.where(valid[:, :, None, :], logits, NEG)
        p = jax.nn.softmax(logits, axis=-1).astype(v.dtype)
        return jnp.einsum('bqhk,bqkhd->bqhd', p, vg)

    out = lax.map(block, jnp.arange(n_blk))
    return jnp.moveaxis(out, 0, 1).reshape(B, S, H, Dh)

def _retention(q, k, v):
    B, S, H, Dk = q.shape
    Dv = v.shape[-1]
    C = RET_CHUNK
    N = S // C
    log_g = jnp.log(1.0 - 2.0 ** (-5.0 - jnp.arange(H, dtype=jnp.float32)))
    qc = q.astype(jnp.float32).reshape(B, N, C, H, Dk)
    kc = k.astype(jnp.float32).reshape(B, N, C, H, Dk)
    vc = v.astype(jnp.float32).reshape(B, N, C, H, Dv)
    j = jnp.arange(C, dtype=jnp.float32)
    diff = j[:, None] - j[None, :]
    dmask = jnp.where(diff[None] >= 0,
                      jnp.exp(log_g[:, None, None] * jnp.maximum(diff, 0.0)[None]), 0.0)
    inner = jnp.einsum('bnihd,bnjhd->bnhij', qc, kc) * dmask[None, None]
    o_in = jnp.einsum('bnhij,bnjhe->bnihe', inner, vc)
    kdec = jnp.exp(log_g[:, None] * (C - 1.0 - j)[None, :])
    u = jnp.einsum('bnjhd,hj,bnjhe->bnhde', kc, kdec, vc)
    cdec = jnp.exp(log_g * C)[None, :, None, None]

    def step(r, u_n):
        return r * cdec + u_n, r

    _, r_prev = lax.scan(step, jnp.zeros((B, H, Dk, Dv), jnp.float32), jnp.moveaxis(u, 1, 0))
    r_prev = jnp.moveaxis(r_prev, 0, 1)
    qdec = jnp.exp(log_g[None, :] * (j + 1.0)[:, None])
    o_x = jnp.einsum('bnihd,bnhde->bnihe', qc, r_prev) * qdec[None, None, :, :, None]
    return (o_in + o_x).reshape(B, S, H, Dv).astype(v.dtype)

def _head_groupnorm(o, w):
    of = o.astype(jnp.float32)
    mu = jnp.mean(of, axis=-1, keepdims=True)
    var = jnp.mean(jnp.square(of - mu), axis=-1, keepdims=True)
    y = (of - mu) * lax.rsqrt(var + NORM_EPS)
    B, S, H, Dv = o.shape
    return (y.reshape(B, S, H * Dv) * w.astype(jnp.float32)).astype(o.dtype)

def second_inputs(seed: int = 0) -> dict:
    key = jax.random.key(seed)
    ks = jax.random.split(key, 16)
    f32 = jnp.float32
    D = D_MODEL

    def lin(k, fi, fo):
        return jax.random.normal(k, (fi, fo), f32) * fi ** -0.5

    def gain(k, n):
        return 1.0 + 0.02 * jax.random.normal(k, (n,), f32)

    return {
        "x": jax.random.normal(ks[0], (BATCH, SEQ, D), f32),
        "c": jax.random.normal(ks[1], (BATCH, D), f32),
        "w_ada": lin(ks[2], D, 6 * D) * 0.5,
        "b_ada": 0.01 * jax.random.normal(ks[3], (6 * D,), f32),
        "norm1_w": gain(ks[4], D),
        "w_in": lin(ks[5], D, D_IN),
        "w_attn_proj": lin(ks[6], N_HEADS_A * HEAD_DIM_A, D),
        "w_ret_proj": lin(ks[7], N_HEADS_R * HEAD_DIM_RV, D),
        "gn_w": gain(ks[8], N_HEADS_R * HEAD_DIM_RV),
        "w_out": lin(ks[9], D, D),
        "norm2_w": gain(ks[10], D),
        "w_ffn_gate": lin(ks[11], D, D_FF_2),
        "w_ffn_up": lin(ks[12], D, D_FF_2),
        "w_ffn_down": lin(ks[13], D_FF_2, D),
        "final_norm_w": gain(ks[14], D),
    }

def second_block(x, c, w_ada, b_ada, norm1_w, w_in, w_attn_proj, w_ret_proj, gn_w, w_out,
              norm2_w, w_ffn_gate, w_ffn_up, w_ffn_down, final_norm_w):
    B, S, D = x.shape
    topk = min(TOPK_MAX, S // 4)
    cos_a, sin_a = _rope_tables(S, ROT_DIM, ROPE_THETA)
    cos_r, sin_r = _rope_tables(S, HEAD_DIM_RK, RET_THETA)

    mod = jnp.dot(jax.nn.silu(c), w_ada) + b_ada
    shift1, scale1, gate1, shift2, scale2, gate2 = [m[:, None, :] for m in jnp.split(mod, 6, axis=-1)]

    for _ in range(DEPTH_2):
        h = _rmsnorm(x, norm1_w) * (1.0 + scale1) + shift1
        proj = jnp.dot(h, w_in)
        (qa, ka, va, iq, ik, iw, qr, kr, vr, gr, ga, gb) = jnp.split(
            proj, np.cumsum(SPLIT_SIZES)[:-1], axis=-1)

        qa = _partial_rope(qa.reshape(B, S, N_HEADS_A, HEAD_DIM_A), cos_a, sin_a)
        ka = _partial_rope(ka.reshape(B, S, N_HEADS_A, HEAD_DIM_A), cos_a, sin_a)
        va = va.reshape(B, S, N_HEADS_A, HEAD_DIM_A)
        iq = _partial_rope(iq.reshape(B, S, N_HEADS_IDX, HEAD_DIM_IDX), cos_a, sin_a)
        ik = _partial_rope(ik[:, :, None, :], cos_a, sin_a)[:, :, 0, :]
        att = _dsa_attention(qa, ka, va, iq, ik, iw, topk)
        y_a = jnp.dot(att.reshape(B, S, N_HEADS_A * HEAD_DIM_A), w_attn_proj)

        qr = _rotate(qr.reshape(B, S, N_HEADS_R, HEAD_DIM_RK), cos_r, sin_r)
        kr = _rotate(kr.reshape(B, S, N_HEADS_R, HEAD_DIM_RK), cos_r, sin_r) * (HEAD_DIM_RK ** -0.5)
        ret = _retention(qr, kr, vr.reshape(B, S, N_HEADS_R, HEAD_DIM_RV))
        y_r = jnp.dot(jax.nn.silu(gr) * _head_groupnorm(ret, gn_w), w_ret_proj)

        merged = jax.nn.sigmoid(ga) * y_a + jax.nn.sigmoid(gb) * y_r
        x = x + gate1 * jnp.dot(merged, w_out)

        h2 = _rmsnorm(x, norm2_w) * (1.0 + scale2) + shift2
        ffn = jnp.dot(jax.nn.silu(jnp.dot(h2, w_ffn_gate)) * jnp.dot(h2, w_ffn_up), w_ffn_down)
        x = x + gate2 * ffn

    return _rmsnorm(x, final_norm_w)


def setup_inputs(seed=0):
    out = dict(first_inputs(seed))
    for name, value in second_inputs(seed + 1).items():
        if name != "x":
            out[name + "_2"] = value
    return out


def reference(
    x, norm_g, ffn1_w_in, ffn1_w_out, ffn2_w_in, ffn2_w_out, hyb_w_in, hyb_w_out, conv_dw_w,
    conv_dw_b, conv_ln_g, conv_ln_b, gla_w_in, gla_w_gate, gla_b_gate, gla_norm_g, gla_w_out,
    c_2, w_ada_2, b_ada_2, norm1_w_2, w_in_2, w_attn_proj_2, w_ret_proj_2, gn_w_2, w_out_2,
    norm2_w_2, w_ffn_gate_2, w_ffn_up_2, w_ffn_down_2, final_norm_w_2,
):
    x = first_block(
        x, norm_g, ffn1_w_in, ffn1_w_out, ffn2_w_in, ffn2_w_out, hyb_w_in, hyb_w_out, conv_dw_w,
        conv_dw_b, conv_ln_g, conv_ln_b, gla_w_in, gla_w_gate, gla_b_gate, gla_norm_g,
        gla_w_out,
    )
    return second_block(
        x, c_2, w_ada_2, b_ada_2, norm1_w_2, w_in_2, w_attn_proj_2, w_ret_proj_2, gn_w_2,
        w_out_2, norm2_w_2, w_ffn_gate_2, w_ffn_up_2, w_ffn_down_2, final_norm_w_2,
    )


_drawn_inputs = setup_inputs


def setup_inputs(seed=0):
    import zlib

    import numpy as np

    out = dict(_drawn_inputs(seed))
    spreads = {}
    factors = {'conv_ln_b': 3.476,
     'gla_b_gate': 8.0,
     'b_ada_2': 8.0,
     'norm1_w_2': 8.0,
     'gn_w_2': 8.0,
     'norm2_w_2': 8.0,
     'final_norm_w_2': 2.85}
    for name, (base, spread) in spreads.items():
        noise = np.random.default_rng([zlib.crc32(name.encode()), seed]).standard_normal(out[name].shape)
        drawn = base * np.exp(spread * noise) if base else spread * noise
        out[name] = __import__('jax').numpy.asarray(drawn.astype(out[name].dtype))
    for name, factor in factors.items():
        out[name] = (out[name] * factor).astype(out[name].dtype)
    return out
```

```python
from contextlib import ExitStack

import numpy as np

import concourse.bass as bass
from concourse import mybir

P = 128
D = 1024
FF = 2816
F32 = mybir.dt.float32
F32R = mybir.dt.float32r
U32 = mybir.dt.uint32
ALU = mybir.AluOpType
ACT = mybir.ActivationFunctionType
AX = mybir.AxisListType
EPS = 1e-6
BIG = 3e38
NEG = -1e30

NRAW = 4
NSPL = 3
LOOK = 2
UPTO = 99


class Lane:

    def __init__(self, sem):
        self.sem, self.n, self.ops, self.seen = sem, 0, [], {}

    def wait(self, *after):
        for t in after:
            if t is None:
                continue
            if isinstance(t, list):
                self.wait(*t)
                continue
            sem, v = t
            if self.seen.get(id(sem), 0) < v:
                self.seen[id(sem)] = v
                self.ops.append(lambda e, sem=sem, v=v: e.wait_ge(sem, v))

    def __call__(self, fn, *after):
        self.wait(*after)
        self.n += 1
        self.ops.append(lambda e: fn(e).then_inc(self.sem, 1))
        return (self.sem, self.n)

    def dma(self, dst, src, sem, count, *after):
        self.wait(*after)
        self.ops.append(lambda e: e.dma_start(dst, src).then_inc(sem, 16))
        return (sem, count)

    def run(self, e):
        for op in self.ops:
            op(e)


class Banks:

    def __init__(self, banks):
        self.banks, self.free, self.i = banks, [[] for _ in banks], 0

    def get(self):
        k = self.i % len(self.banks)
        self.i += 1
        waits, self.free[k] = self.free[k], None
        assert waits is not None
        return k, self.banks[k], waits

    def put(self, k, *tokens):
        self.free[k] = list(tokens)


def constants():
    i = np.arange(P)
    cols = {}
    cols["ident"] = np.eye(P)
    cols["tri"] = i[:, None] >= i[None, :]
    valid = i[:, None] < i[None, :]
    cols["mmin"] = np.concatenate([np.where(valid, BIG, 0.0), np.full((P, P), BIG), np.where(valid, BIG, 0.0)], 1)
    cols["mmax"] = -cols["mmin"]
    cols["caus"] = np.where(i[None, :] <= i[:, None], 0.0, NEG)
    lev = [np.eye(P)]
    for m in (1, 2, 4, 8, 16, 32, 64):
        same = (i[:, None] // (2 * m)) == (i[None, :] // (2 * m))
        lev.append(same & (i[:, None] % (2 * m) < m) & (i[None, :] % (2 * m) >= m))
    cols["lev"] = np.concatenate(lev, 1)
    dec = []
    for h in range(4):
        lg = float(np.log(np.float32(1.0 - 2.0 ** (-5.0 - h))))
        dt = i[None, :] - i[:, None]
        dec.append(np.where(dt >= 0, np.exp(lg * np.maximum(dt, 0)), 0.0) * P ** -0.5)
        dec.append(np.exp(lg * (dt + P)) * P ** -0.5)
    cols["dec"] = np.concatenate(dec, 1)
    for nm, dim, theta in (("a", 16, 500000.0), ("r", 128, 10000.0)):
        f32 = np.float32
        inv = f32(1.0) / (f32(theta) ** (np.arange(0, dim, 2, dtype=f32) / f32(dim)))
        ang = (np.arange(256, dtype=f32)[:, None] * inv[None, :]).astype(np.float64)
        for fn, f in (("cos", np.cos), ("sin", np.sin)):
            cols[fn + nm] = np.concatenate([f(ang[:P]), f(ang[P:])], 1)
    at, parts, n = {}, [], 0
    for k in [k for k in cols if k not in ("lev", "dec")] + ["lev", "dec"]:
        v = cols[k]
        v = np.asarray(v, np.float32)
        at[k] = (n, v.shape[1])
        n += v.shape[1]
        parts.append(v)
    return at, np.ascontiguousarray(np.concatenate(parts, 1))


def program(nc, T, const_at, out):
    ctx = ExitStack()
    with ctx:
        def sb(name, cols, dt=F32, parts=P, where=ctx):
            return where.enter_context(nc.sbuf_tensor(name, [parts, cols], dt))

        def sem(name):
            return ctx.enter_context(nc.semaphore(name))

        psum = [ctx.enter_context(nc.psum_tensor(f"ps{i}", [P, 512], F32)) for i in range(8)]
        acc = Banks(psum[:6])
        tb = Banks(psum[6:])
        pe, act, dve, pool, sp = (Lane(sem(n)) for n in ("s_pe", "s_act", "s_dve", "s_pool", "s_sp"))

        nconst = const_at["lev"][0]
        cst = sb("cst", nconst)
        adat = [sb(f"adat{i}", 512) for i in range(2)]
        adaacc = sb("adaacc", 512)
        modc = sb("modc", 48)
        scol = sb("scol", 16)
        s_ada = [sem(f"s_ada{i}") for i in range(2)]
        vcol = sb("vcol", 3 * P)
        h = sb("h", 2 * D)
        xh = sb("xh", 8 * 256, F32R)
        xl = sb("xl", 8 * 256, F32R)
        raw = [sb(f"raw{i}", 2048) for i in range(NRAW)]
        whi = [sb(f"whi{i}", 2048, F32R) for i in range(NSPL)]
        wlo = [sb(f"wlo{i}", 2048, F32R) for i in range(NSPL)]
        rows = [sb(f"row{i}", D) for i in range(2)]
        st = sb("st", 512)
        junk = sb("junk", 1024)
        xtmp = [junk[:, 0:512], junk[:, 512:1024]]
        vin = raw[NRAW - 1][:, 0:3 * P]
        hid = [sb(f"hid{i}", 1024) for i in range(2)]
        s_raw = [sem(f"s_raw{i}") for i in range(NRAW)]
        s_row = [sem(f"s_row{i}") for i in range(2)]
        s_in = sem("s_in")
        s_out = sem("s_out")

        def C(name, a=0, n=None):
            o, w = const_at[name]
            n = w - a if n is None else n
            return cst[:, o + a:o + a + n]

        ident = C("ident")

        t_in = []

        def load(dst, src):
            t_in.append(None)
            sp.dma(dst, src, s_in, 0)

        n_in = 0
        for b in range(2):
            sp.dma(h[:, b * D:(b + 1) * D], T["x"][0, b * P:(b + 1) * P, :], s_in, 0)
            n_in += 1
        sp.dma(cst[:, :], T["const"][:, 0:nconst], s_in, 0)
        sp.dma(vin[0:96, 0:P], T["norm_g"].rearrange("l n (b p) -> (l n b) p", p=P), s_in, 0)
        n_in += 2
        VR = {}
        r = 0
        for nm, src in (("n1", T["norm1_w_2"]), ("n2", T["norm2_w_2"]), ("ba", T["b_ada_2"]), ("bg", T["gla_b_gate"][0]), ("cb", T["conv_dw_b"][0]),
                        ("lg", T["conv_ln_g"][0]), ("lb", T["conv_ln_b"][0])):
            k = src.shape[0] // P
            sp.dma(vin[r:r + k, P:2 * P], src.rearrange("(b p) -> b p", p=P), s_in, 0)
            n_in += 1
            VR[nm] = P + r
            r += k
        sp.dma(vin[0:124, 2 * P:3 * P], T["conv_dw_w"][0].rearrange("k (b p) -> (k b) p", p=P), s_in, 0)
        n_in += 1
        VR["cw"] = 2 * P
        sp.dma(scol[:, 0:8], T["c_2"].rearrange("a (p k) -> (a p) k", k=8), s_in, 0)
        n_in += 1
        t_in = (s_in, 16 * n_in)
        t_scol = act(lambda e: e.activation(scol[:, 8:16], scol[:, 0:8], ACT.Silu), t_in)
        nvec = {0: 96, 1: r, 2: 124}

        k0, bank, w0 = tb.get()

        def f(e):
            for j in range(3):
                last = e.transpose(bank[:, j * P:j * P + nvec[j]], vin[0:nvec[j], j * P:(j + 1) * P],
                                   ident[0:nvec[j], 0:nvec[j]])
            return last
        t = pe(f, t_in, w0)

        def f(e):
            for j in range(3):
                last = e.tensor_copy(vcol[:, j * P:j * P + nvec[j]], bank[:, j * P:j * P + nvec[j]])
            return last
        t_vec = dve(f, t)
        tb.put(k0, t_vec)

        plan = []

        def plan_cols(w, c0, n, nk):
            for k in range(0, nk, 4):
                m = min(4, nk - k)
                plan.append((w[k * P:(k + m) * P, c0:c0 + n].rearrange("(k p) n -> p k n", p=P), m, n))

        def plan_ffn(w_in, w_out):
            for c in range(11):
                for k in (0, 4):
                    if len(w_in) == 1:
                        v = w_in[0][k * P:(k + 4) * P, :].rearrange("(k p) (a n) -> p k a n", p=P, a=2)
                        plan.append((v[:, :, :, c * 256:(c + 1) * 256], 4, 512))
                    else:
                        plan.append(([w[k * P:(k + 4) * P, c * 256:(c + 1) * 256]
                                      .rearrange("(k p) n -> p k n", p=P) for w in w_in], 4, 512))
            for k in range(0, 22, 4):
                m = min(4, 22 - k)
                for n in range(2):
                    plan.append((w_out[k * P:(k + m) * P, n * 512:(n + 1) * 512]
                                 .rearrange("(k p) n -> p k n", p=P), m, 512))

        bg = []

        def pump(n):
            while bg and n > 0:
                bg.pop(0)()
                n -= 1

        unit = {"load": 0, "split": 0, "use": 0}
        t_load, t_split, t_used = [], [], []
        nraw_sem = [0] * NRAW

        def load_unit():
            i = unit["load"]
            unit["load"] += 1
            s = i % NRAW
            src, m, n = plan[i]
            after = t_split[i - NRAW] if i >= NRAW else (t_vec if i == NRAW - 1 else None)
            dst = raw[s][:, 0:m * n]
            if isinstance(src, list):
                dst = dst.rearrange("p (k a n) -> p k a n", k=m, a=2)
                for a in range(2):
                    nraw_sem[s] += 16
                    sp.dma(dst[:, :, a, :], src[a], s_raw[s], 0, after)
            else:
                if len(src.shape) == 4:
                    dst4 = dst.rearrange("p (k a n) -> p k a n", k=m, a=2)
                    for a in range(2):
                        nraw_sem[s] += 16
                        sp.dma(dst4[:, :, a, :], src[:, :, a, :], s_raw[s], 0, after)
                else:
                    nraw_sem[s] += 16
                    sp.dma(dst.rearrange("p (k n) -> p k n", k=m), src, s_raw[s], 0, after)
            t_load.append((s_raw[s], nraw_sem[s]))
            if i >= 8 and UPTO >= 7:
                ada_load()

        def split_unit():
            i = unit["split"]
            unit["split"] += 1
            if unit["load"] <= i:
                load_unit()
            _, m, n = plan[i]
            r, a, b = raw[i % NRAW], whi[i % NSPL], wlo[i % NSPL]
            used = t_used[i - NSPL] if i >= NSPL else None
            ta = act(lambda e: e.activation(a[:, 0:m * n], r[:, 0:m * n], ACT.Copy), t_load[i], used)
            tl = dve(lambda e: e.tensor_tensor(b[:, 0:m * n], r[:, 0:m * n], a[:, 0:m * n].bitcast(F32),
                                               ALU.subtract), ta, t_load[i], used)
            t_split.append([ta, tl])
            while unit["load"] < min(len(plan), i + NRAW + 1):
                load_unit()

        def next_unit():
            i = unit["use"]
            unit["use"] += 1
            while unit["split"] < min(len(plan), i + LOOK + 1) and unit["split"] < i + NSPL:
                split_unit()
            pump(PUMP[0])
            if "due" in ada and unit["load"] >= ada["due"][2] + 3:
                ada_reduce()
            return i

        PUMP = [0]

        def mms(e, ps, i, XH, XL, kb0, tok, m, n, first, final):
            for k in range(m):
                a = XH[:, (kb0 + k) * 256 + tok * P:(kb0 + k) * 256 + (tok + 1) * P]
                b = XL[:, (kb0 + k) * 256 + tok * P:(kb0 + k) * 256 + (tok + 1) * P]
                wh = whi[i % NSPL][:, k * n:(k + 1) * n]
                wl = wlo[i % NSPL][:, k * n:(k + 1) * n]
                e.matmul(ps[:, 0:n], a, wh, start=first and k == 0, stop=False)
                e.matmul(ps[:, 0:n], a, wl, start=False, stop=False)
                last = e.matmul(ps[:, 0:n], b, wh, start=False, stop=final and k == m - 1)
            return last

        def linear(XH, XL, ready, nk, nchunk, evac):
            for c in range(nchunk):
                bk = [acc.get() for _ in range(2)]
                tok_t = [None, None]
                for k in range(0, nk, 4):
                    i = next_unit()
                    _, m, n = plan[i]
                    for tok in range(2):
                        ps = bk[tok][1]
                        tok_t[tok] = pe(lambda e, ps=ps, i=i, k=k, tok=tok, m=m, n=n:
                                        mms(e, ps, i, XH, XL, k, tok, m, n, k == 0, k + m == nk),
                                        t_split[i], [ready[q] for q in range(k, k + m)], bk[tok][2])
                    t_used.append(tok_t[1])
                for tok in range(2):
                    acc.put(bk[tok][0], *evac(c, tok, bk[tok][1], tok_t[tok]))

        ones = sb("ones", P)
        t_ones = dve(lambda e: e.memset(ones[:, :], 1.0))

        st_i = [0]

        def col(n=1):
            if st_i[0] + n > 512:
                st_i[0] = 0
            o = st_i[0]
            st_i[0] += n
            return st[:, o:o + n]

        def rstd(ss, nparts, count, *after):
            if nparts == 2:
                v = col()
                t = dve(lambda e: e.tensor_tensor(v, ss[:, 0:1], ss[:, 1:2], ALU.add), *after)
            else:
                v, t = ss, list(after)
            w, r1, r2 = col(), col(), col()
            t = dve(lambda e: e.tensor_scalar(w, v, 1.0 / count, EPS, ALU.mult, ALU.add), t)
            t = act(lambda e: e.activation(r1, w, ACT.Sqrt), t)
            t = dve(lambda e: e.reciprocal(r2, r1), t)
            return r2, t

        row_n = [0]
        row_cnt = [0, 0]
        row_free = [None, None]

        def row_load(src, n):
            s = row_n[0] % 2
            row_n[0] += 1
            row_cnt[s] += 16
            cnt = row_cnt[s]
            sp.dma(rows[s][:, 0:n], src.rearrange("(a n) -> a n", a=1).to_broadcast([P, n]), s_row[s], 0,
                   row_free[s])
            return s, rows[s], (s_row[s], cnt)

        def transposes(src, ready, ps, dst_cols, waits):
            def f(e):
                for a, c in zip(src, dst_cols):
                    last = e.transpose(ps[:, c:c + P], a, ident)
                return last
            return pe(f, ready, waits)

        xfree = [None] * 8

        def to_x(hready, gcol):
            ready = []
            for kb in range(0, 8, 2):
                k0, ps, w0 = tb.get()
                src = [h[:, tok * D + (kb + j) * P:tok * D + (kb + j + 1) * P] for j in range(2) for tok in range(2)]
                t = transposes(src, hready, ps, [0, P, 2 * P, 3 * P], w0)
                ta = []
                for j in range(2):
                    g = vcol[:, gcol + kb + j:gcol + kb + j + 1]
                    sl = slice((kb + j) * 256, (kb + j + 1) * 256)
                    ta.append(act(lambda e, g=g, sl=sl, j=j, ps=ps: e.activation(
                        xh[:, sl], ps[:, j * 256:(j + 1) * 256], ACT.Copy, scale=g), t, t_vec, xfree[0]))
                for j in range(2):
                    g = vcol[:, gcol + kb + j:gcol + kb + j + 1]
                    sl = slice((kb + j) * 256, (kb + j + 1) * 256)
                    b = dve(lambda e, g=g, sl=sl, j=j, ps=ps: e.scalar_tensor_tensor(
                        xl[:, sl], ps[:, j * 256:(j + 1) * 256], g, xh[:, sl].bitcast(F32), ALU.mult,
                        ALU.subtract), ta, t_vec)
                    ready.append([ta[j], b])
                tb.put(k0, ready[-1])
            return ready

        junk_t = [None, None]
        junk_n = [0]

        def sumsq(src, o, *after):
            k = junk_n[0] % 2
            junk_n[0] += 1
            w = src.shape[1]
            junk_t[k] = act(lambda e: e.activation(junk[:, k * 512:k * 512 + w], src, ACT.Square, accum_out=o),
                            junk_t[k], *after)
            return junk_t[k]

        def h_stats(tok, *after):
            ss = col(2)
            ts = [sumsq(h[:, tok * D + n * 512:tok * D + (n + 1) * 512], ss[:, n:n + 1], *after) for n in range(2)]
            return rstd(ss, 2, D, ts)

        def ffn_body(gT_h, gT_l, ready, rs):
            gready = [None] * 22
            pend = []
            hid_free = [None, None]

            def flush():
                c, ths = pend.pop(0)
                hb = hid[c % 2]
                k0, ps, w0 = tb.get()
                src = [hb[:, tok * 512 + j * P:tok * 512 + (j + 1) * P] for j in range(2) for tok in range(2)]
                t = transposes(src, ths, ps, [0, P, 2 * P, 3 * P], w0)
                hid_free[c % 2] = t
                sl = slice(c * 512, (c + 1) * 512)
                a = act(lambda e: e.activation(gT_h[:, sl], ps[:, :], ACT.Copy), t, gfree[0])
                b = dve(lambda e: e.tensor_tensor(gT_l[:, sl], ps[:, :], gT_h[:, sl].bitcast(F32), ALU.subtract),
                        a, gfree[0])
                tb.put(k0, b)
                gready[2 * c] = gready[2 * c + 1] = [a, b]

            def evac(c, tok, ps, t):
                hb = hid[c % 2]
                s1 = hb[:, tok * 512 + 256:tok * 512 + 512]
                s2 = hb[:, tok * 512:tok * 512 + 256]
                sc, tsc = rs[tok] if rs else (1.0, None)
                a = act(lambda e: e.activation(s1, ps[:, 0:256], ACT.Silu, scale=sc), t, tsc, hid_free[c % 2])
                b = dve(lambda e: e.scalar_tensor_tensor(s2, ps[:, 256:512], sc, s1, ALU.mult, ALU.mult),
                        a, t, tsc)
                if tok == 0:
                    if pend:
                        flush()
                    pend.append((c, [b]))
                else:
                    pend[-1][1].append(b)
                return [a, b]

            linear(xh, xl, ready, 8, 11, evac)
            xfree[0] = (pe.sem, pe.n)
            flush()
            return gready

        gfree = [None]

        def down(XH, XL, ready, nk):
            bk = [[acc.get() for _ in range(2)] for _ in range(2)]
            tt = [[None, None], [None, None]]
            for k in range(0, nk, 4):
                for n in range(2):
                    i = next_unit()
                    _, m, w = plan[i]
                    for tok in range(2):
                        k0, ps, w0 = bk[tok][n]
                        tt[tok][n] = pe(lambda e, ps=ps, i=i, k=k, tok=tok, m=m: mms(
                            e, ps, i, XH, XL, k, tok, m, 512, k == 0, k + m == nk),
                            t_split[i], [ready[q] for q in range(k, k + m)], w0)
                    t_used.append(tt[1][n])
            gfree[0] = (pe.sem, pe.n)
            return [[(bk[tok][n][1], bk[tok][n][0], tt[tok][n]) for n in range(2)] for tok in range(2)]

        def residual(res, factor, gain):
            s, row, trow = gain
            ready = []
            for tok in range(2):
                ss = col(2)
                ts = [sumsq(res[tok][n][0][:, :], ss[:, n:n + 1], res[tok][n][2]) for n in range(2)]
                r1, tr = rstd(ss, 2, D, ts)
                for n in range(2):
                    ps, k0, t = res[tok][n]
                    hs = h[:, tok * D + n * 512:tok * D + (n + 1) * 512]
                    a = dve(lambda e, ps=ps, n=n, r1=r1: e.scalar_tensor_tensor(
                        ps[:, :], ps[:, :], r1, row[:, n * 512:(n + 1) * 512], ALU.mult, ALU.mult), tr, trow, t, ts)
                    b = dve(lambda e, ps=ps, hs=hs: e.scalar_tensor_tensor(
                        hs, ps[:, :], factor, hs, ALU.mult, ALU.add), a)
                    acc.put(k0, b)
                ready.append(b)
            row_free[s] = ready[-1]
            return ready

        def ffn_stage(hready, gcol, gain_src):
            gain = row_load(gain_src, D)
            ready = to_x(hready, gcol)
            rs = [h_stats(tok, hready[tok]) for tok in range(2)]
            with ExitStack() as inner:
                gh = sb(f"gh{gcol}", 22 * 256, F32R, where=inner)
                gl = sb(f"gl{gcol}", 22 * 256, F32R, where=inner)
                gready = ffn_body(gh, gl, ready, rs)
                res = down(gh, gl, gready, 22)
            return residual(res, 0.5, gain)

        def to_T(src, ready, dst, nblk, scale, eng, parts=P, after=None):
            ts = []
            for b0 in range(0, nblk, 2):
                nb = min(2, nblk - b0)
                k0, ps, w0 = tb.get()
                tiles, cs = [], []
                for j in range(nb):
                    for tok in range(2):
                        tiles.append(src(tok)[:, (b0 + j) * P:(b0 + j + 1) * P])
                        cs.append(j * 256 + tok * P)
                t = transposes(tiles, ready, ps, cs, w0)
                v = ps[:, 0:nb * 256].rearrange("p (b n) -> p b n", b=nb)
                o = dst[:, b0:b0 + nb, :]
                if eng is act:
                    t = act(lambda e, o=o, v=v: e.activation(o, v, ACT.Copy, scale=scale), t, after)
                else:
                    t = dve(lambda e, o=o, v=v: e.tensor_scalar(o, v, scale, None, ALU.mult), t, after)
                tb.put(k0, t)
                ts += [t] * nb
            return ts

        def split_to_x(src, sl, ready):
            a = act(lambda e: e.activation(xh[:, sl], src, ACT.Copy), ready, xfree[0])
            b = dve(lambda e: e.tensor_tensor(xl[:, sl], src, xh[:, sl].bitcast(F32), ALU.subtract), a, ready)
            return [a, b]

        def hybrid_stage(hready):
            gain = row_load(T["norm_g"][0, 3], D)
            ready = to_x(hready, 2 * 8)
            rs = [h_stats(tok, hready[tok]) for tok in range(2)]
            with ExitStack() as inner:
                cx = sb("cx", 4 * 286, where=inner)
                Y = sb("Y", 4 * 256, where=inner)
                SQ = sb("SQ", 4 * 256, where=inner)
                qt = sb("qt", 1024, where=inner)
                kt = sb("kt", 1024, where=inner)
                vt = sb("vt", 1024, where=inner)
                qT = sb("qT", 1024, where=inner)
                kT = sb("kT", 1024, where=inner)
                eb = [sb(f"eb{i}", 384, where=inner) for i in range(3)]
                mb = [sb(f"mb{i}", 384, where=inner) for i in range(3)]
                wb = [sb(f"wb{i}", 384, where=inner) for i in range(3)]
                rb = sb("rb", 512, where=inner)
                cx3 = cx[:, :].rearrange("p (b n) -> p b n", b=4)
                sg, ct = hid[0], hid[1]
                t_pad = dve(lambda e: e.memset(cx3[:, :, 0:30], 0.0), (pe.sem, pe.n), (act.sem, act.n))
                st_tok = {}

                def evac(c, tok, ps, t):
                    sc, tsc = rs[tok]
                    o = slice(tok * 512, (tok + 1) * 512)
                    if c == 0:
                        a = act(lambda e: e.activation(sg[:, o], ps[:, :], ACT.Sigmoid, scale=sc), t, tsc,
                                (pe.sem, pe.n), (dve.sem, dve.n))
                        st_tok["g", tok] = a
                        return [a]
                    if c == 1:
                        a = dve(lambda e: e.scalar_tensor_tensor(ct[:, o], ps[:, :], sc, sg[:, o], ALU.mult, ALU.mult),
                                t, tsc, st_tok["g", tok])
                        st_tok["c", tok] = a
                        return [a]
                    dst = {2: qt, 3: kt, 4: vt}[c]
                    a = act(lambda e: e.activation(dst[:, o], ps[:, :], ACT.Copy, scale=sc), t, tsc, t_pad)
                    st_tok[c, tok] = a
                    return [a]

                def after_u():
                    tc = to_T(lambda tok: ct[:, tok * 512:(tok + 1) * 512], [st_tok["c", 0], st_tok["c", 1]],
                              cx3[:, :, 30:286], 4, 1.0, act, after=t_pad)
                    ty = [None] * 4

                    def tap(b, k):
                        def f():
                            y = Y[:, b * 256:(b + 1) * 256]
                            x = cx[:, b * 286 + k:b * 286 + k + 256]
                            w = vcol[:, VR["cw"] + k * 4 + b:VR["cw"] + k * 4 + b + 1]
                            if k == 0:
                                bias = vcol[:, VR["cb"] + b:VR["cb"] + b + 1]
                                ty[b] = dve(lambda e: e.tensor_scalar(y, x, w, bias, ALU.mult, ALU.add),
                                            tc[b], t_pad, t_vec)
                            else:
                                ty[b] = dve(lambda e: e.scalar_tensor_tensor(y, x, w, y, ALU.mult, ALU.add), ty[b])
                        return f
                    for k in range(31):
                        for b in range(4):
                            bg.append(tap(b, k))
                    return ty

                PUMP[0] = 8
                linear(xh, xl, ready, 8, 2, evac)
                ty = after_u()
                linear(xh, xl, ready, 8, 3, lambda c, tok, ps, t: evac(c + 2, tok, ps, t))
                xfree[0] = (pe.sem, pe.n)
                v4 = lambda z: z[:, :].rearrange("p (b n) -> p b n", b=4)
                tq = to_T(lambda tok: qt[:, tok * 512:(tok + 1) * 512], [st_tok[2, 0], st_tok[2, 1]], v4(qT), 4,
                          0.125, act)
                tk = to_T(lambda tok: kt[:, tok * 512:(tok + 1) * 512], [st_tok[3, 0], st_tok[3, 1]], v4(kT), 4,
                          1.0, act)
                tv = [st_tok[4, 0], st_tok[4, 1]]

                Z = {}
                wfree = [None] * 3
                ld = {}
                wd = {}

                def scores(hd):
                    p0, b = 64 * (hd % 2), hd // 2
                    k0, ps, w0 = acc.get()

                    def f(e):
                        q, k = qT[p0:p0 + 64, b * 256:(b + 1) * 256], kT[p0:p0 + 64, b * 256:(b + 1) * 256]
                        e.matmul(ps[:, 0:256], k[:, 0:P], q, start=True, stop=True)
                        return e.matmul(ps[:, 256:384], k[:, P:256], q[:, P:256], start=False, stop=True,
                                        skip_group_check=True)
                    t = pe(f, tq[b], tk[b], w0)
                    z, s = ps[:, 0:384], hd % 3
                    E, M = eb[s][:, :], mb[s][:, :]
                    t1 = act(lambda e: e.activation(E, z, ACT.Abs), t, wfree[s])
                    t2 = act(lambda e: e.activation(E, E, ACT.Exp, scale=-1.0), t1)
                    t3 = act(lambda e: e.activation(E, E, ACT.Ln, bias=1.0), t2)
                    t4 = dve(lambda e: e.tensor_scalar(M, z, -1.0, 0.0, ALU.mult, ALU.min), t1, t, wfree[s])
                    t5 = dve(lambda e: e.tensor_tensor(M, M, E, ALU.subtract), t3, t4)
                    t6 = dve(lambda e: e.tensor_tensor(M, M, C("mmax"), ALU.max), t5)
                    Z[hd] = (k0, ps)
                    ld[hd] = t6

                def weights(hd):
                    k0, ps = Z[hd]
                    s = hd % 3
                    M, W = mb[s], wb[s][:, :]

                    def f(e):
                        e.matmul(ps[:, 0:384], C("tri"), M[:, 0:384], start=False, stop=True, skip_group_check=True)
                        return e.matmul(ps[:, P:256], ones[:, :], M[:, 256:384], start=False, stop=True,
                                        skip_group_check=True)
                    t = pe(f, ld[hd], t_ones)
                    t1 = act(lambda e: e.activation(W, ps[:, 0:384], ACT.Exp), t, wfree[s])
                    acc.put(k0, t1)
                    wd[hd] = dve(lambda e: e.tensor_tensor(W, W, C("mmin"), ALU.min), t1)

                pv = {}

                def values(hd):
                    s, p0, b = hd % 3, 64 * (hd % 2), hd // 2
                    if hd % 2 == 0:
                        pv[b] = acc.get()
                    k0, ps, w0 = pv[b]

                    def f(e):
                        o = ps[p0:p0 + 64, 0:256]
                        e.matmul(o, vt[:, hd * 64:(hd + 1) * 64], wb[s][:, 0:256], start=True, stop=True)
                        return e.matmul(ps[p0:p0 + 64, P:256], vt[:, 512 + hd * 64:512 + (hd + 1) * 64],
                                        wb[s][:, 256:384], start=False, stop=True, skip_group_check=True)
                    wfree[s] = pe(f, wd[hd], tv, w0)
                    if hd % 2 == 1:
                        xr = split_to_x(ps[:, 0:256], slice(b * 256, (b + 1) * 256), wfree[s])
                        acc.put(k0, *xr)
                        return xr

                xr = [None] * 8
                for s in range(10):
                    if s < 8:
                        scores(s)
                    if 0 <= s - 1 < 8:
                        weights(s - 1)
                    if 0 <= s - 2 < 8:
                        r = values(s - 2)
                        if r:
                            xr[(s - 2) // 2] = r
                    pump(12)
                pump(1000)

                k0, ps, w0 = acc.get()

                def f(e):
                    for b in range(4):
                        last = e.matmul(ps[:, 0:256], ones[:, :], Y[:, b * 256:(b + 1) * 256], start=b == 0,
                                        stop=b == 3)
                    return last
                t = pe(f, ty, t_ones, w0)
                tq2 = []
                for b in range(4):
                    y = Y[:, b * 256:(b + 1) * 256]
                    t1 = dve(lambda e, y=y: e.scalar_tensor_tensor(y, ps[:, 0:256], -1.0 / 512, y, ALU.mult, ALU.add),
                             t, ty[b])
                    tq2.append(act(lambda e, b=b, y=y: e.activation(SQ[:, b * 256:(b + 1) * 256], y, ACT.Square), t1,
                                   t_pad))
                acc.put(k0, t1)
                k0, ps2, w0 = acc.get()

                def f(e):
                    for b in range(4):
                        last = e.matmul(ps2[:, 0:256], ones[:, :], SQ[:, b * 256:(b + 1) * 256], start=b == 0,
                                        stop=b == 3)
                    return last
                t = pe(f, tq2, w0)
                t = dve(lambda e: e.tensor_scalar(rb[:, 0:256], ps2[:, 0:256], 1.0 / 512, EPS, ALU.mult, ALU.add), t)
                acc.put(k0, t)
                t = act(lambda e: e.activation(rb[:, 256:512], rb[:, 0:256], ACT.Sqrt), t)
                t = dve(lambda e: e.reciprocal(rb[:, 0:256], rb[:, 256:512]), t)
                for b in range(4):
                    y = Y[:, b * 256:(b + 1) * 256]
                    q = SQ[:, b * 256:(b + 1) * 256]
                    t1 = dve(lambda e, y=y: e.tensor_tensor(y, y, rb[:, 0:256], ALU.mult), t)
                    g = vcol[:, VR["lg"] + b:VR["lg"] + b + 1]
                    bb = vcol[:, VR["lb"] + b:VR["lb"] + b + 1]
                    t2 = act(lambda e, y=y, q=q, g=g, bb=bb: e.activation(q, y, ACT.Silu, scale=g, bias=bb), t1)
                    xr[4 + b] = split_to_x(q, slice((4 + b) * 256, (5 + b) * 256), t2)
                PUMP[0] = 0
                res = down(xh, xl, xr, 8)
                xfree[0] = (pe.sem, pe.n)
            return residual(res, 1.0, gain)

        def to_x2(src, hready):
            ready = []
            for kb in range(0, 8, 2):
                k0, ps, w0 = tb.get()
                tiles = [src(tok)[:, (kb + j) * P:(kb + j + 1) * P] for j in range(2) for tok in range(2)]
                t = transposes(tiles, hready, ps, [0, P, 2 * P, 3 * P], w0)
                r = split_to_x(ps[:, :], slice(kb * 256, (kb + 2) * 256), t)
                tb.put(k0, *r)
                ready += [r, r]
            return ready

        def rstd_n(ss, n, count, *after):
            w, r1, r2 = col(n), col(n), col(n)
            t = dve(lambda e: e.tensor_scalar(w, ss, 1.0 / count, EPS, ALU.mult, ALU.add), *after)
            t = act(lambda e: e.activation(r1, w, ACT.Sqrt), t)
            t = dve(lambda e: e.reciprocal(r2, r1), t)
            return r2, t

        def gla_stage(hready):
            gain = row_load(T["norm_g"][1, 3], D)
            grow = row_load(T["gla_norm_g"][0], 256)
            ready = to_x(hready, (6 + 2) * 8)
            rs = [h_stats(tok, hready[tok]) for tok in range(2)]
            with ExitStack() as inner:
                B = sb("gB", 1024, where=inner)
                QT = sb("gQT", 1024, where=inner)
                KT = sb("gKT", 1024, where=inner)
                X = [sb(f"gX{i}", 1024, where=inner) for i in range(2)]
                E1, G = X
                S = sb("gS", 1024, where=inner)
                OFF = sb("gOFF", 512, where=inner)
                vt = sb("gv", 2048, where=inner)
                sr = sb("gr", 2048, where=inner)
                levm = sb("glev", 8 * P, where=inner)
                lr = sb("glr", 32, where=inner)
                lrT = sb("glrT", 256, where=inner, parts=16)
                wg = sb("gwg", 512, where=inner, parts=16)
                qt, kt = hid[0], hid[1]
                t_free = [(pe.sem, pe.n), (act.sem, act.n), (dve.sem, dve.n)]
                s_wg = sem("s_wg")
                sp.dma(wg[:, :], T["gla_w_gate"][0], s_wg, 0, t_free)
                t_S = dve(lambda e: e.memset(S[:, :], 0.0), t_free)
                got = {}

                def evac(c, tok, ps, t):
                    sc, tsc = rs[tok]
                    o = slice(tok * 512, (tok + 1) * 512)
                    if c == 0:
                        a = act(lambda e: e.activation(lr[:, tok * 16:tok * 16 + 16], ps[:, 0:16], ACT.Copy,
                                                       scale=sc), t, tsc, t_free)
                    elif c in (1, 2):
                        d = (qt, kt)[c - 1]
                        a = act(lambda e: e.activation(d[:, o], ps[:, :], ACT.Copy, scale=sc), t, tsc, t_free)
                    elif c in (3, 4):
                        d = vt[:, tok * D + (c - 3) * 512:tok * D + (c - 2) * 512]
                        a = act(lambda e: e.activation(d, ps[:, :], ACT.Copy, scale=sc), t, tsc, t_free)
                    else:
                        d = sr[:, tok * D + (c - 5) * 512:tok * D + (c - 4) * 512]
                        a = act(lambda e: e.activation(d, ps[:, :], ACT.Silu, scale=sc), t, tsc, t_free)
                    got[c, tok] = a
                    return [a]

                v3 = lambda z: z[:, :].rearrange("p (b n) -> p b n", b=4)
                linear(xh, xl, ready, 8, 1, evac)
                k0, ps, w0 = tb.get()

                def f(e, ps=ps):
                    for tok in range(2):
                        last = e.transpose(ps[0:16, tok * P:(tok + 1) * P], lr[:, tok * 16:tok * 16 + 16], ident)
                    return last
                t = pe(f, got[0, 0], got[0, 1], w0)
                t_lr = dve(lambda e, ps=ps: e.tensor_copy(lrT[:, :], ps[0:16, 0:256]), t, t_free)
                tb.put(k0, t_lr)
                tB = []
                for hp in range(2):
                    k0, ps, w0 = tb.get()

                    def f(e, hp=hp, ps=ps):
                        e.matmul(ps[:, 0:256], wg[:, hp * 256:hp * 256 + P], lrT[:, :], start=True, stop=True)
                        return e.matmul(ps[:, 256:512], wg[:, hp * 256 + P:hp * 256 + 256], lrT[:, :], start=False,
                                        stop=True, skip_group_check=True)
                    t = pe(f, t_lr, (s_wg, 16), w0)
                    ta = []
                    for j in range(2):
                        hd = 2 * hp + j
                        bg_ = vcol[:, VR["bg"] + hd:VR["bg"] + hd + 1]
                        x = slice(hd * 256, (hd + 1) * 256)
                        ta.append(act(lambda e, ps=ps, x=x, j=j, b=bg_: e.activation(
                            E1[:, x], ps[:, j * 256:(j + 1) * 256], ACT.Identity, bias=b), t, t_free))
                    tb.put(k0, *ta)
                    x2 = slice(hp * 512, (hp + 1) * 512)
                    t1 = dve(lambda e, x=x2: e.tensor_scalar(G[:, x], E1[:, x], 0.0, None, ALU.min), ta, t_free)
                    t2 = act(lambda e, x=x2: e.activation(E1[:, x], E1[:, x], ACT.Abs), t1)
                    t2 = act(lambda e, x=x2: e.activation(E1[:, x], E1[:, x], ACT.Exp, scale=-1.0), t2)
                    t2 = act(lambda e, x=x2: e.activation(E1[:, x], E1[:, x], ACT.Ln, bias=1.0), t2)
                    t3 = dve(lambda e, x=x2: e.tensor_tensor(G[:, x], G[:, x], E1[:, x], ALU.subtract), t2)
                    for j in range(4):
                        y = slice(hp * 512 + j * P, hp * 512 + (j + 1) * P)
                        tB.append(dve(lambda e, y=y: e.tensor_tensor_scan(B[:, y], ones[:, :], G[:, y], 0.0,
                                                                          ALU.mult, ALU.add), t3, t_ones, t_free))
                linear(xh, xl, ready, 8, 1, lambda c, *a: evac(c + 1, *a))
                tQ = to_T(lambda tok: qt[:, tok * 512:(tok + 1) * 512], [got[1, 0], got[1, 1]], v3(QT), 4,
                          P ** -0.5, dve, after=t_free)
                linear(xh, xl, ready, 8, 1, lambda c, *a: evac(c + 2, *a))
                tK = to_T(lambda tok: kt[:, tok * 512:(tok + 1) * 512], [got[2, 0], got[2, 1]], v3(KT), 4,
                          1.0, dve, after=t_free)

                sT = {"S": t_S}
                xf = [None, None]
                s_lev = sem("s_lev")
                o_lev = const_at["lev"][0]
                sp.dma(levm[:, :], T["const"][:, o_lev:o_lev + 8 * P], s_lev, 0, t_free)

                def level(n):
                    steps = []
                    Xb, XT = X[n % 2], {}

                    if n == 0:
                        def a0():
                            XT["t"] = [tQ, tK]
                        steps.append(a0)
                    else:
                        m = 2 ** (n - 1)
                        view = lambda z: z[:, :].rearrange("p (x a m) -> p x a m", a=2, m=m)
                        nx = 512 // m
                        ref = view(B)[:, :, 0, m - 1:m].to_broadcast([P, nx, m])

                        def a1():
                            t = dve(lambda e: e.tensor_tensor(view(Xb)[:, :, 0, :], ref, view(B)[:, :, 0, :],
                                                              ALU.subtract), tB, xf[n % 2])
                            if m < P:
                                t2 = dve(lambda e: e.tensor_tensor(view(Xb)[:, :, 1, :], view(B)[:, :, 1, :], ref,
                                                                   ALU.subtract), tB, xf[n % 2])
                            else:
                                t2 = dve(lambda e: e.tensor_copy(view(Xb)[:, :, 1, :], view(B)[:, :, 1, :]), tB,
                                         xf[n % 2])
                            XT["e"] = act(lambda e: e.activation(Xb[:, :], Xb[:, :], ACT.Exp, scale=1.0 / 16), t, t2)

                        def a2():
                            t = dve(lambda e: e.tensor_tensor(view(Xb)[:, :, 0, :], view(Xb)[:, :, 0, :],
                                                              view(KT)[:, :, 0, :], ALU.mult), XT["e"], tK)
                            t2 = dve(lambda e: e.tensor_tensor(view(Xb)[:, :, 1, :], view(Xb)[:, :, 1, :],
                                                               view(QT)[:, :, 1, :], ALU.mult), XT["e"], tQ)
                            XT["t"] = [t, t2]
                        steps += [a1, a2]

                    def half(j):
                        def f():
                            k0, ps, w0 = tb.get()
                            if n < 8:
                                def g(e):
                                    for i in range(4):
                                        y = slice(j * 512 + i * P, j * 512 + (i + 1) * P)
                                        l, r = (KT, QT) if n == 0 else (Xb, Xb)
                                        last = e.matmul(ps[:, i * P:(i + 1) * P], l[:, y], r[:, y], start=i == 0,
                                                        stop=True, skip_group_check=True)
                                    return last
                                t = pe(g, XT["t"], w0)
                                s4 = S[:, j * 512:(j + 1) * 512].rearrange("p (i n) -> p i n", i=4)
                                mk = levm[:, n * P:(n + 1) * P].bitcast(U32).rearrange(
                                    "p (i n) -> p i n", i=1).to_broadcast([P, 4, P])
                                sT[j] = dve(lambda e: e.copy_predicated(
                                    s4, mk, ps[:, :].rearrange("p (i n) -> p i n", i=4)), t, sT.get(j, sT["S"]), (s_lev, 16))
                                tb.put(k0, sT[j])
                            else:
                                def g(e):
                                    for i in range(4):
                                        last = e.matmul(ps[:, i * P:(i + 1) * P], Xb[:, i * 256:i * 256 + P],
                                                        Xb[:, i * 256 + P:(i + 1) * 256], start=i == 0,
                                                        stop=True, skip_group_check=True)
                                    return last
                                t = pe(g, XT["t"], w0)
                                sT["off"] = dve(lambda e: e.tensor_copy(OFF[:, :], ps[:, :]), t, t_free)
                                tb.put(k0, sT["off"])
                            xf[n % 2] = t
                        return f
                    steps.append(half(0))
                    if n < 8:
                        steps.append(half(1))
                    return steps

                for n in range(9):
                    bg.extend(level(n))
                PUMP[0] = 4
                linear(xh, xl, ready, 8, 4, lambda c, *a: evac(c + 3, *a))
                pump(1000)
                PUMP[0] = 0
                xfree[0] = (pe.sem, pe.n)
                orow, torow = grow[1], grow[2]
                tO = []
                for tok in range(2):
                    ss = col(4)
                    bk, ts, tm = [], [], []
                    for hd in range(4):
                        k0, ps, w0 = acc.get()

                        def f(e, hd=hd, tok=tok, ps=ps):
                            vv = lambda b: vt[:, b * D + hd * 256:b * D + (hd + 1) * 256]
                            last = e.matmul(ps[:, 0:256], S[:, hd * 256 + tok * P:hd * 256 + (tok + 1) * P],
                                            vv(tok), start=True, stop=tok == 0)
                            if tok:
                                last = e.matmul(ps[:, 0:256], OFF[:, hd * P:(hd + 1) * P], vv(0), start=False,
                                                stop=True)
                            return last
                        t = pe(f, sT[0], sT[1], sT["off"], got[3, tok], got[4, tok], got[3, 0], got[4, 0], w0)
                        bk.append((k0, ps))
                        tm.append(t)
                        ts.append(sumsq(ps[:, 0:256], ss[:, hd:hd + 1], t))
                    r4, tr = rstd_n(ss, 4, 256, ts)
                    for hd in range(4):
                        k0, ps = bk[hd]
                        o = slice(tok * D + hd * 256, tok * D + (hd + 1) * 256)
                        a = dve(lambda e, ps=ps, hd=hd, r4=r4: e.scalar_tensor_tensor(
                            ps[:, 0:256], ps[:, 0:256], r4[:, hd:hd + 1], orow[:, 0:256], ALU.mult, ALU.mult), tr,
                            torow, ts)
                        b = dve(lambda e, ps=ps, o=o: e.tensor_tensor(sr[:, o], ps[:, 0:256], sr[:, o], ALU.mult),
                                a, got[5, tok], got[6, tok])
                        acc.put(k0, b)
                        tO.append(b)
                row_free[grow[0]] = tO[-1]
                xr = to_x2(lambda tok: sr[:, tok * D:(tok + 1) * D], tO)
                res = down(xh, xl, xr, 8)
                xfree[0] = (pe.sem, pe.n)
            return residual(res, 1.0, gain)

        ada_view = T["w_ada_2"].rearrange("(p k) n -> p k n", k=8)
        ada = {"tile": 0, "t": [], "acc_free": None, "pe": 0}

        def ada_load():
            j = ada["tile"]
            if j >= 96 or "due" in ada:
                return
            ada["tile"] += 1
            c, k = divmod(j, 8)
            s = j % 2
            buf = adat[s]
            sp.dma(buf[:, :], ada_view[:, k, c * 512:(c + 1) * 512], s_ada[s], 0, ada["t"][j - 2] if j >= 2 else None)
            arrived = (s_ada[s], 16 * (j // 2 + 1))
            sc = scol[:, 8 + k:9 + k]
            if k == 0:
                t = pool(lambda e: e.tensor_scalar(adaacc[:, :], buf[:, :], sc, None, ALU.mult), arrived, t_scol,
                         ada["acc_free"], ada["t"][j - 1] if j else None)
            else:
                t = pool(lambda e: e.tensor_scalar(buf[:, :], buf[:, :], sc, None, ALU.mult), arrived, t_scol)
                t = pool(lambda e: e.tensor_tensor(adaacc[:, :], adaacc[:, :], buf[:, :], ALU.add), t,
                         ada["t"][j - 1])
            ada["t"].append(t)
            if k == 7:
                ada["due"] = (c, t, unit["load"])

        def ada_reduce():
            if "due" not in ada:
                return
            c, t, _ = ada.pop("due")
            k0, ps, w0 = tb.get()

            def f(e):
                for j in range(4):
                    last = e.matmul(ps[:, j:j + 1], adaacc[:, j * P:(j + 1) * P], ones[:, 0:1], start=j == 0,
                                    stop=True, skip_group_check=True)
                return last
            t1 = pe(f, t, t_ones, w0)
            b = vcol[:, VR["ba"] + 4 * c:VR["ba"] + 4 * c + 4]
            t2 = dve(lambda e: e.tensor_tensor(modc[:, 4 * c:4 * c + 4], ps[:, 0:4], b, ALU.add), t1, t_vec)
            tb.put(k0, t2)
            ada["acc_free"] = t1
            ada["mod"] = t2

        def snap():
            return [(q.sem, q.n) for q in (pe, act, dve, pool)]

        def to_x3(hready, wcol, shift, scale):
            gw = col(8)
            tg = dve(lambda e: e.scalar_tensor_tensor(gw, modc[:, scale * 8:scale * 8 + 8], 1.0,
                                                      vcol[:, wcol:wcol + 8], ALU.add, ALU.mult), ada["mod"], t_vec)
            txn = []
            for tok in range(2):
                r, tr = h_stats(tok, hready[tok])
                txn.append(dve(lambda e, tok=tok, r=r: e.tensor_scalar(
                    hid[tok][:, :], h[:, tok * D:(tok + 1) * D], r, None, ALU.mult), tr, hready[tok],
                    (pe.sem, pe.n), (act.sem, act.n)))
            ready = []
            tmpfree = [junk_t[0], junk_t[1]]
            for kb in range(0, 8, 2):
                k0, ps, w0 = tb.get()
                tiles = [hid[tok][:, (kb + j) * P:(kb + j + 1) * P] for j in range(2) for tok in range(2)]
                t = transposes(tiles, txn, ps, [0, P, 2 * P, 3 * P], w0)
                t1 = []
                i = (kb // 2) % 2
                for j in range(2):
                    g = gw[:, kb + j:kb + j + 1]
                    s_ = modc[:, shift * 8 + kb + j:shift * 8 + kb + j + 1]
                    t1.append(dve(lambda e, i=i, j=j, ps=ps, g=g, s_=s_: e.tensor_scalar(
                        xtmp[i][:, j * 256:(j + 1) * 256], ps[:, j * 256:(j + 1) * 256], g, s_, ALU.mult, ALU.add),
                        t, tg, tmpfree[i]))
                tb.put(k0, *t1)
                r = split_to_x(xtmp[i][:, :], slice(kb * 256, (kb + 2) * 256), t1)
                tmpfree[i] = r
                ready += [r, r]
            return ready

        def gate_row(which):
            s = row_n[0] % 2
            row_n[0] += 1
            dst = rows[s]
            t_free = snap()
            tr = []
            for n in range(2):
                dg = hid[n]
                td = []
                for j in range(4):
                    cc = modc[:, which * 8 + 4 * n + j:which * 8 + 4 * n + j + 1]
                    td.append(dve(lambda e, j=j, cc=cc, dg=dg: e.tensor_scalar(
                        dg[:, j * P:(j + 1) * P], ident, cc, None, ALU.mult), ada["mod"], t_free))
                k0, ps, w0 = tb.get()
                t = pe(lambda e, ps=ps, dg=dg: e.matmul(ps[:, :], ones[:, :], dg[:, 0:512], start=True, stop=True),
                       td, w0)
                t = act(lambda e, ps=ps, n=n: e.activation(dst[:, n * 512:(n + 1) * 512], ps[:, :], ACT.Copy), t,
                        row_free[s], t_free)
                tb.put(k0, t)
                tr.append(t)
            return s, dst, tr

        def residual_gate(res, gain):
            s, row, trow = gain
            ready = []
            for tok in range(2):
                for n in range(2):
                    ps, k0, t = res[tok][n]
                    hs = h[:, tok * D + n * 512:tok * D + (n + 1) * 512]
                    a = dve(lambda e, ps=ps, n=n: e.tensor_tensor(ps[:, :], ps[:, :], row[:, n * 512:(n + 1) * 512],
                                                                  ALU.mult), t, trow)
                    b = dve(lambda e, ps=ps, hs=hs: e.tensor_tensor(hs, ps[:, :], hs, ALU.add), a)
                    acc.put(k0, b)
                ready.append(b)
            row_free[s] = ready[-1]
            return ready

        def second_mixer(hready):
            with ExitStack() as inner:
                ar = sb("ar2", 14224, where=inner)
                AH = sb("AH", 1024, F32R, where=inner)
                AL = sb("AL", 1024, F32R, where=inner)
                tf = snap()
                off = [0]

                def A(n, at=None):
                    if at is None:
                        at = off[0]
                        off[0] += n
                    return ar[:, at:at + n]
                iqT, qaT, kaT, va, ikT = A(1024), A(1024), A(1024), A(1024), A(256)
                sga, sgb = A(2048, 0), A(2048, 2048)
                MB = A(384)
                SCW = off[0]
                SC, W = A(384), A(384)
                PB = [SC, W]
                pT = [A(384), A(384)]
                off[0] = SCW + 1536
                RSb = A(1536, SCW)
                qrT, krT, vr, sgr = A(1024), A(1024), A(2048), A(2048)
                rt = A(512)
                decay = A(1024)
                iw, ik2 = A(16), A(256)
                assert off[0] <= 14224, off[0]
                s_dec = sem("s_dec")
                o_dec = const_at["dec"][0]
                sp.dma(decay, T["const"][:, o_dec:o_dec + 1024], s_dec, 0, tf)
                gnr = row_load(T["gn_w_2"], D)
                ready = to_x3(hready, VR["n1"], 0, 1)
                v4 = lambda z: z.rearrange("p (b n) -> p b n", b=4)
                rtf = [None]
                hf = [[None], [None]]

                def rope(eng, buf, tok, nh, hd, half, cs, sn, ready, extra=None):
                    v = buf.rearrange("p (x d) -> p x d", d=hd)
                    x1, x2 = v[:, :, 0:half], v[:, :, half:2 * half]
                    w = nh * half
                    t1b = rt[:, 0:w].rearrange("p (x d) -> p x d", d=half)
                    t2b = rt[:, 256:256 + w].rearrange("p (x d) -> p x d", d=half)
                    bc = lambda z: z.rearrange("p (x d) -> p x d", x=1).to_broadcast([P, nh, half])
                    c_, s_ = bc(C(cs, tok * half, half)), bc(C(sn, tok * half, half))
                    tt = lambda o, a, b, op, *w_: eng(lambda e: e.tensor_tensor(o, a, b, op), *w_)
                    a = tt(t1b, x1, s_, ALU.mult, ready, rtf[0], t_in)
                    b = tt(t2b, x2, s_, ALU.mult, ready, rtf[0], t_in)
                    c = tt(x1, x1, c_, ALU.mult, a)
                    d = tt(x2, x2, c_, ALU.mult, b)
                    f1 = tt(x1, x1, t2b, ALU.subtract, c, b)
                    f2 = tt(x2, x2, t1b, ALU.add, d, a)
                    rtf[0] = [f1, f2]
                    return [f1, f2]

                def roped(i, dst, nblk_dims, scale, full):
                    tk = [None, None]

                    def evac(c, tok, ps, t):
                        o = hid[i][:, tok * 512:(tok + 1) * 512]
                        a = act(lambda e: e.activation(o, ps[:, :], ACT.Copy), t, hf[i], tf)
                        if full:
                            tk[tok] = rope(pool, o, tok, 4, 128, 64, "cosr", "sinr", a)
                        else:
                            tk[tok] = rope(pool, o, tok, 8, 64, 8, "cosa", "sina", a)
                        return [a]

                    def finish():
                        r = to_T(lambda tok: hid[i][:, tok * 512:(tok + 1) * 512], tk, dst, 4, scale, act, after=tf)
                        hf[i] = (pe.sem, pe.n)
                        return r
                    return evac, finish

                got = {}
                hf = [[ready[-1], ready[-3], (pe.sem, pe.n)]] * 2

                def ev_ik(c, tok, ps, t):
                    i2 = ik2[:, tok * P:(tok + 1) * P].rearrange("p (a d) -> p a d", a=2)
                    a = act(lambda e: e.activation(i2[:, 0, :], ps[:, 0:64], ACT.Copy), t, tf)
                    b = act(lambda e: e.activation(iw[:, tok * 8:tok * 8 + 8], ps[:, 64:72], ACT.Copy,
                                                   scale=8.0 ** -0.5), t, tf)
                    tr = rope(pool, i2[:, 0, :], tok, 1, 64, 8, "cosa", "sina", a)
                    got["ik", tok] = pool(lambda e: e.tensor_copy(i2[:, 1, :], i2[:, 0, :]), tr)
                    got["iw", tok] = b
                    return [a, b]

                linear(xh, xl, ready, 8, 1, ev_ik)
                e1, f1 = roped(0, v4(iqT), 4, 1.0, False)
                linear(xh, xl, ready, 8, 1, e1)
                k0, ps, w0 = tb.get()
                t = transposes([ik2[:, 0:P], ik2[:, P:256]], [got["ik", 0], got["ik", 1]], ps, [0, P], w0)
                tik = act(lambda e, ps=ps: e.activation(ikT, ps[:, 0:256], ACT.Copy), t, tf)
                tb.put(k0, tik)
                e2, f2 = roped(1, v4(qaT), 4, 0.125, False)
                linear(xh, xl, ready, 8, 1, e2)
                tiq = f1()
                e3, f3 = roped(0, v4(kaT), 4, 1.0, False)
                linear(xh, xl, ready, 8, 1, e3)
                tqa = f2()

                def ev_va(c, tok, ps, t):
                    a = act(lambda e: e.activation(va[:, tok * 512:(tok + 1) * 512], ps[:, :], ACT.Copy), t, tf)
                    got["va", tok] = a
                    return [a]

                ch = {"t": [None, None]}
                cut = [slice(0, P), slice(P, 384)]

                def idx_head(hd):
                    def f():
                        p0, b = 64 * (hd % 2), hd // 2
                        k0, ps, w0 = tb.get()

                        def g(e):
                            q, k = iqT[p0:p0 + 64, b * 256:(b + 1) * 256], ikT[p0:p0 + 64, :]
                            e.matmul(ps[:, 0:P], q[:, 0:P], k[:, 0:P], start=True, stop=True)
                            return e.matmul(ps[:, P:384], q[:, P:256], k, start=False, stop=True,
                                            skip_group_check=True)
                        t = pe(g, tiq[b], tik, w0)
                        R = pT[hd % 2]
                        t = act(lambda e: e.activation(R, ps[:, 0:384], ACT.Relu, scale=0.125), t,
                                ch.get(("r", hd % 2)), tf)
                        tb.put(k0, t)
                        for j in range(2):
                            wv = iw[:, j * 8 + hd:j * 8 + hd + 1]
                            if hd == 0:
                                ch["t"][j] = dve(lambda e, j=j, wv=wv: e.tensor_scalar(
                                    SC[:, cut[j]], R[:, cut[j]], wv, None, ALU.mult), t, got["iw", j], tf)
                            else:
                                ch["t"][j] = dve(lambda e, j=j, wv=wv: e.scalar_tensor_tensor(
                                    SC[:, cut[j]], R[:, cut[j]], wv, SC[:, cut[j]], ALU.mult, ALU.add), t,
                                    ch["t"][j], got["iw", j])
                        ch["r", hd % 2] = list(ch["t"])
                    return f

                def causal():
                    for j, s_ in enumerate((slice(0, P), slice(256, 384))):
                        ch["t"][j] = dve(lambda e, s_=s_: e.tensor_tensor(SC[:, s_], SC[:, s_], C("caus"), ALU.add),
                                         ch["t"][j])

                def top8(n):
                    def f():
                        for j in range(2):
                            src = SC if n == 0 else W
                            m8 = got.setdefault(("m8", j, n % 2), col(8))
                            t = dve(lambda e, j=j, src=src, m8=m8: e.max(m8, src[:, cut[j]]), ch["t"][j], tf)
                            ch["t"][j] = dve(lambda e, j=j, src=src, m8=m8: e.match_replace(
                                W[:, cut[j]], m8, src[:, cut[j]], -BIG), t)
                    return f

                def choose():
                    t = dve(lambda e: e.tensor_scalar(MB, W, -2e38, None, ALU.is_le), ch["t"], tf)
                    t = dve(lambda e: e.tensor_scalar(MB, MB, -1.0, 1e30, ALU.add, ALU.mult), t)
                    for s_ in (slice(0, P), slice(256, 384)):
                        t = dve(lambda e, s_=s_: e.tensor_tensor(MB[:, s_], MB[:, s_], C("caus"), ALU.min), t)
                    ch["m"] = t
                    ch["p"] = [[t], [t]]

                LG = {}

                def logits(hd):
                    p0, b, s = 64 * (hd % 2), hd // 2, hd % 2
                    k0, ps, w0 = tb.get()

                    def g(e):
                        q, k = qaT[p0:p0 + 64, b * 256:(b + 1) * 256], kaT[p0:p0 + 64, b * 256:(b + 1) * 256]
                        e.matmul(ps[:, 0:P], q[:, 0:P], k[:, 0:P], start=True, stop=True)
                        return e.matmul(ps[:, P:384], q[:, P:256], k, start=False, stop=True,
                                        skip_group_check=True)
                    t = pe(g, tqa[b], got["tka"][b], w0)
                    mx, nm, sm, ri = col(2), col(2), col(2), col(2)
                    ts = []
                    for j in range(2):
                        ts.append(dve(lambda e, j=j: e.tensor_tensor_reduce(
                            out=PB[s][:, cut[j]], in0=ps[:, cut[j]], in1=MB[:, cut[j]], scale=1.0, scalar=-BIG,
                            op0=ALU.add, op1=ALU.max, accum_out=mx[:, j:j + 1]), t, ch["m"], ch["p"][s]))
                    tb.put(k0, *ts)
                    t = dve(lambda e: e.tensor_scalar(nm, mx, -1.0, None, ALU.mult), ts)
                    te = [act(lambda e, j=j: e.activation(PB[s][:, cut[j]], PB[s][:, cut[j]], ACT.Exp,
                                                          bias=nm[:, j:j + 1], accum_out=sm[:, j:j + 1]), t, ts)
                          for j in range(2)]
                    t = dve(lambda e: e.reciprocal(ri, sm), te)
                    LG[hd] = [dve(lambda e, j=j: e.tensor_scalar(PB[s][:, cut[j]], PB[s][:, cut[j]], ri[:, j:j + 1],
                                                                 None, ALU.mult), t, te) for j in range(2)]

                def probs(hd):
                    s = hd % 2
                    k0, ps, w0 = tb.get()
                    t = transposes([PB[s][:, 0:P], PB[s][:, P:256], PB[s][:, 256:384]], LG[hd], ps, [0, P, 256], w0)
                    ch["p"][s] = t
                    t = act(lambda e: e.activation(pT[s], ps[:, 0:384], ACT.Copy), t, ch.get(("v", s)), ch["m"])
                    tb.put(k0, t)
                    LG[hd] = t

                def att_values(hd):
                    s, p0, b = hd % 2, 64 * (hd % 2), hd // 2
                    if hd % 2 == 0:
                        ch["pv"] = acc6.get()
                    k0, ps, w0 = ch["pv"]

                    def g(e):
                        e.matmul(ps[p0:p0 + 64, 0:256], va[:, hd * 64:(hd + 1) * 64], pT[s][:, 0:256],
                                 start=True, stop=True)
                        return e.matmul(ps[p0:p0 + 64, P:256], va[:, 512 + hd * 64:512 + (hd + 1) * 64],
                                        pT[s][:, 256:384], start=False, stop=True, skip_group_check=True)
                    t = pe(g, LG[hd], got["va", 0], got["va", 1], w0)
                    ch["v", s] = t
                    if hd % 2 == 1:
                        sl = slice(b * 256, (b + 1) * 256)
                        a = act(lambda e: e.activation(AH[:, sl], ps[:, 0:256], ACT.Copy), t, tf)
                        c = dve(lambda e: e.tensor_tensor(AL[:, sl], ps[:, 0:256], AH[:, sl].bitcast(F32),
                                                          ALU.subtract), a, tf)
                        acc6.put(k0, c)
                        got["att", b] = [a, c]

                acc6 = acc
                for hd in range(8):
                    bg.append(idx_head(hd))
                bg.append(causal)
                for n in range(8):
                    bg.append(top8(n))
                bg.append(choose)
                PUMP[0] = 2
                linear(xh, xl, ready, 8, 1, ev_va)
                got["tka"] = f3()
                for s in range(10):
                    def stp(s=s):
                        if s - 2 >= 0 and s - 2 < 8:
                            att_values(s - 2)
                        if 0 <= s - 1 < 8:
                            probs(s - 1)
                        if s < 8:
                            logits(s)
                    bg.append(stp)
                e4, f4 = roped(1, v4(qrT), 4, 1.0, True)
                linear(xh, xl, ready, 8, 1, e4)
                e5, f5 = roped(0, v4(krT), 4, 1.0, True)
                linear(xh, xl, ready, 8, 1, e5)
                tqr = f4()

                def ev_vr(c, tok, ps, t):
                    o = slice(tok * D + c * 512, tok * D + (c + 1) * 512)
                    a = act(lambda e: e.activation(vr[:, o], ps[:, :], ACT.Copy), t, tf)
                    got["vr", c, tok] = a
                    return [a]

                linear(xh, xl, ready, 8, 2, ev_vr)
                tkr = f5()

                def ev_gr(c, tok, ps, t):
                    o = slice(tok * D + c * 512, tok * D + (c + 1) * 512)
                    a = act(lambda e: e.activation(sgr[:, o], ps[:, :], ACT.Silu), t, tf)
                    b = pool(lambda e: e.tensor_tensor(sgr[:, o], sgr[:, o], gnr[1][:, c * 512:(c + 1) * 512],
                                                       ALU.mult), a, gnr[2])
                    got["gr", c, tok] = b
                    row_free[gnr[0]] = b
                    return [a]

                linear(xh, xl, ready, 8, 2, ev_gr)
                pump(1000)
                t_dsa = snap()

                for hd in range(4):
                    def f(hd=hd):
                        k0, ps, w0 = tb.get()

                        def g(e):
                            q, k = qrT[:, hd * 256:(hd + 1) * 256], krT[:, hd * 256:(hd + 1) * 256]
                            e.matmul(ps[:, 0:256], k[:, 0:P], q, start=True, stop=True)
                            return e.matmul(ps[:, 256:384], k[:, P:256], q[:, P:256], start=False, stop=True,
                                            skip_group_check=True)
                        t = pe(g, tqr[hd], tkr[hd], w0)
                        o = hd * 384
                        a = dve(lambda e: e.tensor_tensor(RSb[:, o:o + 256], ps[:, 0:256],
                                                          decay[:, hd * 256:(hd + 1) * 256], ALU.mult), t, t_dsa,
                                (s_dec, 16))
                        b = dve(lambda e: e.tensor_tensor(RSb[:, o + 256:o + 384], ps[:, 256:384],
                                                          decay[:, hd * 256:hd * 256 + P], ALU.mult), t, t_dsa,
                                (s_dec, 16))
                        tb.put(k0, b)
                        got["rs", hd] = [a, b]
                    bg.append(f)
                for tok in range(2):
                    for hd in range(4):
                        def f(tok=tok, hd=hd):
                            k0, ps, w0 = tb.get()
                            vv = lambda b: vr[:, b * D + hd * 256:b * D + (hd + 1) * 256]

                            def g(e):
                                o = hd * 384
                                if tok == 0:
                                    return e.matmul(ps[:, 0:256], RSb[:, o:o + P], vv(0), start=True, stop=True)
                                e.matmul(ps[:, 0:256], RSb[:, o + P:o + 256], vv(0), start=True, stop=False)
                                return e.matmul(ps[:, 0:256], RSb[:, o + 256:o + 384], vv(1), start=False, stop=True)
                            c = hd // 2
                            t = pe(g, got["rs", hd], got["vr", c, 0], got["vr", c, 1], w0)
                            s6, mv, w1, r1, r2 = col(6), col(2), col(), col(), col()
                            t = dve(lambda e: e.bn_stats(s6, ps[:, 0:256]), t)
                            t = dve(lambda e: e.bn_aggr(mv, s6), t)
                            t3 = dve(lambda e: e.tensor_scalar(w1, mv[:, 1:2], EPS, None, ALU.add), t)
                            t3 = act(lambda e: e.activation(r1, w1, ACT.Sqrt), t3)
                            t3 = dve(lambda e: e.reciprocal(r2, r1), t3)
                            t3 = dve(lambda e: e.tensor_scalar(ps[:, 0:256], ps[:, 0:256], mv[:, 0:1], r2,
                                                               ALU.subtract, ALU.mult), t3)
                            o = slice(tok * D + hd * 256, tok * D + (hd + 1) * 256)
                            t3 = dve(lambda e: e.tensor_tensor(sgr[:, o], ps[:, 0:256], sgr[:, o], ALU.mult), t3,
                                     got["gr", c, tok])
                            tb.put(k0, t3)
                            got["yr", tok, hd] = t3
                        bg.append(f)

                def ev_g(dst, key):
                    def ev(c, tok, ps, t):
                        o = slice(tok * D + c * 512, tok * D + (c + 1) * 512)
                        a = act(lambda e: e.activation(dst[:, o], ps[:, :], ACT.Sigmoid), t, t_dsa)
                        got[key, c, tok] = a
                        return [a]
                    return ev
                linear(xh, xl, ready, 8, 2, ev_g(sga, "ga"))
                linear(xh, xl, ready, 8, 2, ev_g(sgb, "gb"))
                xfree[0] = (pe.sem, pe.n)
                PUMP[0] = 0
                pump(1000)

                def gated(res, dst, key):
                    ts = []
                    for tok in range(2):
                        for n in range(2):
                            ps, k0, t = res[tok][n]
                            o = slice(tok * D + n * 512, tok * D + (n + 1) * 512)
                            b = dve(lambda e, ps=ps, o=o: e.tensor_tensor(dst[:, o], ps[:, :], dst[:, o], ALU.mult),
                                    t, got[key, n, tok])
                            acc.put(k0, b)
                            ts.append(b)
                    return ts
                xr = to_x2(lambda tok: sgr[:, tok * D:(tok + 1) * D], [got["yr", a, b] for a in range(2)
                                                                       for b in range(4)])
                ta = gated(down(AH, AL, [got["att", b] for b in range(4)], 4), sga, "ga")
                tbb = gated(down(xh, xl, xr, 8), sgb, "gb")
                xfree[0] = (pe.sem, pe.n)
                gain = gate_row(2)
                tm = [dve(lambda e, n=n: e.tensor_tensor(sga[:, n * 512:(n + 1) * 512], sga[:, n * 512:(n + 1) * 512],
                                                         sgb[:, n * 512:(n + 1) * 512], ALU.add), ta[n], tbb[n])
                      for n in range(4)]
                xr = to_x2(lambda tok: sga[:, tok * D:(tok + 1) * D], tm)
                res = down(xh, xl, xr, 8)
                xfree[0] = (pe.sem, pe.n)
            return residual_gate(res, gain)

        def second_ffn(hready):
            ready = to_x3(hready, VR["n2"], 3, 4)
            with ExitStack() as inner:
                gh = sb("ghf", 22 * 256, F32R, where=inner)
                gl = sb("glf", 22 * 256, F32R, where=inner)
                gready = ffn_body(gh, gl, ready, None)
                res = down(gh, gl, gready, 22)
                gain = gate_row(5)
            return residual_gate(res, gain)

        def plan_down(w, nk):
            for k in range(0, nk, 4):
                m = min(4, nk - k)
                for n in range(2):
                    plan.append((w[k * P:(k + m) * P, n * 512:(n + 1) * 512]
                                 .rearrange("(k p) n -> p k n", p=P), m, 512))

        if UPTO >= 1:
            plan_ffn([T["ffn1_w_in"][0]], T["ffn1_w_out"][0])
        if UPTO >= 2:
            for c in (4, 3, 0, 1, 2):
                plan_cols(T["hyb_w_in"][0], c * 512, 512, 8)
            plan_down(T["hyb_w_out"][0], 8)
        if UPTO >= 3:
            plan_ffn([T["ffn2_w_in"][0]], T["ffn2_w_out"][0])

        if UPTO >= 4:
            plan_ffn([T["ffn1_w_in"][1]], T["ffn1_w_out"][1])
        if UPTO >= 5:
            plan_cols(T["gla_w_in"][0], 3072, 16, 8)
            for c in range(6):
                plan_cols(T["gla_w_in"][0], c * 512, 512, 8)
            plan_down(T["gla_w_out"][0], 8)
        if UPTO >= 6:
            plan_ffn([T["ffn2_w_in"][1]], T["ffn2_w_out"][1])

        if UPTO >= 7:
            w = T["w_in_2"]
            plan_cols(w, 2048, 72, 8)
            for c in (1536, 0, 512, 1024, 2120, 2632, 3144, 3656, 4168, 4680, 5192, 5704, 6216, 6728):
                plan_cols(w, c, 512, 8)
            plan_down(T["w_attn_proj_2"], 4)
            plan_down(T["w_ret_proj_2"], 8)
            plan_down(T["w_out_2"], 8)
        if UPTO >= 8:
            plan_ffn([T["w_ffn_gate_2"], T["w_ffn_up_2"]], T["w_ffn_down_2"])

        hready = [t_in, t_in]
        if UPTO >= 1:
            hready = ffn_stage(hready, 0, T["norm_g"][0, 1])
        if UPTO >= 2:
            hready = hybrid_stage(hready)
        if UPTO >= 3:
            hready = ffn_stage(hready, 4 * 8, T["norm_g"][0, 5])
        if UPTO >= 4:
            hready = ffn_stage(hready, 6 * 8, T["norm_g"][1, 1])
        if UPTO >= 5:
            hready = gla_stage(hready)
        if UPTO >= 6:
            hready = ffn_stage(hready, 10 * 8, T["norm_g"][1, 5])

        if UPTO >= 7:
            hready = second_mixer(hready)
        if UPTO >= 8:
            hready = second_ffn(hready)
        if UPTO > 8:
            _, row, trow = row_load(T["final_norm_w_2"], D)
            for tok in range(2):
                r, tr = h_stats(tok, hready[tok])
                hs = h[:, tok * D:(tok + 1) * D]
                hready[tok] = dve(lambda e, hs=hs, r=r: e.scalar_tensor_tensor(hs, hs, r, row[:, :], ALU.mult,
                                                                               ALU.mult), tr, trow)

        tout = []
        for tok in range(2):
            sp.dma(out[0, tok * P:(tok + 1) * P, :], h[:, tok * D:(tok + 1) * D], s_out, 0, hready[tok])
        sp.wait((s_out, 32))

        block = ctx.enter_context(nc.Block())
        block.sync(lambda e: sp.run(e))
        block.tensor(lambda e: pe.run(e))
        block.scalar(lambda e: act.run(e))
        block.vector(lambda e: dve.run(e))
        block.gpsimd(lambda e: pool.run(e))


_INS = ["x", "norm_g", "ffn1_w_in", "ffn1_w_out", "ffn2_w_in", "ffn2_w_out", "hyb_w_in", "hyb_w_out", "conv_dw_w",
        "conv_dw_b", "conv_ln_g", "conv_ln_b", "gla_w_in", "gla_w_gate", "gla_b_gate", "gla_norm_g", "gla_w_out",
        "c_2", "w_ada_2", "b_ada_2", "norm1_w_2", "w_in_2", "w_attn_proj_2", "w_ret_proj_2", "gn_w_2", "w_out_2",
        "norm2_w_2", "w_ffn_gate_2", "w_ffn_up_2", "w_ffn_down_2", "final_norm_w_2"]


def kernel(**inputs):
    import numpy as _np
    import concourse.bacc as _bacc
    from concourse import mybir as _mybir
    from concourse.bass_utils import run_bass_kernel_spmd as _run

    nc = _bacc.Bacc("TRN2", target_bir_lowering=False, num_devices=1)
    const_at, const = constants()
    arrays, T = {}, {}
    for name in _INS:
        a = _np.ascontiguousarray(inputs[name])
        arrays[f"in_{name}_dram"] = a
        T[name] = nc.dram_tensor(f"in_{name}_dram", a.shape, _mybir.dt.from_np(a.dtype), kind="ExternalInput").ap()
    arrays["in_const_dram"] = const
    T["const"] = nc.dram_tensor("in_const_dram", const.shape, _mybir.dt.float32, kind="ExternalInput").ap()
    out = nc.dram_tensor("out_0_dram", (1, 256, 1024), _mybir.dt.float32, kind="ExternalOutput").ap()
    program(nc, T, const_at, out)
    r = _run(nc, [arrays], core_ids=[0])
    return r.results[0]["out_0_dram"]
```

```python
from contextlib import ExitStack

import numpy as np

import concourse.bass as bass
from concourse import mybir

P = 128
D = 1024
FF = 2816
F32 = mybir.dt.float32
F32R = mybir.dt.float32r
U32 = mybir.dt.uint32
ALU = mybir.AluOpType
ACT = mybir.ActivationFunctionType
AX = mybir.AxisListType
EPS = 1e-6
BIG = 3e38
NEG = -1e30

NRAW = 3
NSPL = 7
LOOK = 4
HOLD = 3
UPTO = 99


class Lane:

    def __init__(self, sem):
        self.sem, self.n, self.ops, self.seen = sem, 0, [], {}

    def wait(self, *after):
        for t in after:
            if t is None:
                continue
            if isinstance(t, list):
                self.wait(*t)
                continue
            sem, v = t
            if self.seen.get(id(sem), 0) < v:
                self.seen[id(sem)] = v
                self.ops.append(lambda e, sem=sem, v=v: e.wait_ge(sem, v))

    def __call__(self, fn, *after):
        self.wait(*after)
        self.n += 1
        self.ops.append(lambda e: fn(e).then_inc(self.sem, 1))
        return (self.sem, self.n)

    def dma(self, dst, src, sem, count, *after):
        self.wait(*after)
        self.ops.append(lambda e: e.dma_start(dst, src).then_inc(sem, 16))
        return (sem, count)

    def run(self, e):
        for op in self.ops:
            op(e)


class Banks:

    def __init__(self, banks):
        self.banks, self.free, self.i = banks, [[] for _ in banks], 0

    def get(self):
        k = self.i % len(self.banks)
        self.i += 1
        waits, self.free[k] = self.free[k], None
        assert waits is not None
        return k, self.banks[k], waits

    def put(self, k, *tokens):
        self.free[k] = list(tokens)


def constants():
    i = np.arange(P)
    cols = {}
    cols["ident"] = np.eye(P)
    cols["tri"] = i[:, None] >= i[None, :]
    valid = i[:, None] < i[None, :]
    cols["mmin"] = np.concatenate([np.where(valid, BIG, 0.0), np.full((P, P), BIG), np.where(valid, BIG, 0.0)], 1)
    cols["mmax"] = -cols["mmin"]
    cols["caus"] = np.where(i[None, :] <= i[:, None], 0.0, NEG)
    lev = [np.eye(P)]
    for m in (1, 2, 4, 8, 16, 32, 64):
        same = (i[:, None] // (2 * m)) == (i[None, :] // (2 * m))
        lev.append(same & (i[:, None] % (2 * m) < m) & (i[None, :] % (2 * m) >= m))
    cols["lev"] = np.concatenate(lev, 1)
    dec = []
    for h in range(4):
        lg = float(np.log(np.float32(1.0 - 2.0 ** (-5.0 - h))))
        dt = i[None, :] - i[:, None]
        dec.append(np.where(dt >= 0, np.exp(lg * np.maximum(dt, 0)), 0.0) * P ** -0.5)
        dec.append(np.exp(lg * (dt + P)) * P ** -0.5)
    cols["dec"] = np.concatenate(dec, 1)
    for nm, dim, theta in (("a", 16, 500000.0), ("r", 128, 10000.0)):
        f32 = np.float32
        inv = f32(1.0) / (f32(theta) ** (np.arange(0, dim, 2, dtype=f32) / f32(dim)))
        ang = (np.arange(256, dtype=f32)[:, None] * inv[None, :]).astype(np.float64)
        for fn, f in (("cos", np.cos), ("sin", np.sin)):
            cols[fn + nm] = np.concatenate([f(ang[:P]), f(ang[P:])], 1)
    at, parts, n = {}, [], 0
    for k in [k for k in cols if k not in ("lev", "dec")] + ["lev", "dec"]:
        v = cols[k]
        v = np.asarray(v, np.float32)
        at[k] = (n, v.shape[1])
        n += v.shape[1]
        parts.append(v)
    return at, np.ascontiguousarray(np.concatenate(parts, 1))


def program(nc, T, const_at, out):
    ctx = ExitStack()
    with ctx:
        def sb(name, cols, dt=F32, parts=P, where=ctx):
            return where.enter_context(nc.sbuf_tensor(name, [parts, cols], dt))

        def sem(name):
            return ctx.enter_context(nc.semaphore(name))

        psum = [ctx.enter_context(nc.psum_tensor(f"ps{i}", [P, 512], F32)) for i in range(8)]
        acc = Banks(psum[:6])
        tb = Banks(psum[6:])
        pe, act, dve, pool, sp = (Lane(sem(n)) for n in ("s_pe", "s_act", "s_dve", "s_pool", "s_sp"))

        nconst = const_at["lev"][0]
        cst = sb("cst", nconst)
        adat = [sb(f"adat{i}", 512) for i in range(2)]
        adaacc = sb("adaacc", 512)
        modc = sb("modc", 48)
        scol = sb("scol", 16)
        s_ada = [sem(f"s_ada{i}") for i in range(2)]
        vcol = sb("vcol", 3 * P)
        h = sb("h", 2 * D)
        xh = sb("xh", 8 * 256, F32R)
        xl = sb("xl", 8 * 256, F32R)
        raw = [sb(f"raw{i}", 2048) for i in range(NRAW)]
        whi = [sb(f"whi{i}", 1024, F32R) for i in range(NSPL)]
        wlo = [sb(f"wlo{i}", 1024, F32R) for i in range(NSPL)]
        rows = [sb(f"row{i}", D) for i in range(2)]
        st = sb("st", 512)
        junk = sb("junk", 1024)
        xtmp = sb("xtmp", 1024)
        mhalf = sb("mhalf", 8)
        vin = sb("vin", P)
        vin2 = sb("vin2", 2 * P)
        hid = [sb(f"hid{i}", 1024) for i in range(2)]
        s_raw = [sem(f"s_raw{i}") for i in range(NRAW)]
        s_row = [sem(f"s_row{i}") for i in range(2)]
        s_in = sem("s_in")
        s_in2 = sem("s_in2")
        s_out = sem("s_out")

        def C(name, a=0, n=None):
            o, w = const_at[name]
            n = w - a if n is None else n
            return cst[:, o + a:o + a + n]

        ident = C("ident")

        for b in range(2):
            sp.dma(h[:, b * D:(b + 1) * D], T["x"][0, b * P:(b + 1) * P, :], s_in, 0)
        sp.dma(cst[:, 0:P], T["const"][:, 0:P], s_in, 0)
        sp.dma(vin[0:96, 0:P], T["norm_g"].rearrange("l n (b p) -> (l n b) p", p=P), s_in, 0)
        t_in = (s_in, 64)
        n_in = 0
        more = []
        VR = {}
        r = 0
        for nm, src in (("n1", T["norm1_w_2"]), ("n2", T["norm2_w_2"]), ("ba", T["b_ada_2"]),
                        ("bg", T["gla_b_gate"][0]), ("cb", T["conv_dw_b"][0]),
                        ("lg", T["conv_ln_g"][0]), ("lb", T["conv_ln_b"][0])):
            k = src.shape[0] // P
            more.append((vin2[r:r + k, 0:P], src.rearrange("(b p) -> b p", p=P)))
            VR[nm] = P + r
            r += k
        more.append((vin2[0:124, P:2 * P], T["conv_dw_w"][0].rearrange("k (b p) -> (k b) p", p=P)))
        VR["cw"] = 2 * P
        more.append((cst[:, P:nconst], T["const"][:, P:nconst]))
        more.append((scol[:, 0:8], T["c_2"].rearrange("a (p k) -> (a p) k", k=8)))
        t_in2 = (s_in2, 16 * len(more))
        nvec = {0: 96, 1: r, 2: 124}

        def vectors(js, after):
            k0, bank, w0 = tb.get()

            def f(e):
                for j in js:
                    src = vin[:, 0:P] if j == 0 else vin2[:, (j - 1) * P:j * P]
                    last = e.transpose(bank[:, j * P:j * P + nvec[j]], src[0:nvec[j], :], ident[0:nvec[j], 0:nvec[j]])
                return last
            t = pe(f, after, w0)

            def f2(e):
                for j in js:
                    last = e.tensor_copy(vcol[:, j * P:j * P + nvec[j]], bank[:, j * P:j * P + nvec[j]])
                return last
            t = dve(f2, t)
            tb.put(k0, t)
            return t

        t_vec = vectors([0], t_in)
        t_vec2 = []

        def second_vectors():
            t_vec2.append(vectors([1, 2], [t_in2, t_in]))
            t_vec2.append(act(lambda e: e.activation(scol[:, 8:16], scol[:, 0:8], ACT.Silu), t_in2))

        plan = []

        def plan_cols(w, c0, n, nk):
            for k in range(0, nk, 4):
                m = min(4, nk - k)
                plan.append((w[k * P:(k + m) * P, c0:c0 + n].rearrange("(k p) n -> p k n", p=P), m, n))

        def plan_ffn(w_in, w_out):
            for c in range(11):
                for k in (0, 4):
                    if len(w_in) == 1:
                        v = w_in[0][k * P:(k + 4) * P, :].rearrange("(k p) (a n) -> p k a n", p=P, a=2)
                        plan.append((v[:, :, :, c * 256:(c + 1) * 256], 4, 512))
                    else:
                        plan.append(([w[k * P:(k + 4) * P, c * 256:(c + 1) * 256]
                                      .rearrange("(k p) n -> p k n", p=P) for w in w_in], 4, 512))
            for k in range(0, 22, 4):
                m = min(4, 22 - k)
                for n in range(2):
                    plan.append((w_out[k * P:(k + m) * P, n * 512:(n + 1) * 512]
                                 .rearrange("(k p) n -> p k n", p=P), m, 512))

        bg = []

        def pump(n):
            while bg and n > 0:
                bg.pop(0)()
                n -= 1

        unit = {"load": 0, "split": 0, "use": 0}
        t_load, t_used, t_sub, subs = [], {}, [], []
        nraw_sem = [0] * NRAW
        sub_at = {}

        def cut_subs():
            for u, (_, m, n) in enumerate(plan):
                sub_at[u] = len(subs)
                for k in range(0, m, 2):
                    subs.append((u, k, min(2, m - k), n))

        def load_unit():
            i = unit["load"]
            unit["load"] += 1
            s = i % NRAW
            src, m, n = plan[i]
            after = t_sub[sub_at[i - NRAW + 1] - 1] if i >= NRAW else None
            dst = raw[s][:, 0:m * n]
            if isinstance(src, list):
                dst = dst.rearrange("p (k a n) -> p k a n", k=m, a=2)
                for a in range(2):
                    nraw_sem[s] += 16
                    sp.dma(dst[:, :, a, :], src[a], s_raw[s], 0, after)
            elif len(src.shape) == 4:
                dst4 = dst.rearrange("p (k a n) -> p k a n", k=m, a=2)
                for a in range(2):
                    nraw_sem[s] += 16
                    sp.dma(dst4[:, :, a, :], src[:, :, a, :], s_raw[s], 0, after)
            else:
                nraw_sem[s] += 16
                sp.dma(dst.rearrange("p (k n) -> p k n", k=m), src, s_raw[s], 0, after)
            t_load.append((s_raw[s], nraw_sem[s]))
            if i == 1:
                for d, v in more:
                    sp.dma(d, v, s_in2, 0)
            if i >= 8 and UPTO >= 7:
                ada_load()

        def split_sub():
            j = unit["split"]
            unit["split"] += 1
            u, k, m, n = subs[j]
            if unit["load"] <= u:
                load_unit()
            r = raw[u % NRAW][:, k * n:(k + m) * n]
            a, b = whi[j % NSPL], wlo[j % NSPL]
            used = t_used[j - NSPL] if j >= NSPL else None
            ta = act(lambda e: e.activation(a[:, 0:m * n], r, ACT.Copy), t_load[u], used)
            tl = dve(lambda e: e.tensor_tensor(b[:, 0:m * n], r, a[:, 0:m * n].bitcast(F32), ALU.subtract),
                     ta, t_load[u], used)
            t_sub.append([ta, tl])
            while unit["load"] < min(len(plan), u + NRAW) + 0:
                load_unit()
            if j + 1 == len(subs) or subs[j + 1][0] != u:
                if unit["load"] < min(len(plan), u + NRAW + 1):
                    load_unit()

        def next_sub(ahead=LOOK, bgwork=True):
            j = unit["use"]
            unit["use"] += 1
            while unit["split"] < min(len(subs), j + ahead + 1) and (
                    unit["split"] < NSPL or unit["split"] - NSPL in t_used):
                split_sub()
            assert unit["split"] > j
            if j == 6:
                second_vectors()
            if bgwork:
                pump(PUMP[0])
            if "due" in ada and unit["load"] >= ada["due"][2] + 2:
                ada_reduce()
            return j

        PUMP = [0]

        def mms(e, ps, j, XH, XL, kb0, tok, first, final):
            _, _, m, n = subs[j]
            for k in range(m):
                a = XH[:, (kb0 + k) * 256 + tok * P:(kb0 + k) * 256 + (tok + 1) * P]
                b = XL[:, (kb0 + k) * 256 + tok * P:(kb0 + k) * 256 + (tok + 1) * P]
                wh = whi[j % NSPL][:, k * n:(k + 1) * n]
                wl = wlo[j % NSPL][:, k * n:(k + 1) * n]
                e.matmul(ps[:, 0:n], a, wh, start=first and k == 0, stop=False)
                e.matmul(ps[:, 0:n], a, wl, start=False, stop=False)
                last = e.matmul(ps[:, 0:n], b, wh, start=False, stop=final and k == m - 1)
            return last

        def part(j, XH, XL, ready, kb0, nk, tok, ps, wait):
            m = subs[j][2]
            return pe(lambda e: mms(e, ps, j, XH, XL, kb0, tok, kb0 == 0, kb0 + m == nk),
                      t_sub[j], [ready[q][tok] for q in range(kb0, kb0 + m)], wait)

        def linear(XH, XL, ready, nk, nchunk, evac, late=None):
            for c in range(nchunk):
                bk = [acc.get() for _ in range(2)]
                tok_t = [None, None]
                if late and c == 0:
                    js = []
                    for k in range(0, nk, 2):
                        js.append(next_sub(0, False))
                        tok_t[0] = part(js[-1], XH, XL, ready, k, nk, 0, bk[0][1], bk[0][2])
                    late()
                    acc.put(bk[0][0], *evac(c, 0, bk[0][1], tok_t[0]))
                    for i, k in enumerate(range(0, nk, 2)):
                        tok_t[1] = part(js[i], XH, XL, ready, k, nk, 1, bk[1][1], bk[1][2])
                        t_used[js[i]] = tok_t[1]
                        while unit["split"] < js[i] + NSPL - 2 and unit["split"] < len(subs) and (
                                unit["split"] - NSPL in t_used):
                            split_sub()
                    acc.put(bk[1][0], *evac(c, 1, bk[1][1], tok_t[1]))
                    continue
                k = 0
                while k < nk:
                    j = next_sub()
                    for tok in range(2):
                        tok_t[tok] = part(j, XH, XL, ready, k, nk, tok, bk[tok][1], bk[tok][2])
                    t_used[j] = tok_t[1]
                    k += subs[j][2]
                for tok in range(2):
                    acc.put(bk[tok][0], *evac(c, tok, bk[tok][1], tok_t[tok]))

        ones = sb("ones", P)
        t_ones = dve(lambda e: e.memset(ones[:, :], 1.0))

        st_i = [0]

        def col(n=1):
            if st_i[0] + n > 512:
                st_i[0] = 0
            o = st_i[0]
            st_i[0] += n
            return st[:, o:o + n]

        t_mh = pool(lambda e: e.memset(mhalf[:, :], -0.5))

        def rpow(v, n, mult, *after):
            w, r = col(n), col(n)
            t = pool(lambda e: e.tensor_scalar(w, v, mult, EPS, ALU.mult, ALU.add), *after)
            return r, pool(lambda e: e.tensor_tensor(r, w, mhalf[:, 0:n], ALU.pow), t, t_mh)

        def rstd(ss, nparts, count, *after):
            v = col()
            t = pool(lambda e: e.tensor_tensor(v, ss[:, 0:1], ss[:, 1:2], ALU.add), *after)
            return rpow(v, 1, 1.0 / count, t)

        row_n = [0]
        row_cnt = [0, 0]
        row_free = [None, None]

        def row_load(src, n):
            s = row_n[0] % 2
            row_n[0] += 1
            row_cnt[s] += 16
            cnt = row_cnt[s]
            sp.dma(rows[s][:, 0:n], src.rearrange("(a n) -> a n", a=1).to_broadcast([P, n]), s_row[s], 0,
                   row_free[s])
            return s, rows[s], (s_row[s], cnt)

        def transposes(src, ready, ps, dst_cols, waits):
            def f(e):
                for a, c in zip(src, dst_cols):
                    last = e.transpose(ps[:, c:c + P], a, ident)
                return last
            return pe(f, ready, waits)

        def snap():
            return [(q.sem, q.n) for q in (pe, act, dve, pool)]

        xfree = [None]
        xtf = [None, None]

        def xview(z, q, tok):
            return z[:, q * 1024:(q + 1) * 1024].rearrange("p (k n) -> p k n", k=4)[:, :, tok * P:(tok + 1) * P]

        def bcol(z):
            return z.rearrange("p (k o) -> p k o", o=1).to_broadcast([P, 4, P])

        def x_block(tok, src, ready, out, gain=None, shift=None, tg=None):
            for q in range(2):
                k0, ps, w0 = tb.get()
                tiles = [src[:, (4 * q + j) * P:(4 * q + j + 1) * P] for j in range(4)]
                t = transposes(tiles, ready[q], ps, [0, P, 2 * P, 3 * P], w0)
                v = ps[:, :].rearrange("p (k n) -> p k n", k=4)
                ho, lo = xview(xh, q, tok), xview(xl, q, tok)
                if gain is not None:
                    g = bcol(gain[:, 4 * q:4 * q + 4])
                    x = xtmp[:, q * 512:(q + 1) * 512].rearrange("p (k n) -> p k n", k=4)
                    t = dve(lambda e, x=x, v=v, g=g: e.tensor_tensor(x, v, g, ALU.mult), t, xtf[q], tg, t_vec)
                    tb.put(k0, t)
                    if shift is not None:
                        sh = bcol(shift[:, 4 * q:4 * q + 4])
                        t = dve(lambda e, x=x, sh=sh: e.tensor_tensor(x, x, sh, ALU.add), t)
                    v = x
                a = act(lambda e, ho=ho, v=v: e.activation(ho, v, ACT.Copy), t, xfree[0])
                b = dve(lambda e, ho=ho, lo=lo, v=v: e.tensor_tensor(lo, v, ho.bitcast(F32), ALU.subtract), a, t,
                        xfree[0])
                if gain is not None:
                    xtf[q] = [a, b]
                else:
                    tb.put(k0, b)
                for k in range(4 * q, 4 * q + 4):
                    out[k][tok] = [a, b]

        junk_t = [None, None]
        junk_n = [0]

        def sumsq(src, o, *after):
            k = junk_n[0] % 2
            junk_n[0] += 1
            w = src.shape[1]
            junk_t[k] = act(lambda e: e.activation(junk[:, k * 512:k * 512 + w], src, ACT.Square, accum_out=o),
                            junk_t[k], *after)
            return junk_t[k]

        def h_stats(tok, ready):
            ss = col(2)
            ts = [sumsq(h[:, tok * D + n * 512:tok * D + (n + 1) * 512], ss[:, n:n + 1], ready[n]) for n in range(2)]
            return rstd(ss, 2, D, ts)

        def ffn_body(gT_h, gT_l, ready, rs, late):
            gready = [None] * 22
            pend = []
            hid_free = [None, None]

            def flush():
                c, ths = pend.pop(0)
                hb = hid[c % 2]
                k0, ps, w0 = tb.get()
                src = [hb[:, tok * 512 + j * P:tok * 512 + (j + 1) * P] for j in range(2) for tok in range(2)]
                t = transposes(src, ths, ps, [0, P, 2 * P, 3 * P], w0)
                hid_free[c % 2] = t
                sl = slice(c * 512, (c + 1) * 512)
                a = act(lambda e: e.activation(gT_h[:, sl], ps[:, :], ACT.Copy), t, gfree[0])
                b = dve(lambda e: e.tensor_tensor(gT_l[:, sl], ps[:, :], gT_h[:, sl].bitcast(F32), ALU.subtract),
                        a, gfree[0])
                tb.put(k0, b)
                gready[2 * c] = gready[2 * c + 1] = [[a, b]] * 2

            def evac(c, tok, ps, t):
                hb = hid[c % 2]
                s1 = hb[:, tok * 512 + 256:tok * 512 + 512]
                s2 = hb[:, tok * 512:tok * 512 + 256]
                sc, tsc = rs[tok] if rs else (1.0, None)
                a = act(lambda e: e.activation(s1, ps[:, 0:256], ACT.Silu, scale=sc), t, tsc, hid_free[c % 2])
                b = dve(lambda e: e.scalar_tensor_tensor(s2, ps[:, 256:512], sc, s1, ALU.mult, ALU.mult),
                        a, t, tsc)
                if tok == 0:
                    if pend:
                        flush()
                    pend.append((c, [b]))
                else:
                    pend[-1][1].append(b)
                return [a, b]

            linear(xh, xl, ready, 8, 11, evac, late)
            xfree[0] = (pe.sem, pe.n)
            flush()
            return gready

        gfree = [None]

        def down(XH, XL, ready, nk):
            bk = [[acc.get() for _ in range(2)] for _ in range(2)]
            tt = [[None, None], [None, None]]
            seq = []
            for k in range(0, nk, 4):
                for n in range(2):
                    for q in range(k, min(k + 4, nk), 2):
                        seq.append((q, n))
            held = []

            def one(j, q, n, tok):
                tt[tok][n] = part(j, XH, XL, ready, q, nk, tok, bk[tok][n][1], bk[tok][n][2])
            for i, (q, n) in enumerate(seq):
                j = next_sub()
                one(j, q, n, 0)
                if i < len(seq) - HOLD:
                    one(j, q, n, 1)
                    t_used[j] = tt[1][n]
                else:
                    held.append((j, q, n))
            for j, q, n in held:
                one(j, q, n, 1)
                t_used[j] = tt[1][n]
            gfree[0] = (pe.sem, pe.n)
            return [[(bk[tok][n][1], bk[tok][n][0], tt[tok][n]) for n in range(2)] for tok in range(2)]

        def residual(res, factor, gain):
            s, row, trow = gain

            def run(tok):
                ss = col(2)
                ts = [sumsq(res[tok][n][0][:, :], ss[:, n:n + 1], res[tok][n][2]) for n in range(2)]
                r1, tr = rstd(ss, 2, D, ts)
                ready = []
                for n in range(2):
                    ps, k0, t = res[tok][n]
                    hs = h[:, tok * D + n * 512:tok * D + (n + 1) * 512]
                    a = dve(lambda e, ps=ps, n=n: e.scalar_tensor_tensor(
                        ps[:, :], ps[:, :], r1, row[:, n * 512:(n + 1) * 512], ALU.mult, ALU.mult), tr, trow, t, ts)
                    b = dve(lambda e, ps=ps, hs=hs: e.scalar_tensor_tensor(
                        hs, ps[:, :], factor, hs, ALU.mult, ALU.add), a, hfree[tok])
                    acc.put(k0, b)
                    ready.append(b)
                row_free[s] = b
                return ready
            return run

        hfree = [None, None]

        def enter(prev, gcol):
            ready = [[None, None] for _ in range(8)]
            rs = [None, None]

            def prep(tok, hr):
                x_block(tok, h[:, tok * D:(tok + 1) * D], hr, ready, vcol[:, gcol:gcol + 8])
                rs[tok] = h_stats(tok, hr)
                hfree[tok] = [(pe.sem, pe.n), (act.sem, act.n)]
            r0 = prev(0)
            prep(0, r0)
            r1 = prev(1)
            return ready, rs, lambda: prep(1, r1)

        def ffn_stage(prev, gcol, gain_src):
            ready, rs, late = enter(prev, gcol)
            gain = row_load(gain_src, D)
            with ExitStack() as inner:
                gh = sb(f"gh{gcol}", 22 * 256, F32R, where=inner)
                gl = sb(f"gl{gcol}", 22 * 256, F32R, where=inner)
                gready = ffn_body(gh, gl, ready, rs, late)
                res = down(gh, gl, gready, 22)
            return residual(res, 0.5, gain)

        def to_T(src, ready, dst, nblk, scale, eng, parts=P, after=None):
            ts = []
            for b0 in range(0, nblk, 2):
                nb = min(2, nblk - b0)
                k0, ps, w0 = tb.get()
                tiles, cs = [], []
                for j in range(nb):
                    for tok in range(2):
                        tiles.append(src(tok)[:, (b0 + j) * P:(b0 + j + 1) * P])
                        cs.append(j * 256 + tok * P)
                t = transposes(tiles, ready, ps, cs, w0)
                v = ps[:, 0:nb * 256].rearrange("p (b n) -> p b n", b=nb)
                o = dst[:, b0:b0 + nb, :]
                if eng is act:
                    t = act(lambda e, o=o, v=v: e.activation(o, v, ACT.Copy, scale=scale), t, after)
                else:
                    t = dve(lambda e, o=o, v=v: e.tensor_scalar(o, v, scale, None, ALU.mult), t, after)
                tb.put(k0, t)
                ts += [t] * nb
            return ts

        def split_to_x(src, sl, ready):
            a = act(lambda e: e.activation(xh[:, sl], src, ACT.Copy), ready, xfree[0])
            b = dve(lambda e: e.tensor_tensor(xl[:, sl], src, xh[:, sl].bitcast(F32), ALU.subtract), a, ready)
            return [a, b]

        def hybrid_stage(prev):
            ready, rs, late = enter(prev, 2 * 8)
            gain = row_load(T["norm_g"][0, 3], D)
            with ExitStack() as inner:
                cx = sb("cx", 4 * 286, where=inner)
                Y = sb("Y", 4 * 256, where=inner)
                SQ = sb("SQ", 4 * 256, where=inner)
                qt = sb("qt", 1024, where=inner)
                kt = sb("kt", 1024, where=inner)
                vt = sb("vt", 1024, where=inner)
                qT = sb("qT", 1024, where=inner)
                kT = sb("kT", 1024, where=inner)
                eb = [sb(f"eb{i}", 384, where=inner) for i in range(4)]
                mb = [sb(f"mb{i}", 384, where=inner) for i in range(4)]
                wb = [sb(f"wb{i}", 384, where=inner) for i in range(4)]
                pt = [sb(f"pt{i}", 256, where=inner) for i in range(2)]
                rb = sb("rb", 512, where=inner)
                cx3 = cx[:, :].rearrange("p (b n) -> p b n", b=4)
                sg, ct = hid[0], hid[1]
                t_free = snap()
                t_pad = dve(lambda e: e.memset(cx3[:, :, 0:30], 0.0), t_free)
                st_tok = {}

                def evac(c, tok, ps, t):
                    sc, tsc = rs[tok]
                    o = slice(tok * 512, (tok + 1) * 512)
                    if c == 0:
                        a = act(lambda e: e.activation(sg[:, o], ps[:, :], ACT.Sigmoid, scale=sc), t, tsc,
                                (pe.sem, pe.n), (dve.sem, dve.n))
                        st_tok["g", tok] = a
                        return [a]
                    if c == 1:
                        a = dve(lambda e: e.scalar_tensor_tensor(ct[:, o], ps[:, :], sc, sg[:, o], ALU.mult, ALU.mult),
                                t, tsc, st_tok["g", tok])
                        st_tok["c", tok] = a
                        return [a]
                    dst = {2: qt, 3: kt, 4: vt}[c]
                    a = act(lambda e: e.activation(dst[:, o], ps[:, :], ACT.Copy, scale=sc), t, tsc, t_pad)
                    st_tok[c, tok] = a
                    return [a]

                def after_u():
                    tc = to_T(lambda tok: ct[:, tok * 512:(tok + 1) * 512], [st_tok["c", 0], st_tok["c", 1]],
                              cx3[:, :, 30:286], 4, 1.0, act, after=t_pad)
                    ty = [None] * 4

                    def pool_tap(k):
                        def f():
                            b = 3
                            y = Y[:, b * 256:(b + 1) * 256]
                            x = cx[:, b * 286 + k:b * 286 + k + 256]
                            w = vcol[:, VR["cw"] + k * 4 + b:VR["cw"] + k * 4 + b + 1]
                            if k == 0:
                                bias = vcol[:, VR["cb"] + b:VR["cb"] + b + 1]
                                ty[b] = pool(lambda e: e.tensor_scalar(y, x, w, bias, ALU.mult, ALU.add),
                                             tc[b], t_pad, t_vec2, t_free)
                            else:
                                p = pt[k % 2][:, :]
                                t = pool(lambda e: e.tensor_tensor(p, x, w.to_broadcast([P, 256]), ALU.mult),
                                         ptf[k % 2], t_free)
                                ty[b] = pool(lambda e: e.tensor_tensor(y, y, p, ALU.add), ty[b], t)
                                ptf[k % 2] = ty[b]
                        return f
                    ptf = [None, None]

                    def tap(b, k):
                        def f():
                            y = Y[:, b * 256:(b + 1) * 256]
                            x = cx[:, b * 286 + k:b * 286 + k + 256]
                            w = vcol[:, VR["cw"] + k * 4 + b:VR["cw"] + k * 4 + b + 1]
                            if k == 0:
                                bias = vcol[:, VR["cb"] + b:VR["cb"] + b + 1]
                                ty[b] = dve(lambda e: e.tensor_scalar(y, x, w, bias, ALU.mult, ALU.add),
                                            tc[b], t_pad, t_vec2)
                            else:
                                ty[b] = dve(lambda e: e.scalar_tensor_tensor(y, x, w, y, ALU.mult, ALU.add), ty[b])
                        return f
                    for k in range(31):
                        pool_tap(k)()
                        for b in range(3):
                            bg.append(tap(b, k))
                    return ty

                PUMP[0] = 4
                linear(xh, xl, ready, 8, 2, evac, late)
                ty = after_u()
                linear(xh, xl, ready, 8, 3, lambda c, tok, ps, t: evac(c + 2, tok, ps, t))
                xfree[0] = (pe.sem, pe.n)
                v4 = lambda z: z[:, :].rearrange("p (b n) -> p b n", b=4)
                tq = to_T(lambda tok: qt[:, tok * 512:(tok + 1) * 512], [st_tok[2, 0], st_tok[2, 1]], v4(qT), 4,
                          0.125, act)
                tk = to_T(lambda tok: kt[:, tok * 512:(tok + 1) * 512], [st_tok[3, 0], st_tok[3, 1]], v4(kT), 4,
                          1.0, act)
                tv = [st_tok[4, 0], st_tok[4, 1]]

                Z = {}
                wfree = [None] * 4
                ld = {}
                wd = {}

                def scores(hd):
                    p0, b = 64 * (hd % 2), hd // 2
                    k0, ps, w0 = acc.get()

                    def f(e):
                        q, k = qT[p0:p0 + 64, b * 256:(b + 1) * 256], kT[p0:p0 + 64, b * 256:(b + 1) * 256]
                        e.matmul(ps[:, 0:256], k[:, 0:P], q, start=True, stop=True)
                        return e.matmul(ps[:, 256:384], k[:, P:256], q[:, P:256], start=False, stop=True,
                                        skip_group_check=True)
                    t = pe(f, tq[b], tk[b], w0)
                    z, s = ps[:, 0:384], hd % 4
                    E, M = eb[s][:, :], mb[s][:, :]
                    t1 = act(lambda e: e.activation(E, z, ACT.Abs), t, wfree[s], t_free)
                    t4 = act(lambda e: e.activation(M, z, ACT.Relu), t, wfree[s], t_free)
                    t2 = act(lambda e: e.activation(E, E, ACT.Exp, scale=-1.0), t1)
                    t3 = act(lambda e: e.activation(E, E, ACT.Ln, bias=1.0), t2)
                    t5 = dve(lambda e: e.scalar_tensor_tensor(M, M, -1.0, E, ALU.mult, ALU.subtract), t3, t4)
                    t6 = dve(lambda e: e.tensor_tensor(M, M, C("mmax"), ALU.max), t5)
                    Z[hd] = (k0, ps)
                    ld[hd] = t6

                def weights(hd):
                    k0, ps = Z[hd]
                    s = hd % 4
                    M, W = mb[s], wb[s][:, :]

                    def f(e):
                        e.matmul(ps[:, 0:384], C("tri"), M[:, 0:384], start=False, stop=True, skip_group_check=True)
                        return e.matmul(ps[:, P:256], ones[:, :], M[:, 256:384], start=False, stop=True,
                                        skip_group_check=True)
                    t = pe(f, ld[hd], t_ones)
                    t1 = act(lambda e: e.activation(W, ps[:, 0:384], ACT.Exp), t, wfree[s])
                    acc.put(k0, t1)
                    wd[hd] = dve(lambda e: e.tensor_tensor(W, W, C("mmin"), ALU.min), t1)

                pv = {}

                def values(hd):
                    s, p0, b = hd % 4, 64 * (hd % 2), hd // 2
                    if hd % 2 == 0:
                        pv[b] = acc.get()
                    k0, ps, w0 = pv[b]

                    def f(e):
                        o = ps[p0:p0 + 64, 0:256]
                        e.matmul(o, vt[:, hd * 64:(hd + 1) * 64], wb[s][:, 0:256], start=True, stop=True)
                        return e.matmul(ps[p0:p0 + 64, P:256], vt[:, 512 + hd * 64:512 + (hd + 1) * 64],
                                        wb[s][:, 256:384], start=False, stop=True, skip_group_check=True)
                    wfree[s] = pe(f, wd[hd], tv, w0)
                    if hd % 2 == 1:
                        xr = split_to_x(ps[:, 0:256], slice(b * 256, (b + 1) * 256), wfree[s])
                        acc.put(k0, *xr)
                        return xr

                xr = [None] * 8
                for s in range(11):
                    if s < 8:
                        scores(s)
                    if 0 <= s - 1 < 8:
                        weights(s - 1)
                    if 0 <= s - 3 < 8:
                        r = values(s - 3)
                        if r:
                            xr[(s - 3) // 2] = [r, r]
                    pump(4)
                pump(1000)

                k0, ps, w0 = acc.get()

                def f(e):
                    for b in range(4):
                        last = e.matmul(ps[:, 0:256], ones[:, :], Y[:, b * 256:(b + 1) * 256], start=b == 0,
                                        stop=b == 3)
                    return last
                t = pe(f, ty, t_ones, w0)
                tq2 = []
                for b in range(4):
                    y = Y[:, b * 256:(b + 1) * 256]
                    t1 = dve(lambda e, y=y: e.scalar_tensor_tensor(y, ps[:, 0:256], -1.0 / 512, y, ALU.mult, ALU.add),
                             t, ty[b])
                    tq2.append(act(lambda e, b=b, y=y: e.activation(SQ[:, b * 256:(b + 1) * 256], y, ACT.Square), t1,
                                   t_pad))
                acc.put(k0, t1)
                k0, ps2, w0 = acc.get()

                def f(e):
                    for b in range(4):
                        last = e.matmul(ps2[:, 0:256], ones[:, :], SQ[:, b * 256:(b + 1) * 256], start=b == 0,
                                        stop=b == 3)
                    return last
                t = pe(f, tq2, w0)
                t = dve(lambda e: e.tensor_scalar(rb[:, 0:256], ps2[:, 0:256], 1.0 / 512, EPS, ALU.mult, ALU.add), t)
                acc.put(k0, t)
                t = act(lambda e: e.activation(rb[:, 256:512], rb[:, 0:256], ACT.Sqrt), t)
                t = dve(lambda e: e.reciprocal(rb[:, 0:256], rb[:, 256:512]), t)
                for b in range(4):
                    y = Y[:, b * 256:(b + 1) * 256]
                    q = SQ[:, b * 256:(b + 1) * 256]
                    t1 = dve(lambda e, y=y: e.tensor_tensor(y, y, rb[:, 0:256], ALU.mult), t)
                    g = vcol[:, VR["lg"] + b:VR["lg"] + b + 1]
                    bb = vcol[:, VR["lb"] + b:VR["lb"] + b + 1]
                    t2 = act(lambda e, y=y, q=q, g=g, bb=bb: e.activation(q, y, ACT.Silu, scale=g, bias=bb), t1)
                    r = split_to_x(q, slice((4 + b) * 256, (5 + b) * 256), t2)
                    xr[4 + b] = [r, r]
                PUMP[0] = 0
                res = down(xh, xl, xr, 8)
                xfree[0] = (pe.sem, pe.n)
            return residual(res, 1.0, gain)

        def gla_stage(prev):
            ready, rs, late = enter(prev, (6 + 2) * 8)
            gain = row_load(T["norm_g"][1, 3], D)
            grow = row_load(T["gla_norm_g"][0], 256)
            with ExitStack() as inner:
                B = sb("gB", 1024, where=inner)
                QT = sb("gQT", 1024, where=inner)
                KT = sb("gKT", 1024, where=inner)
                X = [sb(f"gX{i}", 1024, where=inner) for i in range(2)]
                E1, G = X
                S = sb("gS", 1024, where=inner)
                OFF = sb("gOFF", 512, where=inner)
                vt = sb("gv", 2048, where=inner)
                sr = sb("gr", 2048, where=inner)
                levm = sb("glev", 8 * P, where=inner)
                lr = sb("glr", 32, where=inner)
                lrT = sb("glrT", 256, where=inner, parts=16)
                wg = sb("gwg", 512, where=inner, parts=16)
                qt, kt = hid[0], hid[1]
                t_free = snap()
                s_wg = sem("s_wg")
                sp.dma(wg[:, :], T["gla_w_gate"][0], s_wg, 0, t_free)
                t_S = dve(lambda e: e.memset(S[:, :], 0.0), t_free)
                got = {}

                def evac(c, tok, ps, t):
                    sc, tsc = rs[tok]
                    o = slice(tok * 512, (tok + 1) * 512)
                    if c == 0:
                        a = act(lambda e: e.activation(lr[:, tok * 16:tok * 16 + 16], ps[:, 0:16], ACT.Copy,
                                                       scale=sc), t, tsc, t_free)
                    elif c in (1, 2):
                        d = (qt, kt)[c - 1]
                        a = act(lambda e: e.activation(d[:, o], ps[:, :], ACT.Copy, scale=sc), t, tsc, t_free)
                    elif c in (3, 4):
                        d = vt[:, tok * D + (c - 3) * 512:tok * D + (c - 2) * 512]
                        a = act(lambda e: e.activation(d, ps[:, :], ACT.Copy, scale=sc), t, tsc, t_free)
                    else:
                        d = sr[:, tok * D + (c - 5) * 512:tok * D + (c - 4) * 512]
                        a = act(lambda e: e.activation(d, ps[:, :], ACT.Silu, scale=sc), t, tsc, t_free)
                    got[c, tok] = a
                    return [a]

                v3 = lambda z: z[:, :].rearrange("p (b n) -> p b n", b=4)
                linear(xh, xl, ready, 8, 1, evac, late)
                k0, ps, w0 = tb.get()

                def f(e, ps=ps):
                    for tok in range(2):
                        last = e.transpose(ps[0:16, tok * P:(tok + 1) * P], lr[:, tok * 16:tok * 16 + 16], ident)
                    return last
                t = pe(f, got[0, 0], got[0, 1], w0)
                t_lr = dve(lambda e, ps=ps: e.tensor_copy(lrT[:, :], ps[0:16, 0:256]), t, t_free)
                tb.put(k0, t_lr)
                tB = []
                for hp in range(2):
                    k0, ps, w0 = tb.get()

                    def f(e, hp=hp, ps=ps):
                        e.matmul(ps[:, 0:256], wg[:, hp * 256:hp * 256 + P], lrT[:, :], start=True, stop=True)
                        return e.matmul(ps[:, 256:512], wg[:, hp * 256 + P:hp * 256 + 256], lrT[:, :], start=False,
                                        stop=True, skip_group_check=True)
                    t = pe(f, t_lr, (s_wg, 16), w0)
                    ta = []
                    for j in range(2):
                        hd = 2 * hp + j
                        bg_ = vcol[:, VR["bg"] + hd:VR["bg"] + hd + 1]
                        x = slice(hd * 256, (hd + 1) * 256)
                        ta.append(act(lambda e, ps=ps, x=x, j=j, b=bg_: e.activation(
                            E1[:, x], ps[:, j * 256:(j + 1) * 256], ACT.Identity, bias=b), t, t_free, t_vec2))
                    tb.put(k0, *ta)
                    x2 = slice(hp * 512, (hp + 1) * 512)
                    t1 = dve(lambda e, x=x2: e.tensor_scalar(G[:, x], E1[:, x], 0.0, None, ALU.min), ta, t_free)
                    t2 = act(lambda e, x=x2: e.activation(E1[:, x], E1[:, x], ACT.Abs), t1)
                    t2 = act(lambda e, x=x2: e.activation(E1[:, x], E1[:, x], ACT.Exp, scale=-1.0), t2)
                    t2 = act(lambda e, x=x2: e.activation(E1[:, x], E1[:, x], ACT.Ln, bias=1.0), t2)
                    t3 = dve(lambda e, x=x2: e.tensor_tensor(G[:, x], G[:, x], E1[:, x], ALU.subtract), t2)
                    for j in range(4):
                        y = slice(hp * 512 + j * P, hp * 512 + (j + 1) * P)
                        tB.append(dve(lambda e, y=y: e.tensor_tensor_scan(B[:, y], ones[:, :], G[:, y], 0.0,
                                                                          ALU.mult, ALU.add), t3, t_ones, t_free))
                linear(xh, xl, ready, 8, 1, lambda c, *a: evac(c + 1, *a))
                tQ = to_T(lambda tok: qt[:, tok * 512:(tok + 1) * 512], [got[1, 0], got[1, 1]], v3(QT), 4,
                          P ** -0.5, dve, after=t_free)
                linear(xh, xl, ready, 8, 1, lambda c, *a: evac(c + 2, *a))
                tK = to_T(lambda tok: kt[:, tok * 512:(tok + 1) * 512], [got[2, 0], got[2, 1]], v3(KT), 4,
                          1.0, dve, after=t_free)

                sT = {"S": t_S}
                xf = [None, None]
                s_lev = sem("s_lev")
                o_lev = const_at["lev"][0]
                sp.dma(levm[:, :], T["const"][:, o_lev:o_lev + 8 * P], s_lev, 0, t_free)

                def level(n):
                    steps = []
                    Xb, XT = X[n % 2], {}

                    if n == 0:
                        def a0():
                            XT["t"] = [tQ, tK]
                        steps.append(a0)
                    else:
                        m = 2 ** (n - 1)
                        view = lambda z: z[:, :].rearrange("p (x a m) -> p x a m", a=2, m=m)
                        nx = 512 // m
                        ref = view(B)[:, :, 0, m - 1:m].to_broadcast([P, nx, m])

                        def a1():
                            t = pool(lambda e: e.tensor_tensor(view(Xb)[:, :, 0, :], ref, view(B)[:, :, 0, :],
                                                              ALU.subtract), tB, xf[n % 2])
                            if m < P:
                                t2 = pool(lambda e: e.tensor_tensor(view(Xb)[:, :, 1, :], view(B)[:, :, 1, :], ref,
                                                                   ALU.subtract), tB, xf[n % 2])
                            else:
                                t2 = dve(lambda e: e.tensor_copy(view(Xb)[:, :, 1, :], view(B)[:, :, 1, :]), tB,
                                         xf[n % 2])
                            XT["e"] = act(lambda e: e.activation(Xb[:, :], Xb[:, :], ACT.Exp, scale=1.0 / 16), t, t2)

                        def a2():
                            t = dve(lambda e: e.tensor_tensor(view(Xb)[:, :, 0, :], view(Xb)[:, :, 0, :],
                                                              view(KT)[:, :, 0, :], ALU.mult), XT["e"], tK)
                            t2 = dve(lambda e: e.tensor_tensor(view(Xb)[:, :, 1, :], view(Xb)[:, :, 1, :],
                                                               view(QT)[:, :, 1, :], ALU.mult), XT["e"], tQ)
                            XT["t"] = [t, t2]
                        steps += [a1, a2]

                    def half(j):
                        def f():
                            k0, ps, w0 = tb.get()
                            if n < 8:
                                def g(e):
                                    for i in range(4):
                                        y = slice(j * 512 + i * P, j * 512 + (i + 1) * P)
                                        l, r = (KT, QT) if n == 0 else (Xb, Xb)
                                        last = e.matmul(ps[:, i * P:(i + 1) * P], l[:, y], r[:, y], start=i == 0,
                                                        stop=True, skip_group_check=True)
                                    return last
                                t = pe(g, XT["t"], w0)
                                s4 = S[:, j * 512:(j + 1) * 512].rearrange("p (i n) -> p i n", i=4)
                                mk = levm[:, n * P:(n + 1) * P].bitcast(U32).rearrange(
                                    "p (i n) -> p i n", i=1).to_broadcast([P, 4, P])
                                sT[j] = dve(lambda e: e.copy_predicated(
                                    s4, mk, ps[:, :].rearrange("p (i n) -> p i n", i=4)), t, sT.get(j, sT["S"]), (s_lev, 16))
                                tb.put(k0, sT[j])
                            else:
                                def g(e):
                                    for i in range(4):
                                        last = e.matmul(ps[:, i * P:(i + 1) * P], Xb[:, i * 256:i * 256 + P],
                                                        Xb[:, i * 256 + P:(i + 1) * 256], start=i == 0,
                                                        stop=True, skip_group_check=True)
                                    return last
                                t = pe(g, XT["t"], w0)
                                sT["off"] = dve(lambda e: e.tensor_copy(OFF[:, :], ps[:, :]), t, t_free)
                                tb.put(k0, sT["off"])
                            xf[n % 2] = t
                        return f
                    steps.append(half(0))
                    if n < 8:
                        steps.append(half(1))
                    return steps

                lv = [level(n) for n in range(9)]
                bg.append(lv[1][0])
                bg.extend(lv[0][1:])
                bg.append(lv[0][0])
                bg.insert(1, bg.pop())
                for n in range(1, 9):
                    bg.append(lv[n][1])
                    if n < 8:
                        bg.append(lv[n + 1][0])
                    bg.extend(lv[n][2:])
                PUMP[0] = 3
                linear(xh, xl, ready, 8, 4, lambda c, *a: evac(c + 3, *a))
                pump(1000)
                PUMP[0] = 0
                xfree[0] = (pe.sem, pe.n)
                orow, torow = grow[1], grow[2]
                xr = [[None, None] for _ in range(8)]
                opened = []

                def outputs(tok, hd):
                    k0, ps, w0 = acc.get()

                    def f(e):
                        vv = lambda b: vt[:, b * D + hd * 256:b * D + (hd + 1) * 256]
                        last = e.matmul(ps[:, 0:256], S[:, hd * 256 + tok * P:hd * 256 + (tok + 1) * P],
                                        vv(tok), start=True, stop=tok == 0)
                        if tok:
                            last = e.matmul(ps[:, 0:256], OFF[:, hd * P:(hd + 1) * P], vv(0), start=False,
                                            stop=True)
                        return last
                    t = pe(f, sT[0], sT[1], sT["off"], got[3, tok], got[4, tok], got[3, 0], got[4, 0], w0)
                    ss = col()
                    ts = sumsq(ps[:, 0:256], ss, t)
                    r, tr = rpow(ss, 1, 1.0 / 256, ts)
                    return tok, hd, k0, ps, r, tr

                def normed(tok, hd, k0, ps, r, tr):
                    o = slice(tok * D + hd * 256, tok * D + (hd + 1) * 256)
                    a = dve(lambda e: e.scalar_tensor_tensor(
                        ps[:, 0:256], ps[:, 0:256], r, orow[:, 0:256], ALU.mult, ALU.mult), tr, torow)
                    b = dve(lambda e: e.tensor_tensor(sr[:, o], ps[:, 0:256], sr[:, o], ALU.mult),
                            a, got[5, tok], got[6, tok])
                    acc.put(k0, b)
                    got["o", tok, hd] = row_free[grow[0]] = b

                for n in range(11):
                    if n < 8:
                        opened.append(outputs(n // 4, n % 4))
                    if n >= 3:
                        normed(*opened.pop(0))
                    if n in (6, 10):
                        tok = n // 8
                        x_block(tok, sr[:, tok * D:(tok + 1) * D],
                                [[got["o", tok, 2 * q], got["o", tok, 2 * q + 1]] for q in range(2)], xr)
                res = down(xh, xl, xr, 8)
                xfree[0] = (pe.sem, pe.n)
            return residual(res, 1.0, gain)

        ada_view = T["w_ada_2"].rearrange("(p k) n -> p k n", k=8)
        ada = {"tile": 0, "t": [], "acc_free": None, "pe": 0}

        def ada_load():
            j = ada["tile"]
            if j >= 96 or "due" in ada:
                return
            ada["tile"] += 1
            c, k = divmod(j, 8)
            sp.dma(adat[j % 2][:, :], ada_view[:, k, c * 512:(c + 1) * 512], s_ada[j % 2], 0,
                   ada["t"][j - 2] if j >= 2 else None)
            if k:
                ada_add(j - 1)
            if k == 7:
                ada["due"] = (c, j, unit["load"])

        def ada_add(j):
            k = j % 8
            buf = adat[j % 2][:, :]
            arrived = (s_ada[j % 2], 16 * (j // 2 + 1))
            sc = scol[:, 8 + k:9 + k]
            last = ada["t"][j - 1] if j else None
            if k == 0:
                t = dve(lambda e: e.tensor_scalar(adaacc[:, :], buf, sc, None, ALU.mult), arrived, t_vec2,
                        ada["acc_free"], last)
            else:
                t = dve(lambda e: e.scalar_tensor_tensor(adaacc[:, :], buf, sc, adaacc[:, :], ALU.mult, ALU.add),
                        arrived, last)
            ada["t"].append(t)

        def ada_reduce():
            if "due" not in ada:
                return
            c, j, _ = ada.pop("due")
            ada_add(j)
            t = ada["t"][j]
            k0, ps, w0 = tb.get()

            def f(e):
                for j in range(4):
                    last = e.matmul(ps[:, j:j + 1], adaacc[:, j * P:(j + 1) * P], ones[:, 0:1], start=j == 0,
                                    stop=True, skip_group_check=True)
                return last
            t1 = pe(f, t, t_ones, w0)
            b = vcol[:, VR["ba"] + 4 * c:VR["ba"] + 4 * c + 4]
            t2 = dve(lambda e: e.tensor_tensor(modc[:, 4 * c:4 * c + 4], ps[:, 0:4], b, ALU.add), t1, t_vec2)
            tb.put(k0, t2)
            ada["acc_free"] = t1
            ada["mod"] = t2

        def enter_ada(prev, wcol, shift, scale):
            gw = col(8)
            tg = dve(lambda e: e.scalar_tensor_tensor(gw, modc[:, scale * 8:scale * 8 + 8], 1.0,
                                                      vcol[:, wcol:wcol + 8], ALU.add, ALU.mult), ada["mod"], t_vec2)
            ready = [[None, None] for _ in range(8)]
            tf = snap()

            def prep(tok, hr):
                r, tr = h_stats(tok, hr)
                tx = [dve(lambda e, q=q: e.tensor_scalar(
                    hid[tok][:, q * 512:(q + 1) * 512], h[:, tok * D + q * 512:tok * D + (q + 1) * 512], r, None,
                    ALU.mult), tr, hr[q], tf) for q in range(2)]
                x_block(tok, hid[tok][:, :], tx, ready, gw, modc[:, shift * 8:shift * 8 + 8], tg)
                hfree[tok] = [tx, (act.sem, act.n)]
            prep(0, prev(0))
            r1 = prev(1)
            return ready, lambda: prep(1, r1)

        def gate_row(which):
            s = row_n[0] % 2
            row_n[0] += 1
            dst = rows[s]
            t_free = snap()
            tr = []
            for n in range(2):
                dg = hid[n]
                td = []
                for j in range(4):
                    cc = modc[:, which * 8 + 4 * n + j:which * 8 + 4 * n + j + 1]
                    td.append(dve(lambda e, j=j, cc=cc, dg=dg: e.tensor_scalar(
                        dg[:, j * P:(j + 1) * P], ident, cc, None, ALU.mult), ada["mod"], t_free))
                k0, ps, w0 = tb.get()
                t = pe(lambda e, ps=ps, dg=dg: e.matmul(ps[:, :], ones[:, :], dg[:, 0:512], start=True, stop=True),
                       td, w0)
                t = act(lambda e, ps=ps, n=n: e.activation(dst[:, n * 512:(n + 1) * 512], ps[:, :], ACT.Copy), t,
                        row_free[s], t_free)
                tb.put(k0, t)
                tr.append(t)
            return s, dst, tr

        def residual_gate(res, gain):
            s, row, trow = gain

            def run(tok):
                ready = []
                for n in range(2):
                    ps, k0, t = res[tok][n]
                    hs = h[:, tok * D + n * 512:tok * D + (n + 1) * 512]
                    a = dve(lambda e, ps=ps, n=n: e.tensor_tensor(ps[:, :], ps[:, :], row[:, n * 512:(n + 1) * 512],
                                                                  ALU.mult), t, trow)
                    b = dve(lambda e, ps=ps, hs=hs: e.tensor_tensor(hs, ps[:, :], hs, ALU.add), a, hfree[tok])
                    acc.put(k0, b)
                    ready.append(b)
                row_free[s] = b
                return ready
            return run

        def second_mixer(prev):
            with ExitStack() as inner:
                ar = sb("ar2", 13712, where=inner)
                AH = sb("AH", 1024, F32R, where=inner)
                AL = sb("AL", 1024, F32R, where=inner)
                tf = snap()
                off = [0]

                def A(n, at=None):
                    if at is None:
                        at = off[0]
                        off[0] += n
                    return ar[:, at:at + n]
                iqT, qaT, kaT, va, ikT = A(1024), A(1024), A(1024), A(1024), A(256)
                sga, sgb = A(2048, 0), A(2048, 2048)
                MB = A(384)
                SCW = off[0]
                SC, W = A(384), A(384)
                PB = [SC, W, iqT[:, 0:384]]
                pT = [A(384), A(384), iqT[:, 384:768]]
                off[0] = SCW + 1536
                RSb = A(1536, SCW)
                qrT, krT, vr, sgr = A(1024), A(1024), A(2048), A(2048)
                rt = A(512)
                decay = hid[1][:, :]
                iw, ik2 = A(16), A(256)
                assert off[0] <= 13712, off[0]
                s_dec = sem("s_dec")
                ready, late = enter_ada(prev, VR["n1"], 0, 1)
                gnr = row_load(T["gn_w_2"], D)
                v4 = lambda z: z.rearrange("p (b n) -> p b n", b=4)
                rtf = [None]
                hf = [[None], [None]]

                def rope(eng, buf, tok, nh, hd, half, cs, sn, ready, extra=None):
                    v = buf.rearrange("p (x d) -> p x d", d=hd)
                    x1, x2 = v[:, :, 0:half], v[:, :, half:2 * half]
                    w = nh * half
                    t1b = rt[:, 0:w].rearrange("p (x d) -> p x d", d=half)
                    t2b = rt[:, 256:256 + w].rearrange("p (x d) -> p x d", d=half)
                    bc = lambda z: z.rearrange("p (x d) -> p x d", x=1).to_broadcast([P, nh, half])
                    c_, s_ = bc(C(cs, tok * half, half)), bc(C(sn, tok * half, half))
                    tt = lambda o, a, b, op, *w_: eng(lambda e: e.tensor_tensor(o, a, b, op), *w_)
                    a = tt(t1b, x1, s_, ALU.mult, ready, rtf[0], t_in2, tf)
                    b = tt(t2b, x2, s_, ALU.mult, ready, rtf[0], t_in2, tf)
                    c = tt(x1, x1, c_, ALU.mult, a)
                    d = tt(x2, x2, c_, ALU.mult, b)
                    f1 = tt(x1, x1, t2b, ALU.subtract, c, b)
                    f2 = tt(x2, x2, t1b, ALU.add, d, a)
                    rtf[0] = [f1, f2]
                    return [f1, f2]

                def roped(i, dst, nblk_dims, scale, full):
                    tk = [None, None]

                    def evac(c, tok, ps, t):
                        o = hid[i][:, tok * 512:(tok + 1) * 512]
                        a = act(lambda e: e.activation(o, ps[:, :], ACT.Copy), t, hf[i], tf)
                        if full:
                            tk[tok] = rope(pool, o, tok, 4, 128, 64, "cosr", "sinr", a)
                        else:
                            tk[tok] = rope(pool, o, tok, 8, 64, 8, "cosa", "sina", a)
                        return [a]

                    def finish():
                        r = to_T(lambda tok: hid[i][:, tok * 512:(tok + 1) * 512], tk, dst, 4, scale, act, after=tf)
                        hf[i] = (pe.sem, pe.n)
                        return r
                    return evac, finish

                got = {}
                def ev_ik(c, tok, ps, t):
                    i2 = ik2[:, tok * P:(tok + 1) * P].rearrange("p (a d) -> p a d", a=2)
                    a = act(lambda e: e.activation(i2[:, 0, :], ps[:, 0:64], ACT.Copy), t, tf)
                    b = act(lambda e: e.activation(iw[:, tok * 8:tok * 8 + 8], ps[:, 64:72], ACT.Copy,
                                                   scale=8.0 ** -0.5), t, tf)
                    tr = rope(pool, i2[:, 0, :], tok, 1, 64, 8, "cosa", "sina", a)
                    got["ik", tok] = pool(lambda e: e.tensor_copy(i2[:, 1, :], i2[:, 0, :]), tr)
                    got["iw", tok] = b
                    return [a, b]

                linear(xh, xl, ready, 8, 1, ev_ik, late)
                hf = [(pe.sem, pe.n)] * 2
                e1, f1 = roped(0, v4(iqT), 4, 1.0, False)
                linear(xh, xl, ready, 8, 1, e1)
                k0, ps, w0 = tb.get()
                t = transposes([ik2[:, 0:P], ik2[:, P:256]], [got["ik", 0], got["ik", 1]], ps, [0, P], w0)
                tik = act(lambda e, ps=ps: e.activation(ikT, ps[:, 0:256], ACT.Copy), t, tf)
                tb.put(k0, tik)
                e2, f2 = roped(1, v4(qaT), 4, 0.125, False)
                linear(xh, xl, ready, 8, 1, e2)
                tiq = f1()
                e3, f3 = roped(0, v4(kaT), 4, 1.0, False)
                linear(xh, xl, ready, 8, 1, e3)
                tqa = f2()

                def ev_va(c, tok, ps, t):
                    a = act(lambda e: e.activation(va[:, tok * 512:(tok + 1) * 512], ps[:, :], ACT.Copy), t, tf)
                    got["va", tok] = a
                    return [a]

                ch = {"t": [None, None]}
                cut = [slice(0, P), slice(P, 384)]

                def idx_head(hd):
                    def f():
                        p0, b = 64 * (hd % 2), hd // 2
                        k0, ps, w0 = tb.get()

                        def g(e):
                            q, k = iqT[p0:p0 + 64, b * 256:(b + 1) * 256], ikT[p0:p0 + 64, :]
                            e.matmul(ps[:, 0:P], q[:, 0:P], k[:, 0:P], start=True, stop=True)
                            return e.matmul(ps[:, P:384], q[:, P:256], k, start=False, stop=True,
                                            skip_group_check=True)
                        t = pe(g, tiq[b], tik, w0)
                        R = pT[hd % 2]
                        t = act(lambda e: e.activation(R, ps[:, 0:384], ACT.Relu, scale=0.125), t,
                                ch.get(("r", hd % 2)), tf)
                        tb.put(k0, t)
                        for j in range(2):
                            wv = iw[:, j * 8 + hd:j * 8 + hd + 1]
                            if hd == 0:
                                ch["t"][j] = dve(lambda e, j=j, wv=wv: e.tensor_scalar(
                                    SC[:, cut[j]], R[:, cut[j]], wv, None, ALU.mult), t, got["iw", j], tf)
                            else:
                                ch["t"][j] = dve(lambda e, j=j, wv=wv: e.scalar_tensor_tensor(
                                    SC[:, cut[j]], R[:, cut[j]], wv, SC[:, cut[j]], ALU.mult, ALU.add), t,
                                    ch["t"][j], got["iw", j])
                        ch["r", hd % 2] = list(ch["t"])
                        ch["idx"] = (pe.sem, pe.n)
                    return f

                def causal():
                    for j, s_ in enumerate((slice(0, P), slice(256, 384))):
                        ch["t"][j] = dve(lambda e, s_=s_: e.tensor_tensor(SC[:, s_], SC[:, s_], C("caus"), ALU.add),
                                         ch["t"][j])

                def top8(n):
                    def f():
                        for j in range(2):
                            src = SC if n == 0 else W
                            m8 = got.setdefault(("m8", j, n % 2), col(8))
                            t = dve(lambda e, j=j, src=src, m8=m8: e.max(m8, src[:, cut[j]]), ch["t"][j], tf)
                            ch["t"][j] = dve(lambda e, j=j, src=src, m8=m8: e.match_replace(
                                W[:, cut[j]], m8, src[:, cut[j]], -BIG), t)
                    return f

                def choose():
                    t = dve(lambda e: e.tensor_scalar(MB, W, -2e38, None, ALU.is_le), ch["t"], tf)
                    t = dve(lambda e: e.tensor_scalar(MB, MB, -1.0, 1e30, ALU.add, ALU.mult), t)
                    for s_ in (slice(0, P), slice(256, 384)):
                        t = dve(lambda e, s_=s_: e.tensor_tensor(MB[:, s_], MB[:, s_], C("caus"), ALU.min), t)
                    ch["m"] = t
                    ch["p"] = [[t], [t], [t, ch["idx"]]]

                LG = {}

                def logits(hd):
                    p0, b, s = 64 * (hd % 2), hd // 2, hd % 3
                    k0, ps, w0 = tb.get()

                    def g(e):
                        q, k = qaT[p0:p0 + 64, b * 256:(b + 1) * 256], kaT[p0:p0 + 64, b * 256:(b + 1) * 256]
                        e.matmul(ps[:, 0:P], q[:, 0:P], k[:, 0:P], start=True, stop=True)
                        return e.matmul(ps[:, P:384], q[:, P:256], k, start=False, stop=True,
                                        skip_group_check=True)
                    t = pe(g, tqa[b], got["tka"][b], w0)
                    mx, nm, sm, ri = col(2), col(2), col(2), col(2)
                    ts = []
                    for j in range(2):
                        ts.append(dve(lambda e, j=j: e.tensor_tensor_reduce(
                            out=PB[s][:, cut[j]], in0=ps[:, cut[j]], in1=MB[:, cut[j]], scale=1.0, scalar=-BIG,
                            op0=ALU.add, op1=ALU.max, accum_out=mx[:, j:j + 1]), t, ch["m"], ch["p"][s]))
                    tb.put(k0, *ts)
                    t = dve(lambda e: e.tensor_scalar(nm, mx, -1.0, None, ALU.mult), ts)
                    te = [act(lambda e, j=j: e.activation(PB[s][:, cut[j]], PB[s][:, cut[j]], ACT.Exp,
                                                          bias=nm[:, j:j + 1], accum_out=sm[:, j:j + 1]), t, ts)
                          for j in range(2)]
                    t = dve(lambda e: e.reciprocal(ri, sm), te)
                    LG[hd] = [dve(lambda e, j=j: e.tensor_scalar(PB[s][:, cut[j]], PB[s][:, cut[j]], ri[:, j:j + 1],
                                                                 None, ALU.mult), t, te) for j in range(2)]

                def probs(hd):
                    s = hd % 3
                    k0, ps, w0 = tb.get()
                    t = transposes([PB[s][:, 0:P], PB[s][:, P:256], PB[s][:, 256:384]], LG[hd], ps, [0, P, 256], w0)
                    ch["p"][s] = t
                    t = act(lambda e: e.activation(pT[s], ps[:, 0:384], ACT.Copy), t, ch.get(("v", s)), ch["m"])
                    tb.put(k0, t)
                    LG[hd] = t

                def att_values(hd):
                    s, p0, b = hd % 3, 64 * (hd % 2), hd // 2
                    if hd % 2 == 0:
                        ch["pv"] = acc6.get()
                    k0, ps, w0 = ch["pv"]

                    def g(e):
                        e.matmul(ps[p0:p0 + 64, 0:256], va[:, hd * 64:(hd + 1) * 64], pT[s][:, 0:256],
                                 start=True, stop=True)
                        return e.matmul(ps[p0:p0 + 64, P:256], va[:, 512 + hd * 64:512 + (hd + 1) * 64],
                                        pT[s][:, 256:384], start=False, stop=True, skip_group_check=True)
                    t = pe(g, LG[hd], got["va", 0], got["va", 1], w0)
                    ch["v", s] = t
                    if hd % 2 == 1:
                        sl = slice(b * 256, (b + 1) * 256)
                        a = act(lambda e: e.activation(AH[:, sl], ps[:, 0:256], ACT.Copy), t, tf)
                        c = dve(lambda e: e.tensor_tensor(AL[:, sl], ps[:, 0:256], AH[:, sl].bitcast(F32),
                                                          ALU.subtract), a, tf)
                        acc6.put(k0, c)
                        got["att", b] = [[a, c]] * 2

                acc6 = acc
                for hd in range(8):
                    bg.append(idx_head(hd))
                bg.append(causal)
                for n in range(8):
                    bg.append(top8(n))
                bg.append(choose)
                PUMP[0] = 1
                linear(xh, xl, ready, 8, 1, ev_va)
                got["tka"] = f3()
                for s in range(11):
                    def stp(s=s):
                        if 0 <= s - 3 < 8:
                            att_values(s - 3)
                        if 0 <= s - 2 < 8:
                            probs(s - 2)
                        if s < 8:
                            logits(s)
                    bg.append(stp)
                e4, f4 = roped(1, v4(qrT), 4, 1.0, True)
                linear(xh, xl, ready, 8, 1, e4)
                e5, f5 = roped(0, v4(krT), 4, 1.0, True)
                linear(xh, xl, ready, 8, 1, e5)
                tqr = f4()

                def ev_vr(c, tok, ps, t):
                    o = slice(tok * D + c * 512, tok * D + (c + 1) * 512)
                    a = act(lambda e: e.activation(vr[:, o], ps[:, :], ACT.Copy), t, tf)
                    got["vr", c, tok] = a
                    return [a]

                linear(xh, xl, ready, 8, 2, ev_vr)
                tkr = f5()
                o_dec = const_at["dec"][0]
                sp.dma(decay, T["const"][:, o_dec:o_dec + 1024], s_dec, 0, snap())

                def ev_gr(c, tok, ps, t):
                    o = slice(tok * D + c * 512, tok * D + (c + 1) * 512)
                    a = act(lambda e: e.activation(sgr[:, o], ps[:, :], ACT.Silu), t, tf)
                    b = pool(lambda e: e.tensor_tensor(sgr[:, o], sgr[:, o], gnr[1][:, c * 512:(c + 1) * 512],
                                                       ALU.mult), a, gnr[2])
                    got["gr", c, tok] = b
                    row_free[gnr[0]] = b
                    return [a]

                linear(xh, xl, ready, 8, 2, ev_gr)
                pump(1000)
                t_dsa = snap()

                for hd in range(4):
                    def f(hd=hd):
                        k0, ps, w0 = tb.get()

                        def g(e):
                            q, k = qrT[:, hd * 256:(hd + 1) * 256], krT[:, hd * 256:(hd + 1) * 256]
                            e.matmul(ps[:, 0:256], k[:, 0:P], q, start=True, stop=True)
                            return e.matmul(ps[:, 256:384], k[:, P:256], q[:, P:256], start=False, stop=True,
                                            skip_group_check=True)
                        t = pe(g, tqr[hd], tkr[hd], w0)
                        o = hd * 384
                        a = dve(lambda e: e.tensor_tensor(RSb[:, o:o + 256], ps[:, 0:256],
                                                          decay[:, hd * 256:(hd + 1) * 256], ALU.mult), t, t_dsa,
                                (s_dec, 16))
                        b = dve(lambda e: e.tensor_tensor(RSb[:, o + 256:o + 384], ps[:, 256:384],
                                                          decay[:, hd * 256:hd * 256 + P], ALU.mult), t, t_dsa,
                                (s_dec, 16))
                        tb.put(k0, b)
                        got["rs", hd] = [a, b]
                    bg.append(f)
                for tok in range(2):
                    for hd in range(4):
                        def f(tok=tok, hd=hd):
                            k0, ps, w0 = tb.get()
                            vv = lambda b: vr[:, b * D + hd * 256:b * D + (hd + 1) * 256]

                            def g(e):
                                o = hd * 384
                                if tok == 0:
                                    return e.matmul(ps[:, 0:256], RSb[:, o:o + P], vv(0), start=True, stop=True)
                                e.matmul(ps[:, 0:256], RSb[:, o + P:o + 256], vv(0), start=True, stop=False)
                                return e.matmul(ps[:, 0:256], RSb[:, o + 256:o + 384], vv(1), start=False, stop=True)
                            c = hd // 2
                            t = pe(g, got["rs", hd], got["vr", c, 0], got["vr", c, 1], w0)
                            s6, mv = col(6), col(2)
                            t = dve(lambda e: e.bn_stats(s6, ps[:, 0:256]), t)
                            t = dve(lambda e: e.bn_aggr(mv, s6), t)
                            r2, t3 = rpow(mv[:, 1:2], 1, 1.0, t)
                            t3 = dve(lambda e: e.tensor_scalar(ps[:, 0:256], ps[:, 0:256], mv[:, 0:1], r2,
                                                               ALU.subtract, ALU.mult), t3)
                            o = slice(tok * D + hd * 256, tok * D + (hd + 1) * 256)
                            t3 = dve(lambda e: e.tensor_tensor(sgr[:, o], ps[:, 0:256], sgr[:, o], ALU.mult), t3,
                                     got["gr", c, tok])
                            tb.put(k0, t3)
                            got["yr", tok, hd] = t3
                        bg.append(f)

                def ev_g(dst, key):
                    def ev(c, tok, ps, t):
                        o = slice(tok * D + c * 512, tok * D + (c + 1) * 512)
                        a = act(lambda e: e.activation(dst[:, o], ps[:, :], ACT.Sigmoid), t, t_dsa)
                        got[key, c, tok] = a
                        return [a]
                    return ev
                linear(xh, xl, ready, 8, 2, ev_g(sga, "ga"))
                linear(xh, xl, ready, 8, 2, ev_g(sgb, "gb"))
                xfree[0] = (pe.sem, pe.n)
                PUMP[0] = 0
                pump(1000)

                def gated(res, dst, key):
                    ts = []
                    for tok in range(2):
                        for n in range(2):
                            ps, k0, t = res[tok][n]
                            o = slice(tok * D + n * 512, tok * D + (n + 1) * 512)
                            b = dve(lambda e, ps=ps, o=o: e.tensor_tensor(dst[:, o], ps[:, :], dst[:, o], ALU.mult),
                                    t, got[key, n, tok])
                            acc.put(k0, b)
                            ts.append(b)
                    return ts
                xr = [[None, None] for _ in range(8)]
                for tok in range(2):
                    x_block(tok, sgr[:, tok * D:(tok + 1) * D],
                            [[got["yr", tok, 2 * q], got["yr", tok, 2 * q + 1]] for q in range(2)], xr)
                gain = gate_row(2)
                ta = gated(down(AH, AL, [got["att", b] for b in range(4)], 4), sga, "ga")
                tbb = gated(down(xh, xl, xr, 8), sgb, "gb")
                xfree[0] = (pe.sem, pe.n)
                tm = [dve(lambda e, n=n: e.tensor_tensor(sga[:, n * 512:(n + 1) * 512], sga[:, n * 512:(n + 1) * 512],
                                                         sgb[:, n * 512:(n + 1) * 512], ALU.add), ta[n], tbb[n])
                      for n in range(4)]
                xr = [[None, None] for _ in range(8)]
                for tok in range(2):
                    x_block(tok, sga[:, tok * D:(tok + 1) * D], tm[2 * tok:2 * tok + 2], xr)
                res = down(xh, xl, xr, 8)
                xfree[0] = (pe.sem, pe.n)
            return residual_gate(res, gain)

        def second_ffn(prev):
            ready, late = enter_ada(prev, VR["n2"], 3, 4)
            with ExitStack() as inner:
                gh = sb("ghf", 22 * 256, F32R, where=inner)
                gl = sb("glf", 22 * 256, F32R, where=inner)
                gready = ffn_body(gh, gl, ready, None, late)
                gain = gate_row(5)
                res = down(gh, gl, gready, 22)
            return residual_gate(res, gain)

        def plan_down(w, nk):
            for k in range(0, nk, 4):
                m = min(4, nk - k)
                for n in range(2):
                    plan.append((w[k * P:(k + m) * P, n * 512:(n + 1) * 512]
                                 .rearrange("(k p) n -> p k n", p=P), m, 512))

        if UPTO >= 1:
            plan_ffn([T["ffn1_w_in"][0]], T["ffn1_w_out"][0])
        if UPTO >= 2:
            for c in (4, 3, 0, 1, 2):
                plan_cols(T["hyb_w_in"][0], c * 512, 512, 8)
            plan_down(T["hyb_w_out"][0], 8)
        if UPTO >= 3:
            plan_ffn([T["ffn2_w_in"][0]], T["ffn2_w_out"][0])

        if UPTO >= 4:
            plan_ffn([T["ffn1_w_in"][1]], T["ffn1_w_out"][1])
        if UPTO >= 5:
            plan_cols(T["gla_w_in"][0], 3072, 16, 8)
            for c in range(6):
                plan_cols(T["gla_w_in"][0], c * 512, 512, 8)
            plan_down(T["gla_w_out"][0], 8)
        if UPTO >= 6:
            plan_ffn([T["ffn2_w_in"][1]], T["ffn2_w_out"][1])

        if UPTO >= 7:
            w = T["w_in_2"]
            plan_cols(w, 2048, 72, 8)
            for c in (1536, 0, 512, 1024, 2120, 2632, 3144, 3656, 4168, 4680, 5192, 5704, 6216, 6728):
                plan_cols(w, c, 512, 8)
            plan_down(T["w_attn_proj_2"], 4)
            plan_down(T["w_ret_proj_2"], 8)
            plan_down(T["w_out_2"], 8)
        if UPTO >= 8:
            plan_ffn([T["w_ffn_gate_2"], T["w_ffn_up_2"]], T["w_ffn_down_2"])

        cut_subs()
        stages = [lambda p: ffn_stage(p, 0, T["norm_g"][0, 1]), hybrid_stage,
                  lambda p: ffn_stage(p, 4 * 8, T["norm_g"][0, 5]),
                  lambda p: ffn_stage(p, 6 * 8, T["norm_g"][1, 1]), gla_stage,
                  lambda p: ffn_stage(p, 10 * 8, T["norm_g"][1, 5]), second_mixer, second_ffn]
        prev = lambda tok: [t_in, t_in]
        for stage in stages[:UPTO]:
            prev = stage(prev)
        frow = row_load(T["final_norm_w_2"], D)
        for tok in range(2):
            hr = prev(tok)
            if UPTO > 8:
                r, tr = h_stats(tok, hr)
                for n in range(2):
                    hs = h[:, tok * D + n * 512:tok * D + (n + 1) * 512]
                    hr[n] = dve(lambda e, hs=hs, r=r, n=n: e.scalar_tensor_tensor(
                        hs, hs, r, frow[1][:, n * 512:(n + 1) * 512], ALU.mult, ALU.mult), tr, frow[2])
            for n in range(2):
                sp.dma(out[0, tok * P:(tok + 1) * P, n * 512:(n + 1) * 512],
                       h[:, tok * D + n * 512:tok * D + (n + 1) * 512], s_out, 0, hr[n])
        sp.wait((s_out, 64))

        block = ctx.enter_context(nc.Block())
        block.sync(lambda e: sp.run(e))
        block.tensor(lambda e: pe.run(e))
        block.scalar(lambda e: act.run(e))
        block.vector(lambda e: dve.run(e))
        block.gpsimd(lambda e: pool.run(e))


_INS = ["x", "norm_g", "ffn1_w_in", "ffn1_w_out", "ffn2_w_in", "ffn2_w_out", "hyb_w_in", "hyb_w_out", "conv_dw_w",
        "conv_dw_b", "conv_ln_g", "conv_ln_b", "gla_w_in", "gla_w_gate", "gla_b_gate", "gla_norm_g", "gla_w_out",
        "c_2", "w_ada_2", "b_ada_2", "norm1_w_2", "w_in_2", "w_attn_proj_2", "w_ret_proj_2", "gn_w_2", "w_out_2",
        "norm2_w_2", "w_ffn_gate_2", "w_ffn_up_2", "w_ffn_down_2", "final_norm_w_2"]


def kernel(**inputs):
    import numpy as _np
    import concourse.bacc as _bacc
    from concourse import mybir as _mybir
    from concourse.bass_utils import run_bass_kernel_spmd as _run

    nc = _bacc.Bacc("TRN2", target_bir_lowering=False, num_devices=1)
    const_at, const = constants()
    arrays, T = {}, {}
    for name in _INS:
        a = _np.ascontiguousarray(inputs[name])
        arrays[f"in_{name}_dram"] = a
        T[name] = nc.dram_tensor(f"in_{name}_dram", a.shape, _mybir.dt.from_np(a.dtype), kind="ExternalInput").ap()
    arrays["in_const_dram"] = const
    T["const"] = nc.dram_tensor("in_const_dram", const.shape, _mybir.dt.float32, kind="ExternalInput").ap()
    out = nc.dram_tensor("out_0_dram", (1, 256, 1024), _mybir.dt.float32, kind="ExternalOutput").ap()
    program(nc, T, const_at, out)
    r = _run(nc, [arrays], core_ids=[0])
    return r.results[0]["out_0_dram"]
```

```python
from contextlib import ExitStack

import numpy as np

import concourse.bass as bass
from concourse import mybir

P = 128
D = 1024
FF = 2816
F32 = mybir.dt.float32
F32R = mybir.dt.float32r
U32 = mybir.dt.uint32
ALU = mybir.AluOpType
ACT = mybir.ActivationFunctionType
AX = mybir.AxisListType
EPS = 1e-6
BIG = 3e38
NEG = -1e30

NRAW = 3
NSPL = 7
LOOK = 4
HOLD = 3


class Lane:

    def __init__(self, sem):
        self.sem, self.n, self.ops, self.seen = sem, 0, [], {}

    def wait(self, *after):
        for t in after:
            if t is None:
                continue
            if isinstance(t, list):
                self.wait(*t)
                continue
            sem, v = t
            if self.seen.get(id(sem), 0) < v:
                self.seen[id(sem)] = v
                self.ops.append(lambda e, sem=sem, v=v: e.wait_ge(sem, v))

    def __call__(self, fn, *after):
        self.wait(*after)
        self.n += 1
        self.ops.append(lambda e: fn(e).then_inc(self.sem, 1))
        return (self.sem, self.n)

    def dma(self, dst, src, sem, count, *after):
        self.wait(*after)
        self.ops.append(lambda e: e.dma_start(dst, src).then_inc(sem, 16))
        return (sem, count)

    def run(self, e):
        for op in self.ops:
            op(e)


class Banks:

    def __init__(self, banks):
        self.banks, self.free, self.i = banks, [[] for _ in banks], 0

    def get(self):
        k = self.i % len(self.banks)
        self.i += 1
        waits, self.free[k] = self.free[k], None
        assert waits is not None
        return k, self.banks[k], waits

    def put(self, k, *tokens):
        self.free[k] = list(tokens)


def constants():
    i = np.arange(P)
    cols = {}
    cols["ident"] = np.eye(P)
    cols["tri"] = i[:, None] >= i[None, :]
    valid = i[:, None] < i[None, :]
    cols["mmin"] = np.concatenate([np.where(valid, BIG, 0.0), np.full((P, P), BIG), np.where(valid, BIG, 0.0)], 1)
    cols["mmax"] = -cols["mmin"]
    cols["caus"] = np.where(i[None, :] <= i[:, None], 0.0, NEG)
    lev = [np.eye(P)]
    for m in (1, 2, 4, 8, 16, 32, 64):
        same = (i[:, None] // (2 * m)) == (i[None, :] // (2 * m))
        lev.append(same & (i[:, None] % (2 * m) < m) & (i[None, :] % (2 * m) >= m))
    cols["lev"] = np.concatenate(lev, 1)
    dec = []
    for h in range(4):
        lg = float(np.log(np.float32(1.0 - 2.0 ** (-5.0 - h))))
        dt = i[None, :] - i[:, None]
        dec.append(np.where(dt >= 0, np.exp(lg * np.maximum(dt, 0)), 0.0) * P ** -0.5)
        dec.append(np.exp(lg * (dt + P)) * P ** -0.5)
    cols["dec"] = np.concatenate(dec, 1)
    for nm, dim, theta in (("a", 16, 500000.0), ("r", 128, 10000.0)):
        f32 = np.float32
        inv = f32(1.0) / (f32(theta) ** (np.arange(0, dim, 2, dtype=f32) / f32(dim)))
        ang = (np.arange(256, dtype=f32)[:, None] * inv[None, :]).astype(np.float64)
        for fn, f in (("cos", np.cos), ("sin", np.sin)):
            cols[fn + nm] = np.concatenate([f(ang[:P]), f(ang[P:])], 1)
    at, parts, n = {}, [], 0
    for k in [k for k in cols if k not in ("lev", "dec")] + ["lev", "dec"]:
        v = cols[k]
        v = np.asarray(v, np.float32)
        at[k] = (n, v.shape[1])
        n += v.shape[1]
        parts.append(v)
    return at, np.ascontiguousarray(np.concatenate(parts, 1))


def program(nc, T, const_at, out):
    ctx = ExitStack()
    with ctx:
        def sb(name, cols, dt=F32, parts=P, where=ctx):
            return where.enter_context(nc.sbuf_tensor(name, [parts, cols], dt))

        def sem(name):
            return ctx.enter_context(nc.semaphore(name))

        psum = [ctx.enter_context(nc.psum_tensor(f"ps{i}", [P, 512], F32)) for i in range(8)]
        acc = Banks(psum[:6])
        tb = Banks(psum[6:])
        pe, act, dve, pool, sp = (Lane(sem(n)) for n in ("s_pe", "s_act", "s_dve", "s_pool", "s_sp"))

        nconst = const_at["lev"][0]
        cst = sb("cst", nconst)
        adat = [sb(f"adat{i}", 512) for i in range(2)]
        adaacc = sb("adaacc", 512)
        modc = sb("modc", 48)
        scol = sb("scol", 16)
        s_ada = [sem(f"s_ada{i}") for i in range(2)]
        vcol = sb("vcol", 3 * P)
        h = sb("h", 2 * D)
        xh = sb("xh", 8 * 256, F32R)
        xl = sb("xl", 8 * 256, F32R)
        raw = [sb(f"raw{i}", 2048) for i in range(NRAW)]
        whi = [sb(f"whi{i}", 1024, F32R) for i in range(NSPL)]
        wlo = [sb(f"wlo{i}", 1024, F32R) for i in range(NSPL)]
        rows = [sb(f"row{i}", D) for i in range(2)]
        st = sb("st", 512)
        junk = sb("junk", 1024)
        xtmp = sb("xtmp", 1024)
        mhalf = sb("mhalf", 8)
        vin = sb("vin", P)
        vin2 = sb("vin2", 2 * P)
        hid = [sb(f"hid{i}", 1024) for i in range(2)]
        s_raw = [sem(f"s_raw{i}") for i in range(NRAW)]
        s_row = [sem(f"s_row{i}") for i in range(2)]
        s_first = sem("s_first")
        s_in = sem("s_in")
        s_in2 = sem("s_in2")
        s_out = sem("s_out")

        def C(name, a=0, n=None):
            o, w = const_at[name]
            n = w - a if n is None else n
            return cst[:, o + a:o + a + n]

        ident = C("ident")

        s_x = [sem(f"s_x{i}") for i in range(3)]
        act.dma(cst[:, 0:P], T["const"][:, 0:P], s_in, 0)
        act.dma(vin[0:96, 0:P], T["norm_g"].rearrange("l n (b p) -> (l n b) p", p=P), s_in, 0)
        for i, n in enumerate((0, 512)):
            sp.dma(h[:, n:n + 512], T["x"][0, 0:P, n:n + 512], s_x[i], 0)
        t_in = (s_in, 32)
        t_x = [[[t_in, (s_x[0], 16)], [t_in, (s_x[1], 16)]], [(s_x[2], 16)] * 2]
        n_in = 0
        more = []
        VR = {}
        r = 0
        for nm, src in (("n1", T["norm1_w_2"]), ("n2", T["norm2_w_2"]), ("ba", T["b_ada_2"]),
                        ("bg", T["gla_b_gate"][0]), ("cb", T["conv_dw_b"][0]),
                        ("lg", T["conv_ln_g"][0]), ("lb", T["conv_ln_b"][0])):
            k = src.shape[0] // P
            more.append((vin2[r:r + k, 0:P], src.rearrange("(b p) -> b p", p=P)))
            VR[nm] = P + r
            r += k
        more.append((vin2[0:124, P:2 * P], T["conv_dw_w"][0].rearrange("k (b p) -> (k b) p", p=P)))
        VR["cw"] = 2 * P
        more.append((cst[:, P:nconst], T["const"][:, P:nconst]))
        more.append((scol[:, 0:8], T["c_2"].rearrange("a (p k) -> (a p) k", k=8)))
        t_in2 = (s_in2, 16 * len(more))
        nvec = {0: 96, 1: r, 2: 124}

        def vectors(js, after):
            k0, bank, w0 = tb.get()

            def f(e):
                for j in js:
                    src = vin[:, 0:P] if j == 0 else vin2[:, (j - 1) * P:j * P]
                    last = e.transpose(bank[:, j * P:j * P + nvec[j]], src[0:nvec[j], :], ident[0:nvec[j], 0:nvec[j]])
                return last
            t = pe(f, after, w0)

            def f2(e):
                for j in js:
                    last = e.tensor_copy(vcol[:, j * P:j * P + nvec[j]], bank[:, j * P:j * P + nvec[j]])
                return last
            t = dve(f2, t)
            tb.put(k0, t)
            return t

        t_vec = vectors([0], t_in)
        t_vec2 = []

        def second_vectors():
            t_vec2.append(vectors([1, 2], [t_in2, t_in]))
            t_vec2.append(act(lambda e: e.activation(scol[:, 8:16], scol[:, 0:8], ACT.Silu), t_in2))

        plan = []

        def plan_cols(w, c0, n, nk):
            for k in range(0, nk, 4):
                m = min(4, nk - k)
                plan.append((w[k * P:(k + m) * P, c0:c0 + n].rearrange("(k p) n -> p k n", p=P), m, n))

        def plan_ffn(w_in, w_out):
            for c in range(11):
                for k in (0, 4):
                    if len(w_in) == 1:
                        v = w_in[0][k * P:(k + 4) * P, :].rearrange("(k p) (a n) -> p k a n", p=P, a=2)
                        plan.append((v[:, :, :, c * 256:(c + 1) * 256], 4, 512))
                    else:
                        plan.append(([w[k * P:(k + 4) * P, c * 256:(c + 1) * 256]
                                      .rearrange("(k p) n -> p k n", p=P) for w in w_in], 4, 512))
            for k in range(0, 22, 4):
                m = min(4, 22 - k)
                for n in range(2):
                    plan.append((w_out[k * P:(k + m) * P, n * 512:(n + 1) * 512]
                                 .rearrange("(k p) n -> p k n", p=P), m, 512))

        bg = []

        def pump(n):
            while bg and n > 0:
                bg.pop(0)()
                n -= 1

        unit = {"load": 0, "split": 0, "use": 0}
        t_load, t_used, t_sub, subs = [], {}, [], []
        nraw_sem = [0] * NRAW
        sub_at = {}

        def cut_subs():
            for u, (_, m, n) in enumerate(plan):
                sub_at[u] = len(subs)
                for k in range(0, m, 2):
                    subs.append((u, k, min(2, m - k), n))

        def load_unit():
            i = unit["load"]
            unit["load"] += 1
            s = i % NRAW
            src, m, n = plan[i]
            after = t_sub[sub_at[i - NRAW + 1] - 1] if i >= NRAW else None
            dst = raw[s][:, 0:m * n]
            if i == 0:
                dst4 = dst.rearrange("p (k a n) -> p k a n", k=m, a=2)
                for k, sm in ((0, s_raw[s]), (2, s_first)):
                    for a in range(2):
                        sp.dma(dst4[:, k:k + 2, a, :], src[:, k:k + 2, a, :], sm, 0)
                nraw_sem[s] += 32
                t_load.append([(s_raw[s], 32), (s_first, 32)])
                return
            if isinstance(src, list):
                dst = dst.rearrange("p (k a n) -> p k a n", k=m, a=2)
                for a in range(2):
                    nraw_sem[s] += 16
                    sp.dma(dst[:, :, a, :], src[a], s_raw[s], 0, after)
            elif len(src.shape) == 4:
                dst4 = dst.rearrange("p (k a n) -> p k a n", k=m, a=2)
                for a in range(2):
                    nraw_sem[s] += 16
                    sp.dma(dst4[:, :, a, :], src[:, :, a, :], s_raw[s], 0, after)
            else:
                nraw_sem[s] += 16
                sp.dma(dst.rearrange("p (k n) -> p k n", k=m), src, s_raw[s], 0, after)
            t_load.append([(s_raw[s], nraw_sem[s])] * 2)
            if i == 3:
                for d, v in more:
                    sp.dma(d, v, s_in2, 0)
            if i >= 8:
                ada_load()

        def split_sub():
            j = unit["split"]
            unit["split"] += 1
            u, k, m, n = subs[j]
            if unit["load"] <= u:
                load_unit()
            r = raw[u % NRAW][:, k * n:(k + m) * n]
            a, b = whi[j % NSPL], wlo[j % NSPL]
            used = t_used[j - NSPL] if j >= NSPL else None
            ta = act(lambda e: e.activation(a[:, 0:m * n], r, ACT.Copy), t_load[u][k // 2], used)
            tl = dve(lambda e: e.tensor_tensor(b[:, 0:m * n], r, a[:, 0:m * n].bitcast(F32), ALU.subtract),
                     ta, t_load[u][k // 2], used)
            t_sub.append([ta, tl])
            while unit["load"] < min(len(plan), u + NRAW):
                load_unit()
            if j + 1 == len(subs) or subs[j + 1][0] != u:
                if unit["load"] < min(len(plan), u + NRAW + 1):
                    load_unit()

        def next_sub(ahead=LOOK, bgwork=True):
            j = unit["use"]
            unit["use"] += 1
            while unit["split"] < min(len(subs), j + ahead + 1) and (
                    unit["split"] < NSPL or unit["split"] - NSPL in t_used):
                split_sub()
            assert unit["split"] > j
            if j == 6:
                second_vectors()
            for item in [q for q in soon if q[0] <= j]:
                soon.remove(item)
                item[1]()
            if bgwork:
                pump(PUMP[0])
            if "due" in ada and not ada["in"] and unit["load"] > ada["last"]:
                ada_reduce()
            return j

        soon = []

        def later(n, fn):
            soon.append((unit["use"] + n, fn))

        PUMP = [0]

        def mms(e, ps, j, XH, XL, kb0, tok, first, final, which):
            _, _, m, n = subs[j]
            for k in range(m):
                a = XH[:, (kb0 + k) * 256 + tok * P:(kb0 + k) * 256 + (tok + 1) * P]
                b = XL[:, (kb0 + k) * 256 + tok * P:(kb0 + k) * 256 + (tok + 1) * P]
                wh = whi[j % NSPL][:, k * n:(k + 1) * n]
                wl = wlo[j % NSPL][:, k * n:(k + 1) * n]
                if which != 1:
                    e.matmul(ps[:, 0:n], a, wh, start=first and k == 0, stop=False)
                    last = e.matmul(ps[:, 0:n], a, wl, start=False, stop=False)
                if which != 0:
                    last = e.matmul(ps[:, 0:n], b, wh, start=False, stop=final and k == m - 1)
            return last

        def ahead(n):
            while unit["split"] < min(len(subs), unit["use"] + n):
                split_sub()

        def part(j, XH, XL, ready, kb0, nk, tok, ps, wait):
            m = subs[j][2]
            rd = [ready[q][tok] for q in range(kb0, kb0 + m)]
            do = lambda which: lambda e: mms(e, ps, j, XH, XL, kb0, tok, kb0 == 0, kb0 + m == nk, which)
            if all(pe.seen.get(id(r[1][0]), 0) >= r[1][1] for r in rd):
                return pe(do(2), t_sub[j], rd, wait)
            pe(do(0), t_sub[j], [r[0] for r in rd], wait)
            return pe(do(1), [r[1] for r in rd])

        def linear(XH, XL, ready, nk, nchunk, evac, late=None, whole=False):
            for c in range(nchunk):
                bk = [acc.get() for _ in range(2)]
                tok_t = [None, None]
                if late and c == 0:
                    js = []
                    for k in range(0, nk, 2):
                        js.append(next_sub(0, False))
                        if k + 2 == nk and not whole:
                            then = late()
                        tok_t[0] = part(js[-1], XH, XL, ready, k, nk, 0, bk[0][1], bk[0][2])
                    if whole:
                        then = late()
                    for _ in range(2):
                        if unit["split"] < len(subs) and (unit["split"] < NSPL or unit["split"] - NSPL in t_used):
                            split_sub()
                    for i, k in enumerate(range(0, nk, 2)):
                        tok_t[1] = part(js[i], XH, XL, ready, k, nk, 1, bk[1][1], bk[1][2])
                        t_used[js[i]] = tok_t[1]
                        if i == 0:
                            acc.put(bk[0][0], *evac(c, 0, bk[0][1], tok_t[0]))
                        if i == 1 and then:
                            then()
                        while unit["split"] < js[i] + NSPL - 2 and unit["split"] < len(subs) and (
                                unit["split"] - NSPL in t_used):
                            split_sub()
                    acc.put(bk[1][0], *evac(c, 1, bk[1][1], tok_t[1]))
                    continue
                k = 0
                while k < nk:
                    j = next_sub()
                    for tok in range(2):
                        tok_t[tok] = part(j, XH, XL, ready, k, nk, tok, bk[tok][1], bk[tok][2])
                    t_used[j] = tok_t[1]
                    k += subs[j][2]
                for tok in range(2):
                    acc.put(bk[tok][0], *evac(c, tok, bk[tok][1], tok_t[tok]))

        ones = sb("ones", P)
        t_ones = dve(lambda e: e.memset(ones[:, :], 1.0))

        st_i = [0]

        def col(n=1):
            if st_i[0] + n > 512:
                st_i[0] = 0
            o = st_i[0]
            st_i[0] += n
            return st[:, o:o + n]

        t_mh = pool(lambda e: e.memset(mhalf[:, :], -0.5))

        def rpow(v, n, mult, *after, factor=1.0):
            w, r = col(n), col(n)
            f = factor ** -2
            t = pool(lambda e: e.tensor_scalar(w, v, mult * f, EPS * f, ALU.mult, ALU.add), *after)
            return r, pool(lambda e: e.tensor_tensor(r, w, mhalf[:, 0:n], ALU.pow), t, t_mh)

        def rstd(ss, count, *after, factor=1.0):
            v = col()
            t = pool(lambda e: e.tensor_tensor(v, ss[:, 0:1], ss[:, 1:2], ALU.add), *after)
            return rpow(v, 1, 1.0 / count, t, factor=factor)

        row_n = [0]
        row_cnt = [0, 0]
        row_free = [None, None]

        def row_load(src, n):
            s = row_n[0] % 2
            row_n[0] += 1
            row_cnt[s] += 16
            cnt = row_cnt[s]
            sp.dma(rows[s][:, 0:n], src.rearrange("(a n) -> a n", a=1).to_broadcast([P, n]), s_row[s], 0,
                   row_free[s])
            return s, rows[s], (s_row[s], cnt)

        def transposes(src, ready, ps, dst_cols, waits):
            def f(e):
                for a, c in zip(src, dst_cols):
                    last = e.transpose(ps[:, c:c + P], a, ident)
                return last
            return pe(f, ready, waits)

        def snap():
            return [(q.sem, q.n) for q in (pe, act, dve, pool)]

        xfree = [None]
        xtf = [None, None]

        def xview(z, q, tok):
            return z[:, q * 1024:(q + 1) * 1024].rearrange("p (k n) -> p k n", k=4)[:, :, tok * P:(tok + 1) * P]

        def bcol(z):
            return z.rearrange("p (k o) -> p k o", o=1).to_broadcast([P, 4, P])

        def x_block(tok, src, ready, out, gain=None, shift=None, tg=None):
            for q in range(2):
                k0, ps, w0 = tb.get()
                tiles = [src[:, (4 * q + j) * P:(4 * q + j + 1) * P] for j in range(4)]
                t = transposes(tiles, ready[q], ps, [0, P, 2 * P, 3 * P], w0)
                v = ps[:, :].rearrange("p (k n) -> p k n", k=4)
                ho, lo = xview(xh, q, tok), xview(xl, q, tok)
                if gain is not None:
                    g = bcol(gain[:, 4 * q:4 * q + 4])
                    x = xtmp[:, q * 512:(q + 1) * 512].rearrange("p (k n) -> p k n", k=4)
                    if shift is None:
                        t = dve(lambda e, x=x, v=v, g=g: e.tensor_tensor(x, v, g, ALU.mult), t, xtf[q], tg, t_vec)
                    else:
                        t = [dve(lambda e, x=x, v=v, k=k, q=q: e.tensor_scalar(
                            x[:, k, :], v[:, k, :], gain[:, 4 * q + k:4 * q + k + 1],
                            shift[:, 4 * q + k:4 * q + k + 1], ALU.mult, ALU.add), t, xtf[q], tg)
                            for k in range(4)][-1]
                    tb.put(k0, t)
                    v = x
                a = act(lambda e, ho=ho, v=v: e.activation(ho, v, ACT.Copy), t, xfree[0])
                b = dve(lambda e, ho=ho, lo=lo, v=v: e.tensor_tensor(lo, v, ho.bitcast(F32), ALU.subtract), a, t,
                        xfree[0])
                if gain is not None:
                    xtf[q] = [a, b]
                else:
                    tb.put(k0, b)
                for k in range(4 * q, 4 * q + 4):
                    out[k][tok] = [a, b]

        junk_t = [None, None]
        junk_n = [0]

        def sumsq(src, o, *after):
            k = junk_n[0] % 2
            junk_n[0] += 1
            w = src.shape[1]
            junk_t[k] = act(lambda e: e.activation(junk[:, k * 512:k * 512 + w], src, ACT.Square, accum_out=o),
                            junk_t[k], *after)
            return junk_t[k]

        def h_stats(tok, ready):
            ss = col(2)
            ts = [sumsq(h[:, tok * D + n * 512:tok * D + (n + 1) * 512], ss[:, n:n + 1], ready[n]) for n in range(2)]
            return rstd(ss, D, ts)

        def ffn_body(gT_h, gT_l, ready, rs, late):
            gready = [None] * 22
            pend = []
            hid_free = [snap(), snap()]

            def flush():
                c, ths = pend.pop(0)
                hb = hid[c % 2]
                k0, ps, w0 = tb.get()
                src = [hb[:, tok * 512 + j * P:tok * 512 + (j + 1) * P] for j in range(2) for tok in range(2)]
                t = transposes(src, ths, ps, [0, P, 2 * P, 3 * P], w0)
                hid_free[c % 2] = t
                sl = slice(c * 512, (c + 1) * 512)
                a = act(lambda e: e.activation(gT_h[:, sl], ps[:, :], ACT.Copy), t, gfree[0])
                b = dve(lambda e: e.tensor_tensor(gT_l[:, sl], ps[:, :], gT_h[:, sl].bitcast(F32), ALU.subtract),
                        a, gfree[0])
                tb.put(k0, b)
                gready[2 * c] = gready[2 * c + 1] = [[a, b]] * 2

            def evac(c, tok, ps, t):
                hb = hid[c % 2]
                s1 = hb[:, tok * 512 + 256:tok * 512 + 512]
                s2 = hb[:, tok * 512:tok * 512 + 256]
                sc, tsc = rs[tok] if rs else (1.0, None)
                a = act(lambda e: e.activation(s1, ps[:, 0:256], ACT.Silu, scale=sc), t, tsc, hid_free[c % 2])
                b = dve(lambda e: e.scalar_tensor_tensor(s2, ps[:, 256:512], sc, s1, ALU.mult, ALU.mult),
                        a, t, tsc)
                if tok == 0:
                    if pend:
                        flush()
                    pend.append((c, [b]))
                else:
                    pend[-1][1].append(b)
                return [a, b]

            linear(xh, xl, ready, 8, 11, evac, late, rs is None)
            xfree[0] = (pe.sem, pe.n)
            later(2, flush)
            return gready

        gfree = [None]

        def down(XH, XL, ready, nk, late=None):
            bk = [[acc.get() for _ in range(2)] for _ in range(2)]
            tt = [[None, None], [None, None]]
            seq = []
            for k in range(0, nk, 4):
                for n in range(2):
                    for q in range(k, min(k + 4, nk), 2):
                        seq.append((q, n))
            held = []

            def one(j, q, n, tok):
                tt[tok][n] = part(j, XH, XL, ready, q, nk, tok, bk[tok][n][1], bk[tok][n][2])
            for i, (q, n) in enumerate(seq):
                j = next_sub()
                one(j, q, n, 0)
                held.append((j, q, n))
                if late and i == HOLD - 1:
                    late()
                if i < len(seq) - HOLD and not late or len(held) > HOLD:
                    j, q, n = held.pop(0)
                    one(j, q, n, 1)
                    t_used[j] = tt[1][n]
            for j, q, n in held:
                one(j, q, n, 1)
                t_used[j] = tt[1][n]
            gfree[0] = (pe.sem, pe.n)
            return [[(bk[tok][n][1], bk[tok][n][0], tt[tok][n]) for n in range(2)] for tok in range(2)]

        def residual(res, factor, gain):
            s, row, trow = gain

            def run(tok):
                ss = col(2)
                ts = [sumsq(res[tok][n][0][:, :], ss[:, n:n + 1], res[tok][n][2]) for n in range(2)]
                r1, tr = rstd(ss, D, ts, factor=factor)
                tf = [(dve.sem, dve.n), (act.sem, act.n - 2)]
                ready, tx = [], []
                for n in range(2):
                    ps, k0, t = res[tok][n]
                    tx.append(dve(lambda e, ps=ps, n=n: e.tensor_tensor(
                        hid[tok][:, n * 512:(n + 1) * 512], ps[:, :], row[:, n * 512:(n + 1) * 512], ALU.mult),
                        trow, t, ts[n], tf))
                    acc.put(k0, ts[n], tx[n])
                row_free[s] = tx[1]
                for n in range(2):
                    hs = h[:, tok * D + n * 512:tok * D + (n + 1) * 512]
                    ready.append(dve(lambda e, n=n, hs=hs: e.scalar_tensor_tensor(
                        hs, hid[tok][:, n * 512:(n + 1) * 512], r1, hs, ALU.mult, ALU.add), tr, tx[n], hfree[tok]))
                return ready
            return run

        hfree = [None, None]

        def enter(prev, gcol):
            ready = [[None, None] for _ in range(8)]
            rs = [None, None]

            def prep(tok, hr):
                x_block(tok, h[:, tok * D:(tok + 1) * D], hr, ready, vcol[:, gcol:gcol + 8])

            def stats(tok, hr):
                rs[tok] = h_stats(tok, hr)
                hfree[tok] = [(pe.sem, pe.n), (act.sem, act.n)]

            def late():
                prep(1, r1)
                if not rs[0]:
                    stats(0, r0)
                return lambda: stats(1, r1)
            r0 = prev(0)
            prep(0, r0)
            if unit["split"]:
                ahead(4)
            r1 = prev(1)
            if unit["split"]:
                stats(0, r0)
            return ready, rs, late

        def ffn_stage(prev, gcol, gain_src):
            ready, rs, late = enter(prev, gcol)
            gain = row_load(gain_src, D)
            with ExitStack() as inner:
                gh = sb(f"gh{gcol}", 22 * 256, F32R, where=inner)
                gl = sb(f"gl{gcol}", 22 * 256, F32R, where=inner)
                gready = ffn_body(gh, gl, ready, rs, late)
                res = down(gh, gl, gready, 22)
            return residual(res, 0.5, gain)

        def to_T(src, ready, dst, nblk, scale, eng, parts=P, after=None):
            ts = []
            for b0 in range(0, nblk, 2):
                nb = min(2, nblk - b0)
                k0, ps, w0 = tb.get()
                tiles, cs = [], []
                for j in range(nb):
                    for tok in range(2):
                        tiles.append(src(tok)[:, (b0 + j) * P:(b0 + j + 1) * P])
                        cs.append(j * 256 + tok * P)
                t = transposes(tiles, ready, ps, cs, w0)
                v = ps[:, 0:nb * 256].rearrange("p (b n) -> p b n", b=nb)
                o = dst[:, b0:b0 + nb, :]
                if eng is act:
                    t = act(lambda e, o=o, v=v: e.activation(o, v, ACT.Copy, scale=scale), t, after)
                else:
                    t = dve(lambda e, o=o, v=v: e.tensor_scalar(o, v, scale, None, ALU.mult), t, after)
                tb.put(k0, t)
                ts += [t] * nb
            return ts

        def split_to_x(src, sl, ready):
            a = act(lambda e: e.activation(xh[:, sl], src, ACT.Copy), ready, xfree[0])
            b = dve(lambda e: e.tensor_tensor(xl[:, sl], src, xh[:, sl].bitcast(F32), ALU.subtract), a, ready)
            return [a, b]

        def hybrid_stage(prev):
            ready, rs, late = enter(prev, 2 * 8)
            gain = row_load(T["norm_g"][0, 3], D)
            with ExitStack() as inner:
                cx = sb("cx", 4 * 286, where=inner)
                Y = sb("Y", 4 * 256, where=inner)
                SQ = sb("SQ", 4 * 256, where=inner)
                qt = sb("qt", 1024, where=inner)
                kt = sb("kt", 1024, where=inner)
                vt = sb("vt", 1024, where=inner)
                qT = sb("qT", 1024, where=inner)
                kT = sb("kT", 1024, where=inner)
                eb = [sb(f"eb{i}", 384, where=inner) for i in range(4)]
                mb = [sb(f"mb{i}", 384, where=inner) for i in range(4)]
                wb = [sb(f"wb{i}", 384, where=inner) for i in range(4)]
                pt = [sb(f"pt{i}", 256, where=inner) for i in range(2)]
                rb = sb("rb", 512, where=inner)
                cx3 = cx[:, :].rearrange("p (b n) -> p b n", b=4)
                sg, ct = hid[0], hid[1]
                t_free = snap()
                t_pad = dve(lambda e: e.memset(cx3[:, :, 0:30], 0.0), t_free)
                st_tok = {}

                def evac(c, tok, ps, t):
                    sc, tsc = rs[tok]
                    o = slice(tok * 512, (tok + 1) * 512)
                    if c == 0:
                        a = act(lambda e: e.activation(sg[:, o], ps[:, :], ACT.Sigmoid, scale=sc), t, tsc,
                                (pe.sem, pe.n), (dve.sem, dve.n))
                        st_tok["g", tok] = a
                        return [a]
                    if c == 1:
                        a = dve(lambda e: e.scalar_tensor_tensor(ct[:, o], ps[:, :], sc, sg[:, o], ALU.mult, ALU.mult),
                                t, tsc, st_tok["g", tok])
                        st_tok["c", tok] = a
                        return [a]
                    dst = {2: qt, 3: kt, 4: vt}[c]
                    a = act(lambda e: e.activation(dst[:, o], ps[:, :], ACT.Copy, scale=sc), t, tsc, t_pad)
                    st_tok[c, tok] = a
                    return [a]

                def after_u():
                    tc = to_T(lambda tok: ct[:, tok * 512:(tok + 1) * 512], [st_tok["c", 0], st_tok["c", 1]],
                              cx3[:, :, 30:286], 4, 1.0, act, after=t_pad)

                    def pool_tap(k):
                        def f():
                            b = 3
                            y = Y[:, b * 256:(b + 1) * 256]
                            x = cx[:, b * 286 + k:b * 286 + k + 256]
                            w = vcol[:, VR["cw"] + k * 4 + b:VR["cw"] + k * 4 + b + 1]
                            if k == 0:
                                bias = vcol[:, VR["cb"] + b:VR["cb"] + b + 1]
                                ty[b] = pool(lambda e: e.tensor_scalar(y, x, w, bias, ALU.mult, ALU.add),
                                             tc[b], t_pad, t_vec2, t_free)
                            else:
                                p = pt[k % 2][:, :]
                                t = pool(lambda e: e.tensor_tensor(p, x, w.to_broadcast([P, 256]), ALU.mult),
                                         ptf[k % 2], t_free)
                                ty[b] = pool(lambda e: e.tensor_tensor(y, y, p, ALU.add), ty[b], t)
                                ptf[k % 2] = ty[b]
                        return f
                    ptf = [None, None]
                    NT = 21

                    def tap(b, k):
                        def f():
                            y = Y[:, b * 256:(b + 1) * 256]
                            x = cx[:, b * 286 + k:b * 286 + k + 256]
                            w = vcol[:, VR["cw"] + k * 4 + b:VR["cw"] + k * 4 + b + 1]
                            if k == 0:
                                bias = vcol[:, VR["cb"] + b:VR["cb"] + b + 1]
                                ty[b] = dve(lambda e: e.tensor_scalar(y, x, w, bias, ALU.mult, ALU.add),
                                            tc[b], t_pad, t_vec2)
                            else:
                                ty[b] = dve(lambda e: e.scalar_tensor_tensor(y, x, w, y, ALU.mult, ALU.add), ty[b])
                        return f
                    def more_taps(k):
                        y = SQ[:, 512:768]
                        x = cx[:, 2 * 286 + k:2 * 286 + k + 256]
                        w = vcol[:, VR["cw"] + k * 4 + 2:VR["cw"] + k * 4 + 3]
                        if k == NT:
                            return pool(lambda e: e.tensor_tensor(y, x, w.to_broadcast([P, 256]), ALU.mult),
                                        tc[2], t_free)
                        p = pt[k % 2][:, :]
                        t = pool(lambda e: e.tensor_tensor(p, x, w.to_broadcast([P, 256]), ALU.mult), ptf[k % 2])
                        ptf[k % 2] = pool(lambda e: e.tensor_tensor(y, y, p, ALU.add), t)
                        return ptf[k % 2]

                    def join():
                        ty[2] = dve(lambda e: e.tensor_tensor(Y[:, 512:768], Y[:, 512:768], SQ[:, 512:768],
                                                              ALU.add), ty[2], tm)
                    for k in range(31):
                        pool_tap(k)()
                        for b in range(3):
                            if b < 2 or k < NT:
                                bg.append(tap(b, k))
                    for k in range(NT, 31):
                        tm = more_taps(k)
                    joins.append(join)

                v4 = lambda z: z[:, :].rearrange("p (b n) -> p b n", b=4)
                tq, tk, ty, joins = [], [], [None] * 4, []
                PUMP[0] = 5
                linear(xh, xl, ready, 8, 2, evac, late)
                later(1, after_u)
                linear(xh, xl, ready, 8, 1, lambda c, tok, ps, t: evac(2, tok, ps, t))
                later(1, lambda: tq.extend(to_T(lambda tok: qt[:, tok * 512:(tok + 1) * 512],
                                                [st_tok[2, 0], st_tok[2, 1]], v4(qT), 4, 0.125, act)))
                linear(xh, xl, ready, 8, 1, lambda c, tok, ps, t: evac(3, tok, ps, t))
                later(1, lambda: tk.extend(to_T(lambda tok: kt[:, tok * 512:(tok + 1) * 512],
                                                [st_tok[3, 0], st_tok[3, 1]], v4(kT), 4, 1.0, act)))

                Z = {}
                wfree = [None] * 4
                ld = {}
                wd = {}

                def scores(hd):
                    p0, b = 64 * (hd % 2), hd // 2
                    k0, ps, w0 = acc.get()

                    def f(e):
                        q, k = qT[p0:p0 + 64, b * 256:(b + 1) * 256], kT[p0:p0 + 64, b * 256:(b + 1) * 256]
                        e.matmul(ps[:, 0:256], k[:, 0:P], q, start=True, stop=True)
                        return e.matmul(ps[:, 256:384], k[:, P:256], q[:, P:256], start=False, stop=True,
                                        skip_group_check=True)
                    t = pe(f, tq[b], tk[b], w0)
                    z, s = ps[:, 0:384], hd % 4
                    E, M = eb[s][:, :], mb[s][:, :]
                    t1 = act(lambda e: e.activation(E, z, ACT.Abs), t, wfree[s], t_free)
                    t4 = act(lambda e: e.activation(M, z, ACT.Relu), t, wfree[s], t_free)
                    Z[hd] = (k0, ps)
                    ld[hd] = [t1, t4]

                def exps(hd):
                    s = hd % 4
                    E = eb[s][:, :]
                    ld[hd][0] = act(lambda e: e.activation(E, E, ACT.Exp, scale=-1.0), ld[hd][0])

                def logs(hd):
                    s = hd % 4
                    E, M = eb[s][:, :], mb[s][:, :]
                    t2, t4 = ld[hd]
                    t3 = act(lambda e: e.activation(E, E, ACT.Ln, bias=1.0), t2)
                    t5 = dve(lambda e: e.scalar_tensor_tensor(M, M, -1.0, E, ALU.mult, ALU.subtract), t3, t4)
                    t6 = dve(lambda e: e.tensor_tensor(M, M, C("mmax"), ALU.max), t5)
                    ld[hd] = t6

                def weights(hd):
                    k0, ps = Z[hd]
                    s = hd % 4
                    M, W = mb[s], wb[s][:, :]

                    def f(e):
                        e.matmul(ps[:, 0:384], C("tri"), M[:, 0:384], start=False, stop=True, skip_group_check=True)
                        return e.matmul(ps[:, P:256], ones[:, :], M[:, 256:384], start=False, stop=True,
                                        skip_group_check=True)
                    t = pe(f, ld[hd], t_ones)
                    t1 = act(lambda e: e.activation(W, ps[:, 0:384], ACT.Exp), t, wfree[s])
                    acc.put(k0, t1)
                    wd[hd] = dve(lambda e: e.tensor_tensor(W, W, C("mmin"), ALU.min), t1)

                pv = {}

                def values(hd):
                    s, p0, b = hd % 4, 64 * (hd % 2), hd // 2
                    if hd % 2 == 0:
                        pv[b] = acc.get()
                    k0, ps, w0 = pv[b]

                    def f(e):
                        o = ps[p0:p0 + 64, 0:256]
                        e.matmul(o, vt[:, hd * 64:(hd + 1) * 64], wb[s][:, 0:256], start=True, stop=True)
                        return e.matmul(ps[p0:p0 + 64, P:256], vt[:, 512 + hd * 64:512 + (hd + 1) * 64],
                                        wb[s][:, 256:384], start=False, stop=True, skip_group_check=True)
                    wfree[s] = pe(f, wd[hd], tv, w0)
                    if hd % 2 == 1:
                        xr = split_to_x(ps[:, 0:256], slice(b * 256, (b + 1) * 256), wfree[s])
                        acc.put(k0, *xr)
                        return xr

                ln = {}

                def opened(g):
                    for hd in (2 * g, 2 * g + 1):
                        scores(hd)
                    for hd in (2 * g, 2 * g + 1):
                        exps(hd)
                y4 = lambda b: Y[:, b * 256:(b + 1) * 256]
                q4 = lambda b: SQ[:, b * 256:(b + 1) * 256]

                def total(z, t):
                    k0, ps, w0 = acc.get()

                    def f(e):
                        for b in range(4):
                            last = e.matmul(ps[:, 0:256], ones[:, :], z(b), start=b == 0, stop=b == 3)
                        return last
                    return k0, ps, pe(f, t, t_ones, w0)

                def centre():
                    pump(1000)
                    joins[0]()
                    k0, ps, t = total(y4, ty)
                    ln["q"] = []
                    for b in range(4):
                        t1 = dve(lambda e, b=b: e.scalar_tensor_tensor(y4(b), ps[:, 0:256], -1.0 / 512, y4(b),
                                                                       ALU.mult, ALU.add), t, ty[b])
                        ln["q"].append(act(lambda e, b=b: e.activation(q4(b), y4(b), ACT.Square), t1, t_pad))
                    acc.put(k0, t1)

                def scale():
                    k0, ps, t = total(q4, ln["q"])
                    t = dve(lambda e: e.tensor_scalar(rb[:, 0:256], ps[:, 0:256], 1.0 / 512, EPS, ALU.mult, ALU.add),
                            t)
                    acc.put(k0, t)
                    t = act(lambda e: e.activation(rb[:, 256:512], rb[:, 0:256], ACT.Sqrt), t)
                    t = dve(lambda e: e.reciprocal(rb[:, 0:256], rb[:, 256:512]), t)
                    ln["y"] = [dve(lambda e, b=b: e.tensor_tensor(y4(b), y4(b), rb[:, 0:256], ALU.mult), t)
                               for b in range(4)]

                def finish():
                    for b in range(4):
                        g = vcol[:, VR["lg"] + b:VR["lg"] + b + 1]
                        bb = vcol[:, VR["lb"] + b:VR["lb"] + b + 1]
                        t2 = act(lambda e, b=b, g=g, bb=bb: e.activation(q4(b), y4(b), ACT.Silu, scale=g, bias=bb),
                                 ln["y"][b])
                        r = split_to_x(q4(b), slice((4 + b) * 256, (5 + b) * 256), t2)
                        xr[4 + b] = [r, r]

                later(2, lambda: opened(0))
                later(3, lambda: [logs(0), logs(1)])
                linear(xh, xl, ready, 8, 1, lambda c, tok, ps, t: evac(4, tok, ps, t))
                xfree[0] = (pe.sem, pe.n)
                tv = [st_tok[4, 0], st_tok[4, 1]]
                xr = [None] * 8
                for g in range(6):
                    if g:
                        if g < 4:
                            opened(g)
                        if 1 <= g < 5:
                            for hd in (2 * g - 2, 2 * g - 1):
                                weights(hd)
                        if g < 4:
                            for hd in (2 * g, 2 * g + 1):
                                logs(hd)
                    if 2 <= g < 6:
                        for hd in (2 * g - 4, 2 * g - 3):
                            r = values(hd)
                        xr[g - 2] = [r, r]
                    pump(6)
                    if g == 4:
                        centre()
                    if g == 5:
                        scale()
                later(1, finish)
                PUMP[0] = 0
                res = down(xh, xl, xr, 8)
                xfree[0] = (pe.sem, pe.n)
            return residual(res, 1.0, gain)

        def gla_stage(prev):
            ready, rs, late = enter(prev, (6 + 2) * 8)
            gain = row_load(T["norm_g"][1, 3], D)
            grow = row_load(T["gla_norm_g"][0], 256)
            with ExitStack() as inner:
                B = sb("gB", 1024, where=inner)
                QT = sb("gQT", 1024, where=inner)
                KT = sb("gKT", 1024, where=inner)
                X = [sb(f"gX{i}", 1024, where=inner) for i in range(4)]
                E1, G = X[:2]
                S = sb("gS", 1024, where=inner)
                OFF = sb("gOFF", 512, where=inner)
                vt = sb("gv", 2048, where=inner)
                sr = sb("gr", 2048, where=inner)
                levm = sb("glev", 8 * P, where=inner)
                lr = sb("glr", 32, where=inner)
                lrT = sb("glrT", 256, where=inner, parts=16)
                wg = sb("gwg", 512, where=inner, parts=16)
                qt, kt = hid[0], hid[1]
                t_free = snap()
                s_wg = sem("s_wg")
                sp.dma(wg[:, :], T["gla_w_gate"][0], s_wg, 0, t_free)
                t_S = dve(lambda e: e.memset(S[:, :], 0.0), t_free)
                got = {}

                def evac(c, tok, ps, t):
                    sc, tsc = rs[tok]
                    o = slice(tok * 512, (tok + 1) * 512)
                    if c == 0:
                        a = act(lambda e: e.activation(lr[:, tok * 16:tok * 16 + 16], ps[:, 0:16], ACT.Copy,
                                                       scale=sc), t, tsc, t_free)
                    elif c in (1, 2):
                        d = (qt, kt)[c - 1]
                        a = act(lambda e: e.activation(d[:, o], ps[:, :], ACT.Copy, scale=sc), t, tsc, t_free)
                    elif c in (3, 4):
                        d = vt[:, tok * D + (c - 3) * 512:tok * D + (c - 2) * 512]
                        a = act(lambda e: e.activation(d, ps[:, :], ACT.Copy, scale=sc), t, tsc, t_free)
                    else:
                        d = sr[:, tok * D + (c - 5) * 512:tok * D + (c - 4) * 512]
                        a = act(lambda e: e.activation(d, ps[:, :], ACT.Silu, scale=sc), t, tsc, t_free)
                    got[c, tok] = a
                    return [a]

                v3 = lambda z: z[:, :].rearrange("p (b n) -> p b n", b=4)
                tQ, tK, tB, t_lr = [], [], [], []
                linear(xh, xl, ready, 8, 1, lambda c, *a: evac(1, *a), late)
                later(1, lambda: tQ.extend(to_T(lambda tok: qt[:, tok * 512:(tok + 1) * 512],
                                                [got[1, 0], got[1, 1]], v3(QT), 4, P ** -0.5, dve, after=t_free)))
                linear(xh, xl, ready, 8, 1, evac)

                def low():
                    k0, ps, w0 = tb.get()

                    def f(e):
                        for tok in range(2):
                            last = e.transpose(ps[0:16, tok * P:(tok + 1) * P], lr[:, tok * 16:tok * 16 + 16],
                                               ident)
                        return last
                    t = pe(f, got[0, 0], got[0, 1], w0)
                    t_lr.append(act(lambda e: e.activation(lrT[:, :], ps[0:16, 0:256], ACT.Copy), t, t_free))
                    tb.put(k0, *t_lr)

                def gates():
                    for hp in range(2):
                        gate_products(hp)
                    t = act(lambda e: e.activation(E1[:, :], E1[:, :], ACT.Exp, scale=-1.0), gt["e"])
                    gt["l"] = act(lambda e: e.activation(E1[:, :], E1[:, :], ACT.Ln, bias=1.0), t)

                def gate_products(hp):
                    k0, ps, w0 = tb.get()

                    def f(e):
                        e.matmul(ps[:, 0:256], wg[:, hp * 256:hp * 256 + P], lrT[:, :], start=True, stop=True)
                        return e.matmul(ps[:, 256:512], wg[:, hp * 256 + P:hp * 256 + 256], lrT[:, :], start=False,
                                        stop=True, skip_group_check=True)
                    t = pe(f, t_lr, (s_wg, 16), w0)
                    ta = []
                    for j in range(2):
                        hd = 2 * hp + j
                        bg_ = vcol[:, VR["bg"] + hd:VR["bg"] + hd + 1]
                        x = slice(hd * 256, (hd + 1) * 256)
                        ta.append(act(lambda e, x=x, j=j, b=bg_: e.activation(
                            E1[:, x], ps[:, j * 256:(j + 1) * 256], ACT.Identity, bias=b), t, t_free, t_vec2))
                    tb.put(k0, *ta)
                    x = slice(hp * 512, (hp + 1) * 512)
                    t1 = dve(lambda e: e.tensor_scalar(G[:, x], E1[:, x], 0.0, None, ALU.min), ta, t_free)
                    gt["e"] = act(lambda e: e.activation(E1[:, x], E1[:, x], ACT.Abs), t1)

                def decays():
                    t = dve(lambda e: e.tensor_tensor(G[:, :], G[:, :], E1[:, :], ALU.subtract), gt["l"])
                    for j in range(8):
                        y = slice(j * P, (j + 1) * P)
                        tB.append(dve(lambda e, y=y: e.tensor_tensor_scan(B[:, y], ones[:, :], G[:, y], 0.0,
                                                                          ALU.mult, ALU.add), t, t_ones, t_free))
                gt = {}
                later(3, low)
                later(5, gates)
                later(7, decays)
                linear(xh, xl, ready, 8, 1, lambda c, *a: evac(2, *a))

                sT = {"S": t_S}
                xf = [t_free] * 4
                s_lev = sem("s_lev")
                o_lev = const_at["lev"][0]
                sp.dma(levm[:, :], T["const"][:, o_lev:o_lev + 8 * P], s_lev, 0, t_free)

                def level(n):
                    steps = []
                    Xb, XT = X[n % 4], {}

                    if n == 0:
                        def a0():
                            XT["t"] = [tQ, tK]
                        steps.append(a0)
                    else:
                        m = 2 ** (n - 1)
                        view = lambda z: z[:, :].rearrange("p (x a m) -> p x a m", a=2, m=m)
                        nx = 512 // m
                        ref = view(B)[:, :, 0, m - 1:m].to_broadcast([P, nx, m])

                        def a1():
                            t = pool(lambda e: e.tensor_tensor(view(Xb)[:, :, 0, :], ref, view(B)[:, :, 0, :],
                                                              ALU.subtract), tB, xf[n % 4])
                            if m < P:
                                t2 = pool(lambda e: e.tensor_tensor(view(Xb)[:, :, 1, :], view(B)[:, :, 1, :], ref,
                                                                   ALU.subtract), tB, xf[n % 4])
                            else:
                                t2 = dve(lambda e: e.tensor_copy(view(Xb)[:, :, 1, :], view(B)[:, :, 1, :]), tB,
                                         xf[n % 4])
                            XT["a"] = [t, t2]

                        def ae():
                            XT["e"] = act(lambda e: e.activation(Xb[:, :], Xb[:, :], ACT.Exp, scale=1.0 / 16),
                                          XT["a"])

                        def a2():
                            eng = (pool, dve)[n % 2]
                            t = eng(lambda e: e.tensor_tensor(view(Xb)[:, :, 0, :], view(Xb)[:, :, 0, :],
                                                              view(KT)[:, :, 0, :], ALU.mult), XT["e"], tK)
                            t2 = dve(lambda e: e.tensor_tensor(view(Xb)[:, :, 1, :], view(Xb)[:, :, 1, :],
                                                               view(QT)[:, :, 1, :], ALU.mult), XT["e"], tQ)
                            XT["t"] = [t, t2]
                        steps += [a1, ae, a2]

                    def half(j):
                        def f():
                            k0, ps, w0 = tb.get()
                            if n < 8:
                                def g(e):
                                    for i in range(4):
                                        y = slice(j * 512 + i * P, j * 512 + (i + 1) * P)
                                        l, r = (KT, QT) if n == 0 else (Xb, Xb)
                                        last = e.matmul(ps[:, i * P:(i + 1) * P], l[:, y], r[:, y], start=i == 0,
                                                        stop=True, skip_group_check=True)
                                    return last
                                t = pe(g, XT["t"], w0)
                                s4 = S[:, j * 512:(j + 1) * 512].rearrange("p (i n) -> p i n", i=4)
                                mk = levm[:, n * P:(n + 1) * P].bitcast(U32).rearrange(
                                    "p (i n) -> p i n", i=1).to_broadcast([P, 4, P])
                                sT[j] = dve(lambda e: e.copy_predicated(
                                    s4, mk, ps[:, :].rearrange("p (i n) -> p i n", i=4)), t, sT.get(j, sT["S"]), (s_lev, 16))
                                tb.put(k0, sT[j])
                            else:
                                def g(e):
                                    for i in range(4):
                                        last = e.matmul(ps[:, i * P:(i + 1) * P], Xb[:, i * 256:i * 256 + P],
                                                        Xb[:, i * 256 + P:(i + 1) * 256], start=i == 0,
                                                        stop=True, skip_group_check=True)
                                    return last
                                t = pe(g, XT["t"], w0)
                                sT["off"] = dve(lambda e: e.tensor_copy(OFF[:, :], ps[:, :]), t, t_free)
                                tb.put(k0, sT["off"])
                            xf[n % 4] = t
                        return f
                    steps.append(half(0))
                    if n < 8:
                        steps.append(half(1))
                    return steps

                lv = [level(n) for n in range(9)]

                def keys():
                    tK.extend(to_T(lambda tok: kt[:, tok * 512:(tok + 1) * 512], [got[2, 0], got[2, 1]], v3(KT), 4,
                                   1.0, dve, after=t_free))
                none = lambda: None
                bg.extend([keys, none, none, lv[0][0]] + lv[0][1:] + [none] * 3)
                for n in range(-2, 9):
                    now = [lv[k][i] for k, i in ((n + 3, 0), (n + 2, 1), (n + 1, 2)) if 1 <= k < 9]
                    bg.extend(now + [none] * (4 - len(now)) if n < 1 else now + lv[n][3:])
                PUMP[0] = 3
                linear(xh, xl, ready, 8, 1, lambda c, *a: evac(c + 3, *a))
                PUMP[0] = 4
                linear(xh, xl, ready, 8, 3, lambda c, *a: evac(c + 4, *a))
                pump(1000)
                PUMP[0] = 0
                xfree[0] = (pe.sem, pe.n)
                orow, torow = grow[1], grow[2]
                xr = [[None, None] for _ in range(8)]
                opened = []

                def outputs(tok, hd):
                    k0, ps, w0 = acc.get()

                    def f(e):
                        vv = lambda b: vt[:, b * D + hd * 256:b * D + (hd + 1) * 256]
                        last = e.matmul(ps[:, 0:256], S[:, hd * 256 + tok * P:hd * 256 + (tok + 1) * P],
                                        vv(tok), start=True, stop=tok == 0)
                        if tok:
                            last = e.matmul(ps[:, 0:256], OFF[:, hd * P:(hd + 1) * P], vv(0), start=False,
                                            stop=True)
                        return last
                    t = pe(f, sT[0], sT[1], sT["off"], got[3, tok], got[4, tok], got[3, 0], got[4, 0], w0)
                    ss = col()
                    ts = sumsq(ps[:, 0:256], ss, t)
                    r, tr = rpow(ss, 1, 1.0 / 256, ts)
                    return tok, hd, k0, ps, r, tr

                def normed(tok, hd, k0, ps, r, tr):
                    o = slice(tok * D + hd * 256, tok * D + (hd + 1) * 256)
                    a = dve(lambda e: e.scalar_tensor_tensor(
                        ps[:, 0:256], ps[:, 0:256], r, orow[:, 0:256], ALU.mult, ALU.mult), tr, torow)
                    b = dve(lambda e: e.tensor_tensor(sr[:, o], ps[:, 0:256], sr[:, o], ALU.mult),
                            a, got[5, tok], got[6, tok])
                    acc.put(k0, b)
                    got["o", tok, hd] = row_free[grow[0]] = b

                def operand(tok):
                    x_block(tok, sr[:, tok * D:(tok + 1) * D],
                            [[got["o", tok, 2 * q], got["o", tok, 2 * q + 1]] for q in range(2)], xr)

                for n in range(11):
                    if n < 8:
                        opened.append(outputs(n // 4, n % 4))
                    if n >= 3:
                        normed(*opened.pop(0))
                    if n == 6:
                        operand(0)
                res = down(xh, xl, xr, 8, lambda: operand(1))
                xfree[0] = (pe.sem, pe.n)
            return residual(res, 1.0, gain)

        ada_view = T["w_ada_2"].rearrange("(p k) n -> p k n", k=8)
        ada = {"tile": 0, "t": [], "in": [], "acc_free": None}

        def ada_load():
            j = ada["tile"]
            if ada["in"] and (len(ada["in"]) == 2 or "due" in ada):
                ada_add(ada["in"].pop(0))
                ada["last"] = unit["load"]
            if j == 96 or "due" in ada:
                return
            ada["tile"] += 1
            c, k = divmod(j, 8)
            sp.dma(adat[j % 2][:, :], ada_view[:, k, c * 512:(c + 1) * 512], s_ada[j % 2], 0,
                   ada["t"][j - 2] if j >= 2 else None)
            ada["in"].append(j)
            if k == 7:
                ada["due"] = (c, j)

        def ada_add(j):
            k = j % 8
            buf = adat[j % 2][:, :]
            arrived = (s_ada[j % 2], 16 * (j // 2 + 1))
            sc = scol[:, 8 + k:9 + k]
            last = ada["t"][j - 1] if j else None
            if k == 0:
                t = dve(lambda e: e.tensor_scalar(adaacc[:, :], buf, sc, None, ALU.mult), arrived, t_vec2,
                        ada["acc_free"], last)
            else:
                t = dve(lambda e: e.scalar_tensor_tensor(adaacc[:, :], buf, sc, adaacc[:, :], ALU.mult, ALU.add),
                        arrived, last)
            ada["t"].append(t)

        def ada_reduce():
            c, j = ada.pop("due")
            t = ada["t"][j]
            k0, ps, w0 = tb.get()

            def f(e):
                for j in range(4):
                    last = e.matmul(ps[:, j:j + 1], adaacc[:, j * P:(j + 1) * P], ones[:, 0:1], start=j == 0,
                                    stop=True, skip_group_check=True)
                return last
            t1 = pe(f, t, t_ones, w0)
            b = vcol[:, VR["ba"] + 4 * c:VR["ba"] + 4 * c + 4]
            t2 = dve(lambda e: e.tensor_tensor(modc[:, 4 * c:4 * c + 4], ps[:, 0:4], b, ALU.add), t1, t_vec2)
            tb.put(k0, t2)
            ada["acc_free"] = t1
            ada["mod"] = t2

        def enter_ada(prev, wcol, shift, scale):
            gw = col(8)
            tg = dve(lambda e: e.scalar_tensor_tensor(gw, modc[:, scale * 8:scale * 8 + 8], 1.0,
                                                      vcol[:, wcol:wcol + 8], ALU.add, ALU.mult), ada["mod"], t_vec2)
            ready = [[None, None] for _ in range(8)]
            tf = snap()

            def prep(tok, hr):
                r, tr = h_stats(tok, hr)
                tx = [dve(lambda e, q=q: e.tensor_scalar(
                    hid[tok][:, q * 512:(q + 1) * 512], h[:, tok * D + q * 512:tok * D + (q + 1) * 512], r, None,
                    ALU.mult), tr, hr[q], tf) for q in range(2)]
                x_block(tok, hid[tok][:, :], tx, ready, gw, modc[:, shift * 8:shift * 8 + 8], tg)
                hfree[tok] = [tx, (act.sem, act.n)]
            prep(0, prev(0))
            ahead(4)
            r1 = prev(1)

            def late():
                prep(1, r1)
            return ready, late

        gate = {}

        def gate_diag(which):
            t_free = snap()
            gate["d"] = [[dve(lambda e, n=n, j=j: e.tensor_scalar(
                hid[n][:, j * P:(j + 1) * P], ident, modc[:, which * 8 + 4 * n + j:which * 8 + 4 * n + j + 1], None,
                ALU.mult), ada["mod"], t_free) for j in range(4)] for n in range(2)]

        def gate_sum():
            s = row_n[0] % 2
            row_n[0] += 1
            dst = rows[s]
            tr = []
            for n in range(2):
                k0, ps, w0 = tb.get()
                t = pe(lambda e, ps=ps, n=n: e.matmul(ps[:, :], ones[:, :], hid[n][:, 0:512], start=True, stop=True),
                       gate["d"][n], w0)
                t = act(lambda e, ps=ps, n=n: e.activation(dst[:, n * 512:(n + 1) * 512], ps[:, :], ACT.Copy), t,
                        row_free[s])
                tb.put(k0, t)
                tr.append(t)
            gate["row"] = s, dst, tr

        def residual_gate(res, gain):
            s, row, trow = gain

            def run(tok):
                ready = []
                for n in range(2):
                    ps, k0, t = res[tok][n]
                    hs = h[:, tok * D + n * 512:tok * D + (n + 1) * 512]
                    a = dve(lambda e, ps=ps, n=n: e.tensor_tensor(ps[:, :], ps[:, :], row[:, n * 512:(n + 1) * 512],
                                                                  ALU.mult), t, trow)
                    b = dve(lambda e, ps=ps, hs=hs: e.tensor_tensor(hs, ps[:, :], hs, ALU.add), a, hfree[tok])
                    acc.put(k0, b)
                    ready.append(b)
                row_free[s] = b
                return ready
            return run

        def second_mixer(prev):
            with ExitStack() as inner:
                ar = sb("ar2", 13712, where=inner)
                AH = sb("AH", 1024, F32R, where=inner)
                AL = sb("AL", 1024, F32R, where=inner)
                tf = snap()
                off = [0]

                def A(n, at=None):
                    if at is None:
                        at = off[0]
                        off[0] += n
                    return ar[:, at:at + n]
                iqT, qaT, kaT, va, ikT = A(1024), A(1024), A(1024), A(1024), A(256)
                sga, sgb = A(2048, 0), A(2048, 2048)
                MB = A(384)
                SCW = off[0]
                SC, W = A(384), A(384)
                PB = [SC, W, iqT[:, 0:384]]
                pT = [A(384), A(384), iqT[:, 384:768]]
                off[0] = SCW + 1536
                RSb = A(1536, SCW)
                qrT, krT, vr, sgr = A(1024), A(1024), A(2048), A(2048)
                rt = A(512)
                decay = hid[1][:, :]
                iw, ik2 = A(16), A(256)
                assert off[0] <= 13712, off[0]
                s_dec = sem("s_dec")
                ready, late = enter_ada(prev, VR["n1"], 0, 1)
                gnr = row_load(T["gn_w_2"], D)
                v4 = lambda z: z.rearrange("p (b n) -> p b n", b=4)
                rtf = [None]
                hf = [[None], [None]]

                def rope(eng, buf, tok, nh, hd, half, cs, sn, ready, extra=None):
                    v = buf.rearrange("p (x d) -> p x d", d=hd)
                    x1, x2 = v[:, :, 0:half], v[:, :, half:2 * half]
                    w = nh * half
                    t1b = rt[:, 0:w].rearrange("p (x d) -> p x d", d=half)
                    t2b = rt[:, 256:256 + w].rearrange("p (x d) -> p x d", d=half)
                    bc = lambda z: z.rearrange("p (x d) -> p x d", x=1).to_broadcast([P, nh, half])
                    c_, s_ = bc(C(cs, tok * half, half)), bc(C(sn, tok * half, half))
                    tt = lambda o, a, b, op, *w_: eng(lambda e: e.tensor_tensor(o, a, b, op), *w_)
                    a = tt(t1b, x1, s_, ALU.mult, ready, rtf[0], t_in2, tf)
                    b = tt(t2b, x2, s_, ALU.mult, ready, rtf[0], t_in2, tf)
                    c = tt(x1, x1, c_, ALU.mult, a)
                    d = tt(x2, x2, c_, ALU.mult, b)
                    f1 = tt(x1, x1, t2b, ALU.subtract, c, b)
                    f2 = tt(x2, x2, t1b, ALU.add, d, a)
                    rtf[0] = [f1, f2]
                    return [f1, f2]

                def roped(i, dst, nblk_dims, scale, full):
                    tk = [None, None]

                    def evac(c, tok, ps, t):
                        o = hid[i][:, tok * 512:(tok + 1) * 512]
                        a = act(lambda e: e.activation(o, ps[:, :], ACT.Copy), t, hf[i], tf)
                        if full:
                            tk[tok] = rope(pool, o, tok, 4, 128, 64, "cosr", "sinr", a)
                        else:
                            tk[tok] = rope(pool, o, tok, 8, 64, 8, "cosa", "sina", a)
                        return [a]

                    def finish():
                        r = to_T(lambda tok: hid[i][:, tok * 512:(tok + 1) * 512], tk, dst, 4, scale, act, after=tf)
                        hf[i] = (pe.sem, pe.n)
                        return r
                    return evac, finish

                got = {}
                def ev_ik(c, tok, ps, t):
                    i2 = ik2[:, tok * P:(tok + 1) * P].rearrange("p (a d) -> p a d", a=2)
                    a = act(lambda e: e.activation(i2[:, 0, :], ps[:, 0:64], ACT.Copy), t, tf)
                    b = act(lambda e: e.activation(iw[:, tok * 8:tok * 8 + 8], ps[:, 64:72], ACT.Copy,
                                                   scale=8.0 ** -0.5), t, tf)
                    tr = rope(pool, i2[:, 0, :], tok, 1, 64, 8, "cosa", "sina", a)
                    got["ik", tok] = pool(lambda e: e.tensor_copy(i2[:, 1, :], i2[:, 0, :]), tr)
                    got["iw", tok] = b
                    return [a, b]

                first = [None]

                def late_first():
                    late()
                    first[0] = (pe.sem, pe.n)
                    hf[0] = first[0]
                e1, f1 = roped(0, v4(iqT), 4, 1.0, False)
                linear(xh, xl, ready, 8, 1, e1, late_first, True)
                hf[1] = first[0]
                linear(xh, xl, ready, 8, 1, ev_ik)

                def index_keys():
                    k0, ps, w0 = tb.get()
                    t = transposes([ik2[:, 0:P], ik2[:, P:256]], [got["ik", 0], got["ik", 1]], ps, [0, P], w0)
                    got["tik"] = act(lambda e: e.activation(ikT, ps[:, 0:256], ACT.Copy), t, tf)
                    tb.put(k0, got["tik"])
                e2, f2 = roped(1, v4(qaT), 4, 0.125, False)
                later(2, lambda: got.update(tiq=f1()))
                later(3, index_keys)
                linear(xh, xl, ready, 8, 1, e2)
                e3, f3 = roped(0, v4(kaT), 4, 1.0, False)
                later(3, lambda: got.update(tqa=f2()))
                linear(xh, xl, ready, 8, 1, e3)

                def ev_va(c, tok, ps, t):
                    a = act(lambda e: e.activation(va[:, tok * 512:(tok + 1) * 512], ps[:, :], ACT.Copy), t, tf)
                    got["va", tok] = a
                    return [a]

                ch = {"t": [None, None]}
                cut = [slice(0, P), slice(P, 384)]

                def idx_head(hd):
                    def f():
                        p0, b = 64 * (hd % 2), hd // 2
                        k0, ps, w0 = tb.get()

                        def g(e):
                            q, k = iqT[p0:p0 + 64, b * 256:(b + 1) * 256], ikT[p0:p0 + 64, :]
                            e.matmul(ps[:, 0:P], q[:, 0:P], k[:, 0:P], start=True, stop=True)
                            return e.matmul(ps[:, P:384], q[:, P:256], k, start=False, stop=True,
                                            skip_group_check=True)
                        t = pe(g, got["tiq"][b], got["tik"], w0)
                        R = pT[hd % 2]
                        t = act(lambda e: e.activation(R, ps[:, 0:384], ACT.Relu, scale=0.125), t,
                                ch.get(("r", hd % 2)), tf)
                        tb.put(k0, t)
                        for j in range(2):
                            wv = iw[:, j * 8 + hd:j * 8 + hd + 1]
                            if hd == 0:
                                ch["t"][j] = dve(lambda e, j=j, wv=wv: e.tensor_scalar(
                                    SC[:, cut[j]], R[:, cut[j]], wv, None, ALU.mult), t, got["iw", j], tf)
                            else:
                                ch["t"][j] = dve(lambda e, j=j, wv=wv: e.scalar_tensor_tensor(
                                    SC[:, cut[j]], R[:, cut[j]], wv, SC[:, cut[j]], ALU.mult, ALU.add), t,
                                    ch["t"][j], got["iw", j])
                        ch["r", hd % 2] = list(ch["t"])
                        ch["idx"] = (pe.sem, pe.n)
                    return f

                def causal():
                    for j, s_ in enumerate((slice(0, P), slice(256, 384))):
                        ch["t"][j] = dve(lambda e, s_=s_: e.tensor_tensor(SC[:, s_], SC[:, s_], C("caus"), ALU.add),
                                         ch["t"][j])

                def top8(n):
                    def f():
                        for j in range(2):
                            src = SC if n == 0 else W
                            m8 = got.setdefault(("m8", j, n % 2), col(8))
                            t = dve(lambda e, j=j, src=src, m8=m8: e.max(m8, src[:, cut[j]]), ch["t"][j], tf)
                            ch["t"][j] = dve(lambda e, j=j, src=src, m8=m8: e.match_replace(
                                W[:, cut[j]], m8, src[:, cut[j]], -BIG), t)
                    return f

                def choose():
                    t = dve(lambda e: e.tensor_scalar(MB, W, -2e38, None, ALU.is_le), ch["t"], tf)
                    t = dve(lambda e: e.tensor_scalar(MB, MB, -1.0, 1e30, ALU.add, ALU.mult), t)
                    for s_ in (slice(0, P), slice(256, 384)):
                        t = dve(lambda e, s_=s_: e.tensor_tensor(MB[:, s_], MB[:, s_], C("caus"), ALU.min), t)
                    ch["m"] = t
                    ch["p"] = [[t], [t], [t, ch["idx"]]]

                LG = {}

                def logits(hd):
                    p0, b, s = 64 * (hd % 2), hd // 2, hd % 3
                    k0, ps, w0 = tb.get()

                    def g(e):
                        q, k = qaT[p0:p0 + 64, b * 256:(b + 1) * 256], kaT[p0:p0 + 64, b * 256:(b + 1) * 256]
                        e.matmul(ps[:, 0:P], q[:, 0:P], k[:, 0:P], start=True, stop=True)
                        return e.matmul(ps[:, P:384], q[:, P:256], k, start=False, stop=True,
                                        skip_group_check=True)
                    t = pe(g, got["tqa"][b], got["tka"][b], w0)
                    mx, nm, sm, ri = col(2), col(2), col(2), col(2)
                    ts = []
                    for j in range(2):
                        ts.append(dve(lambda e, j=j: e.tensor_tensor_reduce(
                            out=PB[s][:, cut[j]], in0=ps[:, cut[j]], in1=MB[:, cut[j]], scale=1.0, scalar=-BIG,
                            op0=ALU.add, op1=ALU.max, accum_out=mx[:, j:j + 1]), t, ch["m"], ch["p"][s]))
                    tb.put(k0, *ts)
                    t = dve(lambda e: e.tensor_scalar(nm, mx, -1.0, None, ALU.mult), ts)
                    te = [act(lambda e, j=j: e.activation(PB[s][:, cut[j]], PB[s][:, cut[j]], ACT.Exp,
                                                          bias=nm[:, j:j + 1], accum_out=sm[:, j:j + 1]), t, ts)
                          for j in range(2)]
                    t = dve(lambda e: e.reciprocal(ri, sm), te)
                    LG[hd] = [dve(lambda e, j=j: e.tensor_scalar(PB[s][:, cut[j]], PB[s][:, cut[j]], ri[:, j:j + 1],
                                                                 None, ALU.mult), t, te) for j in range(2)]

                def probs(hd):
                    s = hd % 3
                    k0, ps, w0 = tb.get()
                    t = transposes([PB[s][:, 0:P], PB[s][:, P:256], PB[s][:, 256:384]], LG[hd], ps, [0, P, 256], w0)
                    ch["p"][s] = t
                    t = act(lambda e: e.activation(pT[s], ps[:, 0:384], ACT.Copy), t, ch.get(("v", s)), ch["m"])
                    tb.put(k0, t)
                    LG[hd] = t

                def att_values(hd):
                    s, p0, b = hd % 3, 64 * (hd % 2), hd // 2
                    if hd % 2 == 0:
                        ch["pv"] = acc6.get()
                    k0, ps, w0 = ch["pv"]

                    def g(e):
                        e.matmul(ps[p0:p0 + 64, 0:256], va[:, hd * 64:(hd + 1) * 64], pT[s][:, 0:256],
                                 start=True, stop=True)
                        return e.matmul(ps[p0:p0 + 64, P:256], va[:, 512 + hd * 64:512 + (hd + 1) * 64],
                                        pT[s][:, 256:384], start=False, stop=True, skip_group_check=True)
                    t = pe(g, LG[hd], got["va", 0], got["va", 1], w0)
                    ch["v", s] = t
                    if hd % 2 == 1:
                        sl = slice(b * 256, (b + 1) * 256)
                        a = act(lambda e: e.activation(AH[:, sl], ps[:, 0:256], ACT.Copy), t, tf)
                        c = dve(lambda e: e.tensor_tensor(AL[:, sl], ps[:, 0:256], AH[:, sl].bitcast(F32),
                                                          ALU.subtract), a, tf)
                        acc6.put(k0, c)
                        got["att", b] = [[a, c]] * 2

                acc6 = acc
                for hd in range(8):
                    bg.append(idx_head(hd))
                bg.append(causal)
                for n in range(8):
                    bg.append(top8(n))
                bg.append(choose)
                PUMP[0] = 1
                linear(xh, xl, ready, 8, 1, ev_va)
                later(2, lambda: got.update(tka=f3()))
                for s in range(11):
                    def stp(s=s):
                        if 0 <= s - 3 < 8:
                            att_values(s - 3)
                        if 0 <= s - 2 < 8:
                            probs(s - 2)
                        if s < 8:
                            logits(s)
                    bg.append(stp)
                e4, f4 = roped(1, v4(qrT), 4, 1.0, True)
                linear(xh, xl, ready, 8, 1, e4)
                e5, f5 = roped(0, v4(krT), 4, 1.0, True)
                later(3, lambda: got.update(tqr=f4()))
                linear(xh, xl, ready, 8, 1, e5)
                later(3, lambda: got.update(tkr=f5()))

                def ev_vr(c, tok, ps, t):
                    o = slice(tok * D + c * 512, tok * D + (c + 1) * 512)
                    a = act(lambda e: e.activation(vr[:, o], ps[:, :], ACT.Copy), t, tf)
                    got["vr", c, tok] = a
                    return [a]

                linear(xh, xl, ready, 8, 2, ev_vr)
                o_dec = const_at["dec"][0]
                sp.dma(decay, T["const"][:, o_dec:o_dec + 1024], s_dec, 0, snap())

                def ev_gr(c, tok, ps, t):
                    o = slice(tok * D + c * 512, tok * D + (c + 1) * 512)
                    a = act(lambda e: e.activation(sgr[:, o], ps[:, :], ACT.Silu), t, tf)
                    b = pool(lambda e: e.tensor_tensor(sgr[:, o], sgr[:, o], gnr[1][:, c * 512:(c + 1) * 512],
                                                       ALU.mult), a, gnr[2])
                    got["gr", c, tok] = b
                    row_free[gnr[0]] = b
                    return [a]

                linear(xh, xl, ready, 8, 2, ev_gr)
                pump(1000)
                t_dsa = snap()

                for hd in range(4):
                    def f(hd=hd):
                        k0, ps, w0 = tb.get()

                        def g(e):
                            q, k = qrT[:, hd * 256:(hd + 1) * 256], krT[:, hd * 256:(hd + 1) * 256]
                            e.matmul(ps[:, 0:256], k[:, 0:P], q, start=True, stop=True)
                            return e.matmul(ps[:, 256:384], k[:, P:256], q[:, P:256], start=False, stop=True,
                                            skip_group_check=True)
                        t = pe(g, got["tqr"][hd], got["tkr"][hd], w0)
                        o = hd * 384
                        a = dve(lambda e: e.tensor_tensor(RSb[:, o:o + 256], ps[:, 0:256],
                                                          decay[:, hd * 256:(hd + 1) * 256], ALU.mult), t, t_dsa,
                                (s_dec, 16))
                        b = dve(lambda e: e.tensor_tensor(RSb[:, o + 256:o + 384], ps[:, 256:384],
                                                          decay[:, hd * 256:hd * 256 + P], ALU.mult), t, t_dsa,
                                (s_dec, 16))
                        tb.put(k0, b)
                        got["rs", hd] = [a, b]
                    bg.append(f)
                for tok in range(2):
                    for hd in range(4):
                        def f(tok=tok, hd=hd):
                            k0, ps, w0 = tb.get()
                            vv = lambda b: vr[:, b * D + hd * 256:b * D + (hd + 1) * 256]

                            def g(e):
                                o = hd * 384
                                if tok == 0:
                                    return e.matmul(ps[:, 0:256], RSb[:, o:o + P], vv(0), start=True, stop=True)
                                e.matmul(ps[:, 0:256], RSb[:, o + P:o + 256], vv(0), start=True, stop=False)
                                return e.matmul(ps[:, 0:256], RSb[:, o + 256:o + 384], vv(1), start=False, stop=True)
                            c = hd // 2
                            t = pe(g, got["rs", hd], got["vr", c, 0], got["vr", c, 1], w0)
                            s6, mv = col(6), col(2)
                            t = dve(lambda e: e.bn_stats(s6, ps[:, 0:256]), t)
                            t = dve(lambda e: e.bn_aggr(mv, s6), t)
                            r2, t3 = rpow(mv[:, 1:2], 1, 1.0, t)
                            t3 = dve(lambda e: e.tensor_scalar(ps[:, 0:256], ps[:, 0:256], mv[:, 0:1], r2,
                                                               ALU.subtract, ALU.mult), t3)
                            o = slice(tok * D + hd * 256, tok * D + (hd + 1) * 256)
                            t3 = dve(lambda e: e.tensor_tensor(sgr[:, o], ps[:, 0:256], sgr[:, o], ALU.mult), t3,
                                     got["gr", c, tok])
                            tb.put(k0, t3)
                            got["yr", tok, hd] = t3
                        bg.append(f)

                def ev_g(dst, key):
                    def ev(c, tok, ps, t):
                        o = slice(tok * D + c * 512, tok * D + (c + 1) * 512)
                        a = act(lambda e: e.activation(dst[:, o], ps[:, :], ACT.Sigmoid), t, t_dsa)
                        got[key, c, tok] = a
                        return [a]
                    return ev
                linear(xh, xl, ready, 8, 2, ev_g(sga, "ga"))
                linear(xh, xl, ready, 8, 2, ev_g(sgb, "gb"))
                xfree[0] = (pe.sem, pe.n)
                PUMP[0] = 0
                pump(1000)

                def gated(res, dst, key, tok):
                    ts = []
                    for n in range(2):
                        ps, k0, t = res[tok][n]
                        o = slice(tok * D + n * 512, tok * D + (n + 1) * 512)
                        b = dve(lambda e, ps=ps, o=o: e.tensor_tensor(dst[:, o], ps[:, :], dst[:, o], ALU.mult),
                                t, got[key, n, tok])
                        acc.put(k0, b)
                        ts.append(b)
                    return ts
                xr = [[None, None] for _ in range(8)]
                for tok in range(2):
                    x_block(tok, sgr[:, tok * D:(tok + 1) * D],
                            [[got["yr", tok, 2 * q], got["yr", tok, 2 * q + 1]] for q in range(2)], xr)
                ra = down(AH, AL, [got["att", b] for b in range(4)], 4)
                ta = [gated(ra, sga, "ga", tok) for tok in range(2)]
                later(1, lambda: gate_diag(2))
                later(3, gate_sum)
                rr = down(xh, xl, xr, 8)
                xfree[0] = (pe.sem, pe.n)
                xr = [[None, None] for _ in range(8)]

                def merge(tok):
                    tbb = gated(rr, sgb, "gb", tok)
                    tm = []
                    for n in range(2):
                        o = slice(tok * D + n * 512, tok * D + (n + 1) * 512)
                        tm.append(dve(lambda e, o=o: e.tensor_tensor(sga[:, o], sga[:, o], sgb[:, o], ALU.add),
                                      ta[tok][n], tbb[n]))
                    return tm
                x_block(0, sga[:, 0:D], merge(0), xr)
                ahead(3)
                tm1 = merge(1)
                res = down(xh, xl, xr, 8, lambda: x_block(1, sga[:, D:2 * D], tm1, xr))
                xfree[0] = (pe.sem, pe.n)
            return residual_gate(res, gate["row"])

        def second_ffn(prev):
            ready, late = enter_ada(prev, VR["n2"], 3, 4)
            with ExitStack() as inner:
                gh = sb("ghf", 22 * 256, F32R, where=inner)
                gl = sb("glf", 22 * 256, F32R, where=inner)
                gready = ffn_body(gh, gl, ready, None, late)
                later(5, lambda: gate_diag(5))
                later(7, gate_sum)
                res = down(gh, gl, gready, 22)
            return residual_gate(res, gate["row"])

        def plan_down(w, nk):
            for k in range(0, nk, 4):
                m = min(4, nk - k)
                for n in range(2):
                    plan.append((w[k * P:(k + m) * P, n * 512:(n + 1) * 512]
                                 .rearrange("(k p) n -> p k n", p=P), m, 512))

        plan_ffn([T["ffn1_w_in"][0]], T["ffn1_w_out"][0])
        for c in (4, 3, 0, 1, 2):
            plan_cols(T["hyb_w_in"][0], c * 512, 512, 8)
        plan_down(T["hyb_w_out"][0], 8)
        plan_ffn([T["ffn2_w_in"][0]], T["ffn2_w_out"][0])

        plan_ffn([T["ffn1_w_in"][1]], T["ffn1_w_out"][1])
        for c, n in ((0, 512), (3072, 16), (512, 512), (1024, 512), (1536, 512), (2048, 512), (2560, 512)):
            plan_cols(T["gla_w_in"][0], c, n, 8)
        plan_down(T["gla_w_out"][0], 8)
        plan_ffn([T["ffn2_w_in"][1]], T["ffn2_w_out"][1])

        w = T["w_in_2"]
        plan_cols(w, 1536, 512, 8)
        plan_cols(w, 2048, 72, 8)
        for c in (0, 512, 1024, 2120, 2632, 3144, 3656, 4168, 4680, 5192, 5704, 6216, 6728):
            plan_cols(w, c, 512, 8)
        plan_down(T["w_attn_proj_2"], 4)
        plan_down(T["w_ret_proj_2"], 8)
        plan_down(T["w_out_2"], 8)
        plan_ffn([T["w_ffn_gate_2"], T["w_ffn_up_2"]], T["w_ffn_down_2"])

        cut_subs()
        load_unit()
        sp.dma(h[:, D:2 * D], T["x"][0, P:2 * P, :], s_x[2], 0)
        load_unit()
        stages = [lambda p: ffn_stage(p, 0, T["norm_g"][0, 1]), hybrid_stage,
                  lambda p: ffn_stage(p, 4 * 8, T["norm_g"][0, 5]),
                  lambda p: ffn_stage(p, 6 * 8, T["norm_g"][1, 1]), gla_stage,
                  lambda p: ffn_stage(p, 10 * 8, T["norm_g"][1, 5]), second_mixer, second_ffn]
        prev = lambda tok: t_x[tok]
        for stage in stages:
            prev = stage(prev)
        frow = row_load(T["final_norm_w_2"], D)
        for tok in range(2):
            hr = prev(tok)
            r, tr = h_stats(tok, hr)
            for n in range(2):
                hs = h[:, tok * D + n * 512:tok * D + (n + 1) * 512]
                hr[n] = dve(lambda e, hs=hs, r=r, n=n: e.scalar_tensor_tensor(
                    hs, hs, r, frow[1][:, n * 512:(n + 1) * 512], ALU.mult, ALU.mult), tr, frow[2])
            for n in range(2):
                sp.dma(out[0, tok * P:(tok + 1) * P, n * 512:(n + 1) * 512],
                       h[:, tok * D + n * 512:tok * D + (n + 1) * 512], s_out, 0, hr[n])
        sp.wait((s_out, 64))

        block = ctx.enter_context(nc.Block())
        block.sync(lambda e: sp.run(e))
        block.tensor(lambda e: pe.run(e))
        block.scalar(lambda e: act.run(e))
        block.vector(lambda e: dve.run(e))
        block.gpsimd(lambda e: pool.run(e))


_INS = ["x", "norm_g", "ffn1_w_in", "ffn1_w_out", "ffn2_w_in", "ffn2_w_out", "hyb_w_in", "hyb_w_out", "conv_dw_w",
        "conv_dw_b", "conv_ln_g", "conv_ln_b", "gla_w_in", "gla_w_gate", "gla_b_gate", "gla_norm_g", "gla_w_out",
        "c_2", "w_ada_2", "b_ada_2", "norm1_w_2", "w_in_2", "w_attn_proj_2", "w_ret_proj_2", "gn_w_2", "w_out_2",
        "norm2_w_2", "w_ffn_gate_2", "w_ffn_up_2", "w_ffn_down_2", "final_norm_w_2"]


def kernel(**inputs):
    import numpy as _np
    import concourse.bacc as _bacc
    from concourse import mybir as _mybir
    from concourse.bass_utils import run_bass_kernel_spmd as _run

    nc = _bacc.Bacc("TRN2", target_bir_lowering=False, num_devices=1)
    const_at, const = constants()
    arrays, T = {}, {}
    for name in _INS:
        a = _np.ascontiguousarray(inputs[name])
        arrays[f"in_{name}_dram"] = a
        T[name] = nc.dram_tensor(f"in_{name}_dram", a.shape, _mybir.dt.from_np(a.dtype), kind="ExternalInput").ap()
    arrays["in_const_dram"] = const
    T["const"] = nc.dram_tensor("in_const_dram", const.shape, _mybir.dt.float32, kind="ExternalInput").ap()
    out = nc.dram_tensor("out_0_dram", (1, 256, 1024), _mybir.dt.float32, kind="ExternalOutput").ap()
    program(nc, T, const_at, out)
    r = _run(nc, [arrays], core_ids=[0])
    return r.results[0]["out_0_dram"]
```
